# Optimizing a Trainium2 kernel written in Bass

```python
import math
import jax, jax.numpy as jnp
from jax import lax
import numpy as np

D_MODEL = 1024
BATCH = 1
SEQ = 256
DEPTH = 1

HEAD_DIM = 64
BLK = 128
NEG_INF = -1e30

SWA_WINDOW = 128
A_Q_HEADS = 4
A_KV_HEADS = 2
A_GROUP = A_Q_HEADS // A_KV_HEADS
A_COLS = (A_Q_HEADS + 2 * A_KV_HEADS) * HEAD_DIM

DILATED_PAIRS = ((128, 1), (512, 4), (2048, 16))
B_N_GROUPS = len(DILATED_PAIRS)
B_HEADS_PER_GROUP = 4
B_HEADS = B_N_GROUPS * B_HEADS_PER_GROUP
B_COLS = 3 * B_HEADS * HEAD_DIM
SEQ_ALIGN = BLK * max(d for _, d in DILATED_PAIRS)

C_HEADS = 8
C_NOPE = 64
C_ROPE = 32
C_V = 64
Q_LORA = 256
KV_LORA = 128
ROPE_THETA = 10000.0
C_COLS = Q_LORA + KV_LORA + C_ROPE

N_IN = A_COLS + B_COLS + C_COLS
D_MIX = A_Q_HEADS * HEAD_DIM + B_HEADS_PER_GROUP * HEAD_DIM + C_HEADS * C_V

N_BUCKETS = 32
MAX_DISTANCE = 2048
N_BIAS_HEADS = A_Q_HEADS + B_HEADS

N_GROUPS = 4
EXPERTS_PER_GROUP = 8
N_EXPERTS = N_GROUPS * EXPERTS_PER_GROUP
TOP_K = 2
D_EXPERT = 256
ROW_BLK = 256

DEEPNORM_ALPHA = (2 * DEPTH) ** 0.25
DEEPNORM_BETA = (8 * DEPTH) ** -0.25


def layer_norm(x, g, b, eps=1e-5):
    xf = x.astype(jnp.float32)
    mu = xf.mean(-1, keepdims=True)
    var = jnp.square(xf - mu).mean(-1, keepdims=True)
    return ((xf - mu) * lax.rsqrt(var + eps) * g + b).astype(x.dtype)

def rms_norm(x, g, eps=1e-6):
    xf = x.astype(jnp.float32)
    return (xf * lax.rsqrt(jnp.mean(xf * xf, -1, keepdims=True) + eps) * g).astype(x.dtype)

def rotary(x, cos, sin):
    x1, x2 = jnp.split(x, 2, axis=-1)
    return jnp.concatenate([x1 * cos - x2 * sin, x1 * sin + x2 * cos], -1).astype(x.dtype)

def t5_bucket(dist):
    max_exact = N_BUCKETS // 2
    large = max_exact + (jnp.log(jnp.maximum(dist, 1).astype(jnp.float32) / max_exact)
                         / math.log(MAX_DISTANCE / max_exact) * (N_BUCKETS - max_exact)).astype(jnp.int32)
    return jnp.where(dist < max_exact, dist, jnp.minimum(large, N_BUCKETS - 1))

def head_bias(table_cols, dist):
    return table_cols[t5_bucket(jnp.maximum(dist, 0))].transpose(2, 0, 1).astype(jnp.float32)

def band_blocks(t, n_blocks):
    tb = t.reshape((t.shape[0], n_blocks, BLK) + t.shape[2:])
    prev = jnp.pad(tb[:, :-1], ((0, 0), (1, 0)) + ((0, 0),) * (tb.ndim - 2))
    return jnp.concatenate([prev, tb], axis=2)

def banded_logits(q, k, bias, max_dist):
    Bp, L = q.shape[:2]
    n = L // BLK
    qb = q.reshape((Bp, n, BLK) + q.shape[2:])
    kb = band_blocks(k, n)
    s = jnp.einsum('bnqhgd,bnkhd->bnhgqk', qb, kb).astype(jnp.float32) * (q.shape[-1] ** -0.5) + bias
    qi = jnp.arange(BLK)[:, None]
    kj = jnp.arange(2 * BLK)[None, :]
    dist = BLK + qi - kj
    kpos = jnp.arange(n)[:, None, None] * BLK + kj[None] - BLK
    mask = (dist >= 0) & (dist <= max_dist) & (kpos >= 0)
    return jnp.where(mask[None, :, None, None], s, NEG_INF)

def swa_sink_mixer(h_a, sink, bias_a):
    Bsz, T, _ = h_a.shape
    q, k, v = jnp.split(h_a, [A_Q_HEADS * HEAD_DIM, (A_Q_HEADS + A_KV_HEADS) * HEAD_DIM], axis=-1)
    q = q.reshape(Bsz, T, A_KV_HEADS, A_GROUP, HEAD_DIM)
    k = k.reshape(Bsz, T, A_KV_HEADS, HEAD_DIM)
    v = v.reshape(Bsz, T, A_KV_HEADS, HEAD_DIM)
    s = banded_logits(q, k, bias_a, SWA_WINDOW - 1)
    sink_b = sink.astype(jnp.float32).reshape(1, 1, A_KV_HEADS, A_GROUP, 1, 1)
    m = jnp.maximum(s.max(-1, keepdims=True), sink_b)
    e = jnp.exp(s - m)
    p = e / (e.sum(-1, keepdims=True) + jnp.exp(sink_b - m))
    o = jnp.einsum('bnhgqk,bnkhd->bnqhgd', p.astype(v.dtype), band_blocks(v, T // BLK))
    return o.reshape(Bsz, T, A_Q_HEADS * HEAD_DIM)

def dilated_group(q, k, v, bias, dil, steps):
    Bsz, Tp, H, hd = q.shape
    Ls = Tp // dil
    n = Ls // BLK

    def to_sub(t):
        return t.reshape(Bsz, Ls, dil, H, hd).transpose(0, 2, 1, 3, 4).reshape(Bsz * dil, Ls, H, hd)

    qs, ks, vs = to_sub(q), to_sub(k), to_sub(v)
    s = banded_logits(qs[:, :, :, None], ks, bias[:, None], steps)
    m = s.max(-1, keepdims=True)
    e = jnp.exp(s - m)
    l = e.sum(-1, keepdims=True)
    lse = (m + jnp.log(l))[..., 0]
    o = jnp.einsum('bnhgqk,bnkhd->bnqhgd', (e / l).astype(v.dtype), band_blocks(vs, n))
    o = o.reshape(Bsz, dil, Ls, H, hd).transpose(0, 2, 1, 3, 4).reshape(Bsz, Tp, H, hd)
    lse = lse.transpose(0, 1, 4, 2, 3).reshape(Bsz, dil, Ls, H).transpose(0, 2, 1, 3).reshape(Bsz, Tp, H)
    return o, lse

def dilated_mixer(h_b, bias_b):
    Bsz, T, _ = h_b.shape
    T_pad = -(-T // SEQ_ALIGN) * SEQ_ALIGN
    h_b = jnp.pad(h_b, ((0, 0), (0, T_pad - T), (0, 0)))
    shape5 = (Bsz, T_pad, B_N_GROUPS, B_HEADS_PER_GROUP, HEAD_DIM)
    q, k, v = [t.reshape(shape5) for t in jnp.split(h_b, 3, axis=-1)]
    outs, lses = [], []
    for g, (window, dil) in enumerate(DILATED_PAIRS):
        o_g, lse_g = dilated_group(q[:, :, g], k[:, :, g], v[:, :, g], bias_b[g], dil, window // dil)
        outs.append(o_g)
        lses.append(lse_g)
    w = jax.nn.softmax(jnp.stack(lses), axis=0)
    o = jnp.einsum('gbth,gbthd->bthd', w.astype(h_b.dtype), jnp.stack(outs))
    return o[:, :T].reshape(Bsz, T, B_HEADS_PER_GROUP * HEAD_DIM)

def mla_mixer(h_c, q_norm_g, kv_norm_g, w_uq, w_ukv, cos, sin):
    Bsz, T, _ = h_c.shape
    c_q, c_kv, k_rope = jnp.split(h_c, [Q_LORA, Q_LORA + KV_LORA], axis=-1)
    q = (rms_norm(c_q, q_norm_g) @ w_uq).reshape(Bsz, T, C_HEADS, C_NOPE + C_ROPE)
    kv = (rms_norm(c_kv, kv_norm_g) @ w_ukv).reshape(Bsz, T, C_HEADS, C_NOPE + C_V)
    q_nope, q_rope = jnp.split(q, [C_NOPE], axis=-1)
    k_nope, v = jnp.split(kv, [C_NOPE], axis=-1)
    q_rope = rotary(q_rope, cos[:, None], sin[:, None])
    k_rope = rotary(k_rope, cos, sin)
    n = T // BLK
    scale = (C_NOPE + C_ROPE) ** -0.5
    key_pos = jnp.arange(T)

    def to_blocks(t):
        return t.reshape((Bsz, n, BLK) + t.shape[2:]).swapaxes(0, 1)

    def one_block(args):
        qn, qr, blk = args
        s = (jnp.einsum('bqhd,bkhd->bhqk', qn, k_nope)
             + jnp.einsum('bqhd,bkd->bhqk', qr, k_rope)).astype(jnp.float32) * scale
        q_pos = blk * BLK + jnp.arange(BLK)
        s = jnp.where(key_pos[None, :] <= q_pos[:, None], s, NEG_INF)
        p = jax.nn.softmax(s, axis=-1)
        return jnp.einsum('bhqk,bkhd->bqhd', p.astype(v.dtype), v)

    o = lax.map(one_block, (to_blocks(q_nope), to_blocks(q_rope), jnp.arange(n)))
    return o.swapaxes(0, 1).reshape(Bsz, T, C_HEADS * C_V)

def hybrid_mixer(x, w_in, w_out, sink, bias_a, bias_b, q_norm_g, kv_norm_g, w_uq, w_ukv, cos, sin):
    h = x @ w_in
    h_a, h_b, h_c = jnp.split(h, [A_COLS, A_COLS + B_COLS], axis=-1)
    o_a = swa_sink_mixer(h_a, sink, bias_a)
    o_b = dilated_mixer(h_b, bias_b)
    o_c = mla_mixer(h_c, q_norm_g, kv_norm_g, w_uq, w_ukv, cos, sin)
    return jnp.concatenate([o_a, o_b, o_c], axis=-1) @ w_out

def hierarchical_moe(h, w_rg, b_rg, w_re, b_re, w_gate, w_up, w_down):
    Bsz, T, D = h.shape
    n_tok = Bsz * T
    x = h.reshape(n_tok, D)
    g_logits = (x @ w_rg).astype(jnp.float32) + b_rg
    g_prob = jax.nn.softmax(g_logits, axis=-1)
    grp = jnp.argmax(g_logits, axis=-1)
    p_grp = jnp.take_along_axis(g_prob, grp[:, None], axis=-1)
    e_all = jnp.einsum('nd,gde->nge', x, w_re).astype(jnp.float32) + b_re
    e_logits = jnp.take_along_axis(e_all, grp[:, None, None], axis=1)[:, 0]
    top_val, top_idx = lax.top_k(e_logits, TOP_K)
    gate = jax.nn.softmax(top_val, axis=-1) * p_grp
    expert_ids = grp[:, None] * EXPERTS_PER_GROUP + top_idx
    A = n_tok * TOP_K
    flat_e = expert_ids.reshape(A).astype(jnp.int32)
    flat_w = gate.reshape(A)
    flat_tok = jnp.arange(A, dtype=jnp.int32) // TOP_K
    order = jnp.argsort(flat_e)
    e_sorted = flat_e[order]
    counts = jnp.zeros((N_EXPERTS,), jnp.int32).at[flat_e].add(1)
    padded = ((counts + ROW_BLK - 1) // ROW_BLK) * ROW_BLK
    pad_end = jnp.cumsum(padded)
    pad_start = pad_end - padded
    start = jnp.cumsum(counts) - counts
    dest = pad_start[e_sorted] + (jnp.arange(A, dtype=jnp.int32) - start[e_sorted])
    n_blocks = A // ROW_BLK + N_EXPERTS
    P = n_blocks * ROW_BLK
    row_tok = jnp.full((P,), n_tok, jnp.int32).at[dest].set(flat_tok[order])
    row_w = jnp.zeros((P,), h.dtype).at[dest].set(flat_w[order].astype(h.dtype))
    block_expert = jnp.minimum(
        jnp.searchsorted(pad_end, jnp.arange(n_blocks) * ROW_BLK, side='right'), N_EXPERTS - 1)
    x_pad = jnp.concatenate([x, jnp.zeros((1, D), x.dtype)], axis=0)
    rows = x_pad[row_tok].reshape(n_blocks, ROW_BLK, D)

    def block_ffn(args):
        xb, e = args
        return (jax.nn.silu(xb @ w_gate[e]) * (xb @ w_up[e])) @ w_down[e]

    ys = lax.map(block_ffn, (rows, block_expert)).reshape(P, D) * row_w[:, None]
    out = jnp.zeros((n_tok + 1, D), ys.dtype).at[row_tok].add(ys)[:n_tok]
    return out.reshape(Bsz, T, D)

def first_inputs(seed: int = 0) -> dict:
    key = jax.random.key(seed)
    ks = jax.random.split(key, 20)
    f32 = jnp.float32

    def nrm(k, shape, scale):
        return jax.random.normal(k, shape, f32) * scale

    return {
        "x": nrm(ks[0], (BATCH, SEQ, D_MODEL), 1.0),
        "w_in": nrm(ks[1], (DEPTH, D_MODEL, N_IN), D_MODEL ** -0.5),
        "w_out": nrm(ks[2], (DEPTH, D_MIX, D_MODEL), DEEPNORM_BETA * D_MIX ** -0.5),
        "sinks": nrm(ks[3], (DEPTH, A_Q_HEADS), 0.5),
        "rel_bias": nrm(ks[4], (N_BUCKETS, N_BIAS_HEADS), 0.1),
        "mla_q_norm": 1.0 + nrm(ks[5], (DEPTH, Q_LORA), 0.05),
        "mla_kv_norm": 1.0 + nrm(ks[6], (DEPTH, KV_LORA), 0.05),
        "w_uq": nrm(ks[7], (DEPTH, Q_LORA, C_HEADS * (C_NOPE + C_ROPE)), Q_LORA ** -0.5),
        "w_ukv": nrm(ks[8], (DEPTH, KV_LORA, C_HEADS * (C_NOPE + C_V)), KV_LORA ** -0.5),
        "ln1_g": 1.0 + nrm(ks[9], (DEPTH, D_MODEL), 0.05),
        "ln1_b": nrm(ks[10], (DEPTH, D_MODEL), 0.02),
        "w_route_group": nrm(ks[11], (DEPTH, D_MODEL, N_GROUPS), D_MODEL ** -0.5),
        "b_route_group": nrm(ks[12], (DEPTH, N_GROUPS), 0.01),
        "w_route_expert": nrm(ks[13], (DEPTH, N_GROUPS, D_MODEL, EXPERTS_PER_GROUP), D_MODEL ** -0.5),
        "b_route_expert": nrm(ks[14], (DEPTH, N_GROUPS, EXPERTS_PER_GROUP), 0.01),
        "w_expert_gate": nrm(ks[15], (DEPTH, N_EXPERTS, D_MODEL, D_EXPERT), D_MODEL ** -0.5),
        "w_expert_up": nrm(ks[16], (DEPTH, N_EXPERTS, D_MODEL, D_EXPERT), D_MODEL ** -0.5),
        "w_expert_down": nrm(ks[17], (DEPTH, N_EXPERTS, D_EXPERT, D_MODEL), DEEPNORM_BETA * D_EXPERT ** -0.5),
        "ln2_g": 1.0 + nrm(ks[18], (DEPTH, D_MODEL), 0.05),
        "ln2_b": nrm(ks[19], (DEPTH, D_MODEL), 0.02),
    }

def first_block(x, w_in, w_out, sinks, rel_bias, mla_q_norm, mla_kv_norm, w_uq, w_ukv, ln1_g, ln1_b,
              w_route_group, b_route_group, w_route_expert, b_route_expert,
              w_expert_gate, w_expert_up, w_expert_down, ln2_g, ln2_b):
    T = x.shape[1]
    inv_freq = ROPE_THETA ** (-jnp.arange(0, C_ROPE, 2, dtype=jnp.float32) / C_ROPE)
    ang = jnp.arange(T, dtype=jnp.float32)[:, None] * inv_freq[None, :]
    cos, sin = jnp.cos(ang), jnp.sin(ang)
    dist = BLK + jnp.arange(BLK)[:, None] - jnp.arange(2 * BLK)[None, :]
    bias_a = head_bias(rel_bias[:, :A_Q_HEADS], dist).reshape(A_KV_HEADS, A_GROUP, BLK, 2 * BLK)
    bias_b = [head_bias(rel_bias[:, A_Q_HEADS + g * B_HEADS_PER_GROUP:A_Q_HEADS + (g + 1) * B_HEADS_PER_GROUP],
                        dist * dil)
              for g, (_, dil) in enumerate(DILATED_PAIRS)]
    for layer in range(DEPTH):
        y = hybrid_mixer(x, w_in[layer], w_out[layer], sinks[layer], bias_a, bias_b,
                         mla_q_norm[layer], mla_kv_norm[layer], w_uq[layer], w_ukv[layer], cos, sin)
        x = layer_norm(DEEPNORM_ALPHA * x + y, ln1_g[layer], ln1_b[layer])
        y = hierarchical_moe(x, w_route_group[layer], b_route_group[layer], w_route_expert[layer],
                             b_route_expert[layer], w_expert_gate[layer], w_expert_up[layer],
                             w_expert_down[layer])
        x = layer_norm(DEEPNORM_ALPHA * x + y, ln2_g[layer], ln2_b[layer])
    return x


DEPTH_2 = 2

N_DIFF_HEADS = 6
DIFF_QK_DIM = HEAD_DIM // 2
N_GQA_HEADS = 6
N_GQA_KV_HEADS = 2
GQA_GROUP = N_GQA_HEADS // N_GQA_KV_HEADS
N_MEM_HEADS = 4
N_MEM = 256
GRID_W = 64
Q_BLOCK = 128
NORM_EPS = 1e-6

DIFF_W = N_DIFF_HEADS * HEAD_DIM
GQA_W = N_GQA_HEADS * HEAD_DIM
GQA_KV_W = N_GQA_KV_HEADS * HEAD_DIM
MEM_W = N_MEM_HEADS * HEAD_DIM
D_MIX_2 = DIFF_W + GQA_W + MEM_W
IN_SIZES = [DIFF_W, DIFF_W, DIFF_W, DIFF_W, GQA_W, GQA_KV_W, GQA_KV_W, GQA_W, MEM_W, MEM_W]
D_IN = sum(IN_SIZES)
IN_OFFSETS = [int(v) for v in np.cumsum(IN_SIZES)[:-1]]


def rms_norm_2(x, g):
    xf = x.astype(jnp.float32)
    y = xf * lax.rsqrt(jnp.mean(xf * xf, axis=-1, keepdims=True) + NORM_EPS)
    return (y * g.astype(jnp.float32)).astype(x.dtype)

def rope_tables(pos, dim):
    inv = ROPE_THETA ** (-jnp.arange(0, dim, 2, dtype=jnp.float32) / dim)
    ang = pos.astype(jnp.float32)[:, None] * inv[None, :]
    return jnp.cos(ang), jnp.sin(ang)

def apply_rope(x, cos, sin):
    xf = x.astype(jnp.float32)
    half = xf.shape[-1] // 2
    x1, x2 = xf[..., :half], xf[..., half:]
    return jnp.concatenate([x1 * cos - x2 * sin, x2 * cos + x1 * sin], axis=-1).astype(x.dtype)

def apply_axial_rope(x, row_cs, col_cs):
    half = x.shape[-1] // 2
    return jnp.concatenate([apply_rope(x[..., :half], *row_cs),
                            apply_rope(x[..., half:], *col_cs)], axis=-1)

def diff_attention(q1, q2, k1, k2, v, lam):
    B, H, S, d = q1.shape
    nb = S // Q_BLOCK
    scale = d ** -0.5

    def blockify(q):
        return jnp.moveaxis(q.reshape(B, H, nb, Q_BLOCK, d), 2, 0)

    def one(qs):
        a, b = qs
        s1 = jnp.einsum('bhqd,bhkd->bhqk', a, k1).astype(jnp.float32) * scale
        s2 = jnp.einsum('bhqd,bhkd->bhqk', b, k2).astype(jnp.float32) * scale
        p = jax.nn.softmax(s1, axis=-1) - lam * jax.nn.softmax(s2, axis=-1)
        return jnp.einsum('bhqk,bhke->bhqe', p.astype(v.dtype), v)

    o = lax.map(one, (blockify(q1), blockify(q2)))
    return jnp.moveaxis(o, 0, 2).reshape(B, H, S, v.shape[-1])

def gqa_attention(q, k, v):
    B, Hk, G, S, d = q.shape
    nb = S // Q_BLOCK
    scale = d ** -0.5
    qb = jnp.moveaxis(q.reshape(B, Hk, G, nb, Q_BLOCK, d), 3, 0)

    def one(qblk):
        s = jnp.einsum('bhgqd,bhkd->bhgqk', qblk, k).astype(jnp.float32) * scale
        p = jax.nn.softmax(s, axis=-1)
        return jnp.einsum('bhgqk,bhkd->bhgqd', p.astype(v.dtype), v)

    o = lax.map(one, qb)
    return jnp.moveaxis(o, 0, 3).reshape(B, Hk, G, S, d)

def second_inputs(seed: int = 0) -> dict:
    key = jax.random.key(seed)
    ks = jax.random.split(key, 14)
    f32 = jnp.float32
    n = jax.random.normal
    return {
        "x": n(ks[0], (BATCH, SEQ, D_MODEL), f32),
        "mem": n(ks[1], (BATCH, N_MEM, D_MODEL), f32),
        "pre_norm": 1.0 + 0.02 * n(ks[2], (DEPTH_2, D_MODEL), f32),
        "w_in": n(ks[3], (DEPTH_2, D_MODEL, D_IN), f32) * D_MODEL ** -0.5,
        "diff_lambda": 0.1 * n(ks[4], (DEPTH_2, 4, DIFF_QK_DIM), f32),
        "diff_subln": 1.0 + 0.02 * n(ks[5], (DEPTH_2, HEAD_DIM), f32),
        "gqa_q_norm": 1.0 + 0.02 * n(ks[6], (DEPTH_2, HEAD_DIM), f32),
        "gqa_k_norm": 1.0 + 0.02 * n(ks[7], (DEPTH_2, HEAD_DIM), f32),
        "mem_norm": 1.0 + 0.02 * n(ks[8], (DEPTH_2, D_MODEL), f32),
        "w_mem_kv": n(ks[9], (DEPTH_2, D_MODEL, 2 * MEM_W), f32) * D_MODEL ** -0.5,
        "w_out": n(ks[10], (DEPTH_2, D_MIX_2, D_MODEL), f32) * D_MIX_2 ** -0.5,
        "post_norm": 1.0 + 0.02 * n(ks[11], (DEPTH_2, D_MODEL), f32),
    }

def second_block(x, mem, pre_norm, w_in, diff_lambda, diff_subln, gqa_q_norm, gqa_k_norm,
              mem_norm, w_mem_kv, w_out, post_norm):
    B, S, _ = x.shape
    M = mem.shape[1]
    ROWS = S // GRID_W
    t = jnp.arange(S, dtype=jnp.int32)
    row = jnp.repeat(jnp.arange(ROWS, dtype=jnp.int32), GRID_W)
    col = jnp.tile(jnp.arange(GRID_W, dtype=jnp.int32), ROWS)
    lin_cs = rope_tables(t, DIFF_QK_DIM)
    row_cs = rope_tables(row, HEAD_DIM // 2)
    col_cs = rope_tables(col, HEAD_DIM // 2)

    for l in range(DEPTH_2):
        lambda_init = 0.8 - 0.6 * math.exp(-0.3 * l)
        h = rms_norm_2(x, pre_norm[l])
        proj = h @ w_in[l]
        (dq, dk, dv, dgate, gq, gk, gv, ggate, mq, mgate) = jnp.split(proj, IN_OFFSETS, axis=-1)

        dq = apply_rope(dq.reshape(B, S, N_DIFF_HEADS, 2, DIFF_QK_DIM).transpose(0, 2, 3, 1, 4), *lin_cs)
        dk = apply_rope(dk.reshape(B, S, N_DIFF_HEADS, 2, DIFF_QK_DIM).transpose(0, 2, 3, 1, 4), *lin_cs)
        dv = dv.reshape(B, S, N_DIFF_HEADS, HEAD_DIM).transpose(0, 2, 1, 3)
        lp = diff_lambda[l].astype(jnp.float32)
        lam = jnp.exp(jnp.sum(lp[0] * lp[1])) - jnp.exp(jnp.sum(lp[2] * lp[3])) + lambda_init
        oa = diff_attention(dq[:, :, 0], dq[:, :, 1], dk[:, :, 0], dk[:, :, 1], dv, lam)
        oa = rms_norm_2(oa, diff_subln[l]) * (1.0 - lambda_init)
        oa = oa.transpose(0, 2, 1, 3).reshape(B, S, DIFF_W) * jax.nn.silu(dgate)

        gq = rms_norm_2(gq.reshape(B, S, N_GQA_HEADS, HEAD_DIM).transpose(0, 2, 1, 3), gqa_q_norm[l])
        gq = apply_axial_rope(gq, row_cs, col_cs).reshape(B, N_GQA_KV_HEADS, GQA_GROUP, S, HEAD_DIM)
        gk = rms_norm_2(gk.reshape(B, S, N_GQA_KV_HEADS, HEAD_DIM).transpose(0, 2, 1, 3), gqa_k_norm[l])
        gk = apply_axial_rope(gk, row_cs, col_cs)
        gv = gv.reshape(B, S, N_GQA_KV_HEADS, HEAD_DIM).transpose(0, 2, 1, 3)
        ob = gqa_attention(gq, gk, gv).reshape(B, N_GQA_HEADS, S, HEAD_DIM)
        ob = ob.transpose(0, 2, 1, 3).reshape(B, S, GQA_W) * jax.nn.silu(ggate)

        mkv = rms_norm_2(mem, mem_norm[l]) @ w_mem_kv[l]
        mk, mv = jnp.split(mkv, 2, axis=-1)
        mk = mk.reshape(B, M, N_MEM_HEADS, HEAD_DIM).transpose(0, 2, 1, 3)
        mv = mv.reshape(B, M, N_MEM_HEADS, HEAD_DIM).transpose(0, 2, 1, 3)
        mq = mq.reshape(B, S, N_MEM_HEADS, HEAD_DIM).transpose(0, 2, 1, 3)
        sm = jnp.einsum('bhsd,bhmd->bhsm', mq, mk).astype(jnp.float32) * HEAD_DIM ** -0.5
        pm = jax.nn.softmax(sm, axis=-1)
        om = jnp.einsum('bhsm,bhmd->bhsd', pm.astype(mv.dtype), mv)
        om = om.transpose(0, 2, 1, 3).reshape(B, S, MEM_W) * jax.nn.silu(mgate)

        y = jnp.concatenate([oa, ob, om], axis=-1) @ w_out[l]
        x = x + rms_norm_2(y, post_norm[l])
    return x


def setup_inputs(seed=0):
    out = dict(first_inputs(seed))
    for name, value in second_inputs(seed + 1).items():
        if name != "x":
            out[name + "_2"] = value
    return out


def reference(
    x, w_in, w_out, sinks, rel_bias, mla_q_norm, mla_kv_norm, w_uq, w_ukv, ln1_g, ln1_b,
    w_route_group, b_route_group, w_route_expert, b_route_expert, w_expert_gate, w_expert_up,
    w_expert_down, ln2_g, ln2_b, mem_2, pre_norm_2, w_in_2, diff_lambda_2, diff_subln_2,
    gqa_q_norm_2, gqa_k_norm_2, mem_norm_2, w_mem_kv_2, w_out_2, post_norm_2,
):
    x = first_block(
        x, w_in, w_out, sinks, rel_bias, mla_q_norm, mla_kv_norm, w_uq, w_ukv, ln1_g, ln1_b,
        w_route_group, b_route_group, w_route_expert, b_route_expert, w_expert_gate,
        w_expert_up, w_expert_down, ln2_g, ln2_b,
    )
    return second_block(
        x, mem_2, pre_norm_2, w_in_2, diff_lambda_2, diff_subln_2, gqa_q_norm_2, gqa_k_norm_2,
        mem_norm_2, w_mem_kv_2, w_out_2, post_norm_2,
    )


_drawn_inputs = setup_inputs


def setup_inputs(seed=0):
    import zlib

    import numpy as np

    out = dict(_drawn_inputs(seed))
    spreads = {}
    factors = {'sinks': 7.357,
     'rel_bias': 2.99,
     'mla_q_norm': 4.641,
     'b_route_group': 4.45,
     'gqa_q_norm_2': 8.0,
     'gqa_k_norm_2': 8.0,
     'mem_norm_2': 8.0,
     'diff_lambda_2': 2.882,
     'diff_subln_2': 8.0,
     'b_route_expert': 2.982}
    for name, (base, spread) in spreads.items():
        noise = np.random.default_rng([zlib.crc32(name.encode()), seed]).standard_normal(out[name].shape)
        drawn = base * np.exp(spread * noise) if base else spread * noise
        out[name] = __import__('jax').numpy.asarray(drawn.astype(out[name].dtype))
    for name, factor in factors.items():
        out[name] = (out[name] * factor).astype(out[name].dtype)
    return out
```

```python
import math
from contextlib import ExitStack

import numpy as np
import concourse.bass as bass
from concourse import mybir

F32 = mybir.dt.float32
BF16 = mybir.dt.bfloat16
I32 = mybir.dt.int32
ALU = mybir.AluOpType
ACT = mybir.ActivationFunctionType
X = mybir.AxisListType.X

P = 128
T = 256
D = 1024
KC = D // P
COLS = 256
SLOT = KC * COLS
RING = 12
NEG = -1.0e30
LOW = -3.0e38
HD = 64

A_HEADS, B_HEADS, B_GROUPS, C_HEADS = 4, 4, 3, 8
DILATIONS = (1, 4, 16)
C_QK, C_NOPE, C_ROPE = 96, 64, 32
Q_LORA, KV_LORA = 256, 128
C_COLS = Q_LORA + KV_LORA + C_ROPE
A_COLS, B_COLS = 512, 2304
N_BUCKETS = 32
BIAS_HEADS = A_HEADS + B_HEADS * B_GROUPS
VALS = 3 * P - 1
GROUPS, PER_GROUP = 4, 8
EXPERTS = GROUPS * PER_GROUP
DE = 256
ALPHA = 2.0 ** 0.25
HALF = C_ROPE // 2

AT_ONCE = 4
PLACES = P // AT_ONCE
BUNCHES = EXPERTS // AT_ONCE
ROUNDS = T // PLACES
ABSENT = -1024.0

LAYERS = 2
D_HEADS, G_HEADS, M_HEADS = 6, 6, 4
TILES2 = 24
V_TILES = (6, 7, 8, 16)
GATE_TILES = (9, 10, 11, 17, 18, 19, 22, 23)
LAMBDA_INIT = [0.8 - 0.6 * math.exp(-0.3 * l) for l in range(LAYERS)]

_WIDTHS = [("ident", P), ("swap", P), ("headsum", P), ("before", P), ("cos_lin", T), ("sin_lin", T),
           ("cos_ax", T), ("sin_ax", T), ("causal", P), ("cos_c", 2 * HALF), ("sin_c", 2 * HALF),
           ("places", T), ("first32", EXPERTS), ("round_from", (ROUNDS - 1) * BUNCHES)]
CONST = {}
_at = 0
for _name, _w in _WIDTHS:
    CONST[_name] = (_at, _at + _w)
    _at += _w
N_CONST = _at


def constants():
    f = np.float32
    c = {}
    p = np.arange(P)
    c["ident"] = np.eye(P)
    partner = (p // 32) * 32 + (p + 16) % 32
    c["swap"] = (partner[:, None] == p[None, :]).astype(f)
    c["headsum"] = (p[:, None] // HD == p[None, :] // HD).astype(f)
    c["before"] = (p[:, None] < p[None, :]).astype(f)
    inv = (f(10000.0) ** (-np.arange(0, 32, 2, dtype=f) / f(32))).astype(f)
    t = np.arange(T)
    own = inv[p % 16][:, None]
    sign = np.where(p % 32 < 16, -1.0, 1.0)[:, None]
    lin = (t[None, :].astype(f) * own).astype(f)
    c["cos_lin"], c["sin_lin"] = np.cos(lin), np.sin(lin) * sign
    place = np.where((p % HD < 32)[:, None], (t // 64)[None, :], (t % 64)[None, :]).astype(f)
    ax = (place * own).astype(f)
    c["cos_ax"], c["sin_ax"] = np.cos(ax), np.sin(ax) * sign
    c["causal"] = np.where(p[None, :] <= p[:, None], 0.0, NEG)
    tok = p[:, None, None] + P * np.arange(2)[None, :, None]
    ang = (tok.astype(f) * inv[None, None, :]).astype(f)
    c["cos_c"], c["sin_c"] = np.cos(ang).reshape(P, -1), np.sin(ang).reshape(P, -1)
    c["places"] = np.broadcast_to(t[None, :], (P, T))
    c["first32"] = np.broadcast_to(EXPERTS - np.arange(EXPERTS)[None, :], (P, EXPERTS))
    c["round_from"] = np.broadcast_to(
        np.repeat(PLACES * np.arange(1, ROUNDS), BUNCHES)[None, :], (P, (ROUNDS - 1) * BUNCHES))
    table = np.concatenate([np.asarray(c[n], f).reshape(P, -1) for n, _ in _WIDTHS], axis=1)

    dist = 2 * P - 1 - np.arange(VALS)
    d = np.maximum(dist, 0)
    exact = N_BUCKETS // 2
    large = exact + (np.log(np.maximum(d, 1).astype(f) / f(exact)) / f(math.log(2048 / exact))
                     * f(N_BUCKETS - exact)).astype(np.int32)
    bucket = np.where(d < exact, d, np.minimum(large, N_BUCKETS - 1))
    of_bucket = (bucket[None, :] == np.arange(N_BUCKETS)[:, None]).astype(f)
    seen = np.zeros((BIAS_HEADS, VALS), bool)
    seen[:A_HEADS] = (dist >= 0) & (dist <= P - 1)
    for g, dil in enumerate(DILATIONS):
        at = A_HEADS + g * B_HEADS
        seen[at:at + B_HEADS] = (dist >= 0) & (dist % dil == 0) & (dist // dil <= P)
    return {"const_table": np.ascontiguousarray(table, dtype=f), "const_bucket": of_bucket,
            "const_unseen": np.where(seen, 0.0, NEG).astype(f)}


ITEMS = (["c_q", "c_kv", "w_uq", "w_ukv", "a_q", "a_kv"]
         + [f"b_{x}{g}" for g in range(B_GROUPS) for x in "qkv"]
         + [f"w_out{s}" for s in range(4)] + ["router"]
         + [f"mem_{x}{l}" for l in range(LAYERS) for x in "kv"])
FIRST_EXPERT = len(ITEMS)
assert FIRST_EXPERT % RING == 0
ITEMS += [f"expert{e}{y}" for b in range(BUNCHES) for x in ("gu", "d")
          for e in range(AT_ONCE * b, AT_ONCE * (b + 1)) for y in (("g", "u") if x == "gu" else ("d",))]
LOAD_ORDER2 = [0, 1, 2, 3, 4, 7, 8, 6, 10, 5, 9, 11]
for _l in range(LAYERS):
    ITEMS += [f"in{_l}_{n}" for n in LOAD_ORDER2] + [f"out{_l}_{s}" for s in range(4)]
ITEM = {name: n for n, name in enumerate(ITEMS)}
PIECES = {"router": 1 + GROUPS, "a_q": A_HEADS}


def all_loaded(n):
    return 16 * sum(PIECES.get(ITEMS[m], 1) for m in range(n % RING, n + 1, RING))

TAKEN_BY_DVE = ("bias", "y1", "logit", "logitT", "rank", "swap")


def schedule():
    turns = []
    jobs = [("xt", k) for k in range(4)] + [("cnat", 0), ("cnat", 1), ("bias",), ("vec",), ("tile1", 0), ("tile1", 1), ("tile1", 2), ("ct",), ("ckt",), ("tile1", 3),
             ("cq", 0, 0), ("cq", 0, 1), ("cq", 1, 0), ("cq", 1, 1), ("avn",)]
    jobs += [("ck", k) for k in range(4)] + [("cv", 0), ("cv", 1)] + [("cqt", k) for k in range(4)]
    turns.append((jobs, None))
    fill = []
    for g in range(B_GROUPS):
        fill += [("tile1", 4 + 2 * g), ("tile1", 5 + 2 * g), ("tile1", 10 + 2 * g), ("tile1", 11 + 2 * g),
                 ("bv", g, 0), ("bv", g, 1)]
    steps = [("A", 0, h) for h in range(A_HEADS)] + [("C", 0, h) for h in range(C_HEADS)]
    for n, s in enumerate(steps):
        turns.append((fill[n * len(fill) // 12:(n + 1) * len(fill) // 12], s))
    for h in range(B_HEADS):
        turns.append(([], ("B", 0, h)))
    turns += [([], None), ([], None)]
    jobs = [("y1", s, tt) for tt in range(2) for s in range(4)]
    jobs += [("mt", k) for k in range(4)]
    jobs += [("mk", 0, 0), ("mk", 0, 1)]
    jobs += [("x1t", k) for k in range(4)] + [("logit",), ("logitT",), ("mv", 0, 0), ("mv", 0, 1), ("mk", 1, 0),
                                              ("mk", 1, 1), ("mv", 1, 0), ("mv", 1, 1), ("rank",)]
    turns.append((jobs, None))
    turns.append(([], "experts"))
    for l in range(LAYERS):
        jobs = [("xt2", l, k) for k in range(4)]
        for n in range(6):
            jobs.append(("tile2", l, n))
            if n >= 1:
                jobs.append(("swap", l, n - 1))
        jobs += [("tile2", l, 6), ("swap", l, 5), ("tile2", l, 7), ("vn", l, 6), ("tile2", l, 8), ("vn", l, 7),
                 ("tile2", l, 9), ("vn", l, 8)]
        turns.append((jobs, None))
        steps = ([("D", l, h) for h in range(D_HEADS)] + [("G", l, h) for h in range(G_HEADS)]
                 + [("M", l, h) for h in range(M_HEADS)])
        tiles = [15, 16, 12, 13, 14, 17, 20, 21, 10, 11, 18, 19, 22, 23]
        after = []
        for n, s in enumerate(steps):
            jobs = []
            if n < len(tiles):
                t = tiles[n]
                jobs.append(("tile2", l, t))
            jobs += after
            after = []
            if n < len(tiles):
                if 12 <= t <= 15:
                    after = [("hsq", l, t), ("swap", l, t)]
                if t == 16:
                    after = [("vn", l, 16)]
            if n in (4, 6, 8):
                after.append(("hso", l, n // 2 - 2))
            turns.append((jobs, s))
        assert not after
        turns += [([], None), ([], None)]
        turns.append(([("y2", l, s, tt) for tt in range(2) for s in range(4)], None))
    return turns


TURNS = schedule()
JOBS = [job for jobs, _ in TURNS for job in jobs]
JOB = {job: n for n, job in enumerate(JOBS)}
BY_DVE = [job[0] in TAKEN_BY_DVE for job in JOBS]


def taken(n):
    return sum(BY_DVE[m] == BY_DVE[n] for m in range(n + 1))


STEPS = [s for _, s in TURNS if isinstance(s, tuple)]
STEP = {s: n for n, s in enumerate(STEPS)}
S_JOBS = {"A": 1, "B": 3, "C": 1, "D": 2, "G": 1, "M": 1}
T_JOBS = {"A": 1, "B": 3, "C": 1, "D": 1, "G": 1, "M": 1}


def s_first(step):
    return sum(S_JOBS[s[0]] for s in STEPS[:step])


def t_first(step):
    return sum(T_JOBS[s[0]] for s in STEPS[:step])



def opens(step):
    return STEPS[step] in (("A", 0, 0), ("D", 0, 0), ("D", 1, 0))


S_OWNER = [n for n, s in enumerate(STEPS) for _ in range(S_JOBS[s[0]])]


def item_of(job):
    kind = job[0]
    if kind == "cnat":
        return ["c_q", "c_kv"]
    if kind == "cq":
        return ["w_uq"]
    if kind in ("ck", "cv"):
        return ["w_ukv"]
    if kind == "tile1":
        n = job[1]
        return ["a_q"] if n < 2 else ["a_kv"] if n < 4 else [f"b_q{(n - 4) // 2}"] if n < 10 else [f"b_k{(n - 10) // 2}"]
    if kind == "bv":
        return [f"b_v{job[1]}"]
    if kind == "y1":
        return [f"w_out{job[1]}"]
    if kind == "logit":
        return ["router"]
    if kind in ("mk", "mv"):
        return [f"mem_{kind[1]}{job[1]}"]
    if kind == "tile2":
        return [f"in{job[1]}_{job[2] // 2}"]
    if kind == "y2":
        return [f"out{job[1]}_{job[2]}"]
    return []


LAST_JOB = {}
for _n, _job in enumerate(JOBS):
    for _name in item_of(_job):
        LAST_JOB[_name] = _n


def build(nc, ins, out):
    ctx = ExitStack()
    with ctx:
        def sb(name, shape, dt=F32):
            return ctx.enter_context(nc.sbuf_tensor(name, shape, dt))

        def sem(name):
            return ctx.enter_context(nc.semaphore(name))

        ring = sb("ring", [P, RING * SLOT])
        const = sb("const", [P, N_CONST])
        x_nat = sb("x_nat", [P, 2 * D])
        xT = sb("xT", [P, KC * T])
        mixT = sb("mixT", [P, KC * T])
        tiles = sb("tiles", [P, TILES2 * T])
        v_nat = sb("v_nat", [P, 2048])
        q_c = sb("q_c", [P, C_HEADS * T])
        k_c = sb("k_c", [P, C_HEADS * T])
        v_c = sb("v_c", [P, 1024])
        bias = sb("bias", [P, BIAS_HEADS * T])
        probs = sb("probs", [P, 2 * 1152])
        probsT = sb("probsT", [P, 4 * 512])
        vecs = sb("vecs", [P, 41])
        small = sb("small", [P, 256])
        ident_b = sb("ident_b", [P, P], BF16)
        causal_b = sb("causal_b", [P, P], BF16)
        zeros_b = sb("zeros_b", [P, 512], BF16)
        flags = sb("flags", [P, 2 * (ROUNDS - 1) * BUNCHES + 2], I32)
        psum = ctx.enter_context(nc.psum_tensor("psum", [P, 8, 512], F32))

        def bank(n):
            return psum[:, n, :]

        def c_(name):
            a, b = CONST[name]
            return const[:, a:b]

        ident, swap, headsum, before = c_("ident"), c_("swap"), c_("headsum"), c_("before")
        slots = ring[:, :].rearrange("p (s k n) -> p s k n", s=RING, k=KC)
        x2 = x_nat[:, :].rearrange("p (t d) -> p t d", t=2)
        x4 = x_nat[:, :].rearrange("p (t k q) -> p t k q", t=2, k=KC)
        xT3 = xT[:, :].rearrange("p (k t) -> p k t", k=KC)
        y_nat = xT[:, :].rearrange("p (t d) -> p t d", t=2)
        mix3 = mixT[:, :].rearrange("p (k t) -> p k t", k=KC)
        tile3 = tiles[:, :].rearrange("p (n t) -> p n t", n=TILES2)
        qc3 = q_c[:, :].rearrange("p (h t) -> p h t", h=C_HEADS)
        kc3 = k_c[:, :].rearrange("p (h t) -> p h t", h=C_HEADS)
        vc3 = v_c[:, :].rearrange("p (t n) -> p t n", t=2)
        bias3 = bias[:, :].rearrange("p (h t) -> p h t", h=BIAS_HEADS)
        va = v_nat[:, 0:256].rearrange("p (t n) -> p t n", t=2)
        vb = v_nat[:, 256:1792].rearrange("p (t g n) -> p t g n", t=2, g=B_GROUPS)
        v2 = v_nat[:, 0:1024].rearrange("p (t n m) -> p t n m", t=2, n=4)
        ln_row = tiles[:, 4096:6144].rearrange("p (n d) -> p n d", n=2)
        post_row = bias[:, 0:2048].rearrange("p (n d) -> p n d", n=2)
        vec_rows = q_c[:, 1024:1024 + P]
        c_nat = mixT[:, 0:2 * C_COLS].rearrange("p (t n) -> p t n", t=2)
        c_qT = mixT[:, 832:832 + 512].rearrange("p (k t) -> p k t", k=2)
        c_kvT = mixT[:, 1344:1600]
        rope_t = mixT[:, 1600:2048]
        qc_nat = probs[:, 0:1536].rearrange("p (t n) -> p t n", t=2)
        mem_nat = k_c[:, :].rearrange("p (t d) -> p t d", t=2)
        mem4 = k_c[:, :].rearrange("p (t k q) -> p t k q", t=2, k=KC)
        memT = bias[:, :].rearrange("p (l k t) -> p l k t", l=LAYERS, k=KC)
        mem_k = v_c[:, :].rearrange("p (l n t) -> p l n t", l=LAYERS, n=2)
        mem_v = v_nat[:, 1024:2048].rearrange("p (l t n) -> p l t n", l=LAYERS, t=2)
        places4 = tiles[:, 0:256].rearrange("p (t e s) -> p t e s", t=2, e=AT_ONCE)
        places2 = tiles[:, 0:256].rearrange("p (t s) -> p t s", t=2)
        weighed4 = tiles[:, 256:512].rearrange("p (t e s) -> p t e s", t=2, e=AT_ONCE)
        weighed2 = tiles[:, 256:512].rearrange("p (t s) -> p t s", t=2)
        back = tiles[:, 512:768]
        gate_e = tiles[:, 768:1024]
        hidden = tiles[:, 1024:1280]
        hiddenT = tiles[:, 1280:1536].rearrange("p (k s) -> p k s", k=2)
        y_e = tiles[:, 1536:2560]
        gathered = q_c[:, 0:1024].rearrange("p (k s) -> p k s", k=KC)
        more_g = xT[:, :]
        more_u = mixT[:, :]
        more_d = k_c[:, :]
        xn2 = probs[:, 0:2048].rearrange("p (t d) -> p t d", t=2)
        xn4 = probs[:, 0:2048].rearrange("p (t k q) -> p t k q", t=2, k=KC)

        used = [0]

        def col(n, rows_=P):
            a = used[0]
            used[0] += n
            assert used[0] <= 256
            return small[0:rows_, a:a + n]

        eps6, eps5, minus_half = col(1), col(1), col(4)
        sink = col(A_HEADS)
        route_b = col(1)
        c_sq, c_rs = col(4), col(4)
        mx, nm, sm, sink_e = col(2 * 8), col(2 * 4), col(2 * 4), col(2 * 2)
        ln_stats, ln_mv, ln_rs = col(2 * 12), col(4), col(2)
        mem_sq, mem_rs = col(2), col(2)
        x_sq, x_rs = col(2), col(2)
        y_sq, y_rs = col(2), col(2)
        lam_s, lam_e, neg_lam = col(4), col(4), col(2)
        lam_p = k_c[:, 0:256]
        sub_g = col(2)
        stats4 = ln_stats.rearrange("p (t c s) -> p t c s", t=2, c=2)
        mv3 = ln_mv.rearrange("p (t s) -> p t s", t=2)
        bucket_sb, rel_sb = probsT[0:N_BUCKETS, 0:VALS + 1], probsT[0:N_BUCKETS, 384:384 + BIAS_HEADS]
        unseen_sb, bias_sb = probsT[0:BIAS_HEADS, 512:512 + VALS], probsT[0:BIAS_HEADS, 1024:1024 + VALS]
        rope_s = q_c[:, 0:512]
        mem_junk = q_c[:, 0:D]
        rope_a = q_c[:, 7 * T:8 * T]

        def sq_tile(n):
            m = n - 12 if n >= 12 else 4 + n
            return q_c[:, T * m:T * m + T]

        def exp_tile(n):
            m = GATE_TILES.index(n)
            return k_c[:, T * m:T * m + T]

        rt = [0]

        def rcol(n):
            a = rt[0]
            rt[0] += n
            assert rt[0] <= 2048
            return probs[:, a:a + n]

        logitT_sb = rcol(T)
        lg = rcol(72).rearrange("p (t n) -> p t n", t=2)
        g_mx, g_eq, g_sc, g_one, g_dif, g_exp, g_sum, p_grp = (rcol(2), rcol(8), rcol(8), rcol(8), rcol(8), rcol(8),
                                                               rcol(2), rcol(2))
        e_m, e_sc, e_one1, e_one2 = rcol(64), rcol(64), rcol(64), rcol(64)
        e_mx1, e_mx2, e_t, e_x, w_1, w_2 = rcol(2), rcol(2), rcol(2), rcol(2), rcol(2), rcol(2)
        chosen, gates, rank = rcol(64), rcol(64), rcol(64)
        cnt, cnt_b, more_f, scan = rcol(EXPERTS), rcol(BUNCHES), rcol(56), rcol(56)
        any_more = rcol(1)
        ones = rcol(P)
        rank3 = rank.rearrange("p (t e) -> p t e", t=2)
        gates3 = gates.rearrange("p (t e) -> p t e", t=2)
        chosen3 = chosen.rearrange("p (t e) -> p t e", t=2)

        bias_dram = nc.dram_tensor("bias_rows", [BIAS_HEADS, P, VALS], F32, kind="Internal").ap()

        loaded = [sem(f"loaded{s}") for s in range(RING)]
        x_in, const_in, vec_in, small_in = sem("x_in"), sem("const_in"), sem("vec_in"), sem("small_in")
        ln1_in, ln2_in, post_in = sem("ln1_in"), sem("ln2_in"), sem("post_in")
        table_in, bias_out, bias_in, mem_in = sem("table_in"), sem("bias_out"), sem("bias_in"), sem("mem_in")
        p_ready = sem("p_ready")
        p_act, p_dve = sem("p_act"), sem("p_dve")
        setup = sem("setup")
        c_sums, c_rstd, c_scaled = sem("c_sums"), sem("c_rstd"), sem("c_scaled")
        qc_roped, kc_roped = sem("qc_roped"), sem("kc_roped")
        scores, maxed, exped, sink_exped = sem("scores"), sem("maxed"), sem("exped"), sem("sink_exped")
        normed, turned, turned_out = sem("normed"), sem("turned"), sem("turned_out")
        o_ready, o_out = sem("o_ready"), sem("o_out")
        mem_sum, mem_rstd, mem_scaled = sem("mem_sum"), sem("mem_rstd"), sem("mem_scaled")
        ln_var, ln_rstd, ln_done = sem("ln_var"), sem("ln_rstd"), sem("ln_done")
        route_dif, route_exp, route_m, route_x = sem("route_dif"), sem("route_exp"), sem("route_m"), sem("route_x")
        chosen_done, routed = sem("chosen_done"), sem("routed")
        placed, gathered_ready, gathered_out = sem("placed"), sem("gathered_ready"), sem("gathered_out")
        back_ready, back_out = sem("back_ready"), sem("back_out")
        gu_ready, gate_exped, hidden_done = sem("gu_ready"), sem("gate_exped"), sem("hidden_done")
        hT_ready, hT_out = sem("hT_ready"), sem("hT_out")
        y_ready, y0_out, y1_out, summed = sem("y_ready"), sem("y0_out"), sem("y1_out"), sem("summed")
        more_in, more_down_in, more_used = sem("more_in"), sem("more_down_in"), sem("more_used")
        moe_done = sem("moe_done")
        x_sum, x_rstd, x_scaled = sem("x_sum"), sem("x_rstd"), sem("x_scaled")
        y_sum, y_rstd, x_done = sem("y_sum"), sem("y_rstd"), sem("x_done")
        lam_sum, lam_exp = sem("lam_sum"), sem("lam_exp")
        roped, squared, gate_silu, gated = sem("roped"), sem("squared"), sem("gate_silu"), sem("gated")
        o_squared, sub_done, k_copied = sem("o_squared"), sem("sub_done"), sem("k_copied")
        act_chain, dve_chain, moe_chain = sem("act_chain"), sem("dve_chain"), sem("moe_chain")
        stored = sem("stored")

        def rope_nth(l, n):
            order = [j[2] for j in JOBS if j[0] == "swap" and j[1] == l]
            return l * len(order) + order.index(n) + 1

        def hsq_nth(l, n):
            order = [j[2] for j in JOBS if j[0] == "hsq" and j[1] == l]
            return l * len(order) + order.index(n) + 1

        block = ctx.enter_context(nc.Block())

        @block.sync
        def _(sp):
            def source(name):
                w_in, w_out = ins["w_in"][0], ins["w_out"][0]

                def k_rows(w, a, b):
                    return w[:, a:b].rearrange("(k p) n -> p k n", p=P)

                if name == "c_q":
                    return k_rows(w_in, A_COLS + B_COLS, A_COLS + B_COLS + Q_LORA)
                if name == "c_kv":
                    return k_rows(w_in, A_COLS + B_COLS + Q_LORA, A_COLS + B_COLS + C_COLS)
                if name == "a_kv":
                    return k_rows(w_in, 256, 512)
                if name[:2] == "b_":
                    at = A_COLS + 768 * "qkv".index(name[2]) + 256 * int(name[3])
                    return k_rows(w_in, at, at + 256)
                if name[:5] == "w_out":
                    s = int(name[5])
                    return k_rows(w_out, 256 * s, 256 * s + 256)
                if name[:4] == "mem_":
                    at = 256 * "kv".index(name[4])
                    return k_rows(ins["w_mem_kv_2"][int(name[5])], at, at + 256)
                if name[:2] == "in":
                    l, n = int(name[2]), int(name[4:])
                    return k_rows(ins["w_in_2"][l], 256 * n, 256 * n + 256)
                l, s = int(name[3]), int(name[5])
                return k_rows(ins["w_out_2"][l], 256 * s, 256 * s + 256)

            def load(n):
                name, s = ITEMS[n], n % RING
                if name == "w_uq":
                    sp.dma_start(ring[:, s * SLOT:s * SLOT + 1536].rearrange("p (k n) -> p k n", k=2),
                                 ins["w_uq"][0].rearrange("(k p) n -> p k n", p=P)).then_inc(loaded[s], 16)
                elif name == "w_ukv":
                    sp.dma_start(ring[:, s * SLOT:s * SLOT + 1024], ins["w_ukv"][0]).then_inc(loaded[s], 16)
                elif name == "a_q":
                    for m, h in enumerate((0, 2, 1, 3)):
                        sp.dma_start(slots[:, s, :, HD * m:HD * m + HD],
                                     ins["w_in"][0, :, HD * h:HD * h + HD].rearrange("(k p) n -> p k n", p=P)
                                     ).then_inc(loaded[s], 16)
                elif name == "router":
                    sp.dma_start(slots[:, s, :, 0:GROUPS],
                                 ins["w_route_group"][0].rearrange("(k p) n -> p k n", p=P)).then_inc(loaded[s], 16)
                    for g in range(GROUPS):
                        sp.dma_start(slots[:, s, :, GROUPS + PER_GROUP * g:GROUPS + PER_GROUP * (g + 1)],
                                     ins["w_route_expert"][0, g].rearrange("(k p) n -> p k n", p=P)
                                     ).then_inc(loaded[s], 16)
                else:
                    src = source(name)
                    sp.dma_start(slots[:, s, :, 0:src.shape[2]], src).then_inc(loaded[s], 16)

            def load_bunch(b, first):
                for k in range(RING):
                    if not first:
                        if k == 0:
                            sp.wait_ge(gu_ready, b)
                        if k == 2 * AT_ONCE:
                            sp.wait_ge(y_ready, 2 * b)
                    elif FIRST_EXPERT + k >= RING:
                        sp.wait_ge(p_ready, LAST_JOB[ITEMS[FIRST_EXPERT + k - RING]] + 1)
                    name = ("w_expert_gate", "w_expert_up")[k % 2] if k < 2 * AT_ONCE else "w_expert_down"
                    e = k // 2 if k < 2 * AT_ONCE else k - 2 * AT_ONCE
                    w = ins[name][0, bass.ds(b * AT_ONCE + e, 1)]
                    sp.dma_start(ring[:, k * SLOT:(k + 1) * SLOT],
                                 w.rearrange("o (p k) n -> p (o k n)", p=P)).then_inc(loaded[k], 16)

            sp.dma_start(x2, ins["x"][0].rearrange("(t p) d -> p t d", p=P)).then_inc(x_in, 16)
            sp.dma_start(const[:, :], ins["const_table"]).then_inc(const_in, 16)
            for n in range(FIRST_EXPERT):
                if n >= RING:
                    sp.wait_ge(p_ready, LAST_JOB[ITEMS[n - RING]] + 1)
                load(n)
                if n == RING - 1:
                    sp.wait_ge(p_dve, taken(JOB[("bias",)]))
                    sp.dma_start(bias_dram, bias_sb.unsqueeze(1).to_broadcast([BIAS_HEADS, P, VALS])
                                 ).then_inc(bias_out, 16)
                    sp.wait_ge(bias_out, 16)
                    shifted = bass.AP(tensor=bias_dram.tensor, offset=P - 1,
                                      ap=[[VALS - 1, P], [P * VALS, BIAS_HEADS], [1, T]])
                    sp.dma_start(bias3, shifted).then_inc(bias_in, 16)
            load_bunch(0, True)
            with sp.Fori(1, BUNCHES) as b:
                load_bunch(b, False)

            sp.wait_ge(routed, 1)
            some = sp.value_load(flags[0:1, 112:113], min_val=0, max_val=1)
            with sp.If(some):
                with sp.Fori(0, ROUNDS - 1) as r:
                    with sp.Fori(0, BUNCHES) as g:
                        flag = sp.value_load(flags[0:1, bass.ds(r * BUNCHES + g, 1)], min_val=0, max_val=1)
                        with sp.If(flag):
                            n = sp.value_load(flags[0:1, bass.ds(r * BUNCHES + g + 56, 1)], min_val=0, max_val=55)
                            sp.wait_ge(y_ready, n * 2 + 2 * BUNCHES)
                            for e in range(AT_ONCE):
                                if e:
                                    sp.wait_ge(more_used, n * 6 + e)
                                for dst, w in ((more_g, ins["w_expert_gate"]), (more_u, ins["w_expert_up"])):
                                    sp.dma_start(dst, w[0, bass.ds(g * AT_ONCE + e, 1)].rearrange(
                                        "o (p k) n -> p (o k n)", p=P)).then_inc(more_in, 16)
                            for e in range(AT_ONCE):
                                if e:
                                    sp.wait_ge(more_used, n * 6 + 3 + e)
                                sp.dma_start(more_d, ins["w_expert_down"][0, bass.ds(g * AT_ONCE + e, 1)].rearrange(
                                    "o (p k) n -> p (o k n)", p=P)).then_inc(more_down_in, 16)

            after = FIRST_EXPERT + RING * BUNCHES
            for n in range(after, len(ITEMS)):
                if n == after:
                    sp.wait_ge(gu_ready, BUNCHES)
                elif n == after + 2 * AT_ONCE:
                    sp.wait_ge(y_ready, 2 * BUNCHES)
                elif n >= after + RING:
                    sp.wait_ge(p_ready, LAST_JOB[ITEMS[n - RING]] + 1)
                load(n)
            out2 = out[0].rearrange("(t p) d -> p t d", p=P)
            for tt in range(2):
                sp.wait_ge(x_done, 2 * LAYERS - 1 + tt)
                sp.dma_start(out2[:, tt, :], x2[:, tt, :]).then_inc(stored, 16)
            sp.wait_ge(stored, 32)

        @block.gpsimd
        def _(pool):
            
            def vec(at, n, src):
                pool.dma_start(vec_rows[at:at + n, 0:src.shape[1]], src).then_inc(vec_in, 16)

            vec(0, 16, ins["pre_norm_2"].rearrange("l (k q) -> (l k) q", q=P))
            vec(16, 16, ins["mem_norm_2"].rearrange("l (k q) -> (l k) q", q=P))
            vec(32, 2, ins["mla_q_norm"].rearrange("l (k q) -> (l k) q", q=P))
            vec(34, 1, ins["mla_kv_norm"])
            for at, name in ((35, "diff_subln_2"), (37, "gqa_q_norm_2"), (39, "gqa_k_norm_2")):
                for j in range(2):
                    pool.dma_start(vec_rows[at:at + 2, HD * j:HD * j + HD], ins[name]).then_inc(vec_in, 16)
            pool.dma_start(sink, ins["sinks"][0].partition_broadcast(P)).then_inc(small_in, 16)
            pool.dma_start(route_b[0:GROUPS, :], ins["b_route_group"].rearrange("o g -> g o")).then_inc(small_in, 16)
            pool.dma_start(route_b[GROUPS:GROUPS + EXPERTS, :],
                           ins["b_route_expert"].rearrange("o g e -> (g e) o")).then_inc(small_in, 16)
            pool.dma_start(lam_p, ins["diff_lambda_2"].rearrange("l a d -> (l a d)").partition_broadcast(P)
                           ).then_inc(small_in, 16)

            pool.wait_ge(setup, 1)
            pool.wait_ge(c_sums, 1)
            pool.tensor_tensor(c_rs, c_sq, minus_half, ALU.pow).then_inc(c_rstd, 1)
            pool.wait_ge(scores, s_first(STEP[("C", 0, C_HEADS - 1)]) + 1)
            pool.dma_start(mem_nat, ins["mem_2"][0].rearrange("(t p) d -> p t d", p=P)).then_inc(mem_in, 16)
            pool.wait_ge(mem_sum, 1)
            pool.tensor_tensor(mem_rs, mem_sq, minus_half[:, 0:2], ALU.pow).then_inc(mem_rstd, 1)
            pool.wait_ge(scores, s_first(STEP[("B", 0, B_HEADS - 1)]) + 3)
            for n, name in enumerate(("ln1_g", "ln1_b")):
                pool.dma_start(ln_row[:, n, :], ins[name][0].partition_broadcast(P)).then_inc(ln1_in, 16)
            for n in range(2):
                for tt in range(2):
                    pool.wait_ge(ln_var, 2 * n + tt + 1)
                    pool.tensor_tensor(ln_rs[:, tt:tt + 1], mv3[:, tt, 1:2], minus_half[:, 0:1], ALU.pow
                                       ).then_inc(ln_rstd, 1)
                if n == 0:
                    pool.wait_ge(ln_done, 2)
                    for m, name in enumerate(("ln2_g", "ln2_b")):
                        pool.dma_start(ln_row[:, m, :], ins[name][0].partition_broadcast(P)).then_inc(ln2_in, 16)
            for l in range(LAYERS):
                if l == 0:
                    pool.wait_ge(ln_done, 4)
                    for m in range(LAYERS):
                        pool.dma_start(post_row[:, m, :], ins["post_norm_2"][m].partition_broadcast(P)
                                       ).then_inc(post_in, 16)
                pool.wait_ge(x_sum, l + 1)
                pool.tensor_tensor(x_rs, x_sq, minus_half[:, 0:2], ALU.pow).then_inc(x_rstd, 1)
                for tt in range(2):
                    pool.wait_ge(y_sum, 2 * l + tt + 1)
                    pool.tensor_tensor(y_rs[:, tt:tt + 1], y_sq[:, tt:tt + 1], minus_half[:, 0:1], ALU.pow
                                       ).then_inc(y_rstd, 1)

        @block.tensor
        def _(pe):
            def arrived(name):
                pe.wait_ge(loaded[ITEM[name] % RING], all_loaded(ITEM[name]))

            def from_act(job):
                pe.wait_ge(p_act, taken(JOB[job]))

            def from_dve(job):
                pe.wait_ge(p_dve, taken(JOB[job]))

            def slot(name):
                return slots[:, ITEM[name] % RING]

            def flat(name, n):
                s = ITEM[name] % RING
                return ring[:, s * SLOT:s * SLOT + n]

            def project(dst, w, a, b):
                for k in range(KC):
                    mm = pe.matmul(dst, w[:, k, a:b], xT3[:, k, :], start=(k == 0), stop=(k == KC - 1))
                return mm

            def natural(dst, src, tt, w, a, b):
                for k in range(KC):
                    mm = pe.matmul(dst, src[:, k, P * tt:P * tt + P], w[:, k, a:b], start=(k == 0), stop=(k == KC - 1))
                return mm

            def turn4(dst, src4, k):
                for c in range(2):
                    for tt in range(2):
                        mm = pe.transpose(dst[:, c * T + tt * P:c * T + tt * P + P], src4[:, tt, 2 * k + c, :], ident)
                return mm

            def run(job, j):
                kind = job[0]
                dst = bank(6 + j % 2)
                if j >= 2:
                    if BY_DVE[j - 2]:
                        pe.wait_ge(p_dve, taken(j - 2))
                    else:
                        pe.wait_ge(p_act, taken(j - 2))
                for name in item_of(job):
                    arrived(name)
                if kind == "vec":
                    pe.wait_ge(const_in, 16)
                    pe.wait_ge(vec_in, 16 * 10)
                    mm = pe.transpose(dst[:, 0:41], vec_rows[0:41, :], ident[0:41, 0:41])
                elif kind == "xt":
                    pe.wait_ge(x_in, 16)
                    pe.wait_ge(const_in, 16)
                    mm = turn4(dst, x4, job[1])
                elif kind == "bias":
                    pe.wait_ge(table_in, 48)
                    pe.wait_ge(setup, 2)
                    mm = pe.matmul(dst[0:BIAS_HEADS, 0:VALS + 1], rel_sb, bucket_sb, start=True, stop=True)
                elif kind == "cnat":
                    from_act(("xt", 3))
                    tt = job[1]
                    natural(dst[:, 0:Q_LORA], xT3, tt, slot("c_q"), 0, 256)
                    mm = natural(dst[:, Q_LORA:C_COLS], xT3, tt, slot("c_kv"), 0, C_COLS - Q_LORA)
                elif kind == "tile1":
                    from_act(("xt", 3))
                    n = job[1]
                    w = slot(item_of(job)[0])
                    mm = project(dst[:, 0:T], w, P * (n % 2), P * (n % 2) + P)
                elif kind == "avn":
                    from_act(("tile1", 3))
                    for tt in range(2):
                        mm = pe.transpose(dst[:, P * tt:P * tt + P], tile3[:, 3, P * tt:P * tt + P], ident)
                elif kind == "ct":
                    pe.wait_ge(c_scaled, 1)
                    for c in range(2):
                        for tt in range(2):
                            mm = pe.transpose(dst[:, c * T + tt * P:c * T + tt * P + P],
                                              c_nat[:, tt, P * c:P * c + P], ident)
                elif kind == "ckt":
                    pe.wait_ge(kc_roped, 1)
                    for tt in range(2):
                        pe.transpose(dst[:, P * tt:P * tt + P], c_nat[:, tt, Q_LORA:Q_LORA + KV_LORA], ident)
                    for tt in range(2):
                        mm = pe.transpose(dst[0:C_ROPE, T + P * tt:T + P * tt + P],
                                          c_nat[:, tt, Q_LORA + KV_LORA:C_COLS], ident)
                elif kind == "cq":
                    from_act(("ct",))
                    tt, half = job[1:]
                    w = flat("w_uq", 1536).rearrange("p (k n) -> p k n", k=2)
                    for k in range(2):
                        mm = pe.matmul(dst[:, 0:384], c_qT[:, k, P * tt:P * tt + P],
                                       w[:, k, 384 * half:384 * half + 384], start=(k == 0), stop=(k == 1))
                elif kind == "ck":
                    from_act(("ckt",))
                    w = flat("w_ukv", 1024)
                    for m in range(2):
                        h = 2 * job[1] + m
                        mm = pe.matmul(dst[0:C_NOPE, T * m:T * m + T], w[:, P * h:P * h + C_NOPE], c_kvT,
                                       start=True, stop=True)
                elif kind == "cv":
                    from_act(("ckt",))
                    tt = job[1]
                    w = flat("w_ukv", 1024).rearrange("p (h n) -> p h n", h=C_HEADS)[:, :, C_NOPE:P]
                    mm = pe.matmul(dst, c_kvT[:, P * tt:P * tt + P], w, start=True, stop=True)
                elif kind == "cqt":
                    pe.wait_ge(qc_roped, 1)
                    for m in range(2):
                        h = 2 * job[1] + m
                        for tt in range(2):
                            mm = pe.transpose(dst[0:C_QK, T * m + P * tt:T * m + P * tt + P],
                                              qc_nat[:, tt, C_QK * h:C_QK * h + C_QK], ident)
                elif kind == "bv":
                    g, tt = job[1:]
                    mm = natural(dst[:, 0:256], xT3, tt, slot(f"b_v{g}"), 0, 256)
                elif kind == "y1":
                    pe.wait_ge(o_out, STEP[("B", 0, B_HEADS - 1)] + 1)
                    mm = natural(dst[:, 0:256], mix3, job[2], slot(item_of(job)[0]), 0, 256)
                elif kind == "mt":
                    pe.wait_ge(mem_scaled, 2)
                    mm = turn4(dst, mem4, job[1])
                elif kind == "mk":
                    l, n = job[1:]
                    from_act(("mt", 3))
                    w = slot(f"mem_k{l}")
                    for k in range(KC):
                        mm = pe.matmul(dst[:, 0:T], w[:, k, P * n:P * n + P], memT[:, l, k, :],
                                       start=(k == 0), stop=(k == KC - 1))
                elif kind == "mv":
                    l, tt = job[1:]
                    mm = natural(dst[:, 0:256], memT[:, l], tt, slot(f"mem_v{l}"), 0, 256)
                elif kind == "x1t":
                    pe.wait_ge(ln_done, 2)
                    mm = turn4(dst, x4, job[1])
                elif kind == "logit":
                    from_act(("x1t", 3))
                    w = slot("router")
                    for k in range(KC):
                        mm = pe.matmul(dst[0:GROUPS + EXPERTS, 0:T], w[:, k, 0:GROUPS + EXPERTS], xT3[:, k, :],
                                       start=(k == 0), stop=(k == KC - 1))
                elif kind == "logitT":
                    from_dve(("logit",))
                    n = GROUPS + EXPERTS
                    for tt in range(2):
                        mm = pe.transpose(dst[:, n * tt:n * tt + n], logitT_sb[0:n, P * tt:P * tt + P],
                                          ident[0:n, 0:n])
                elif kind == "rank":
                    pe.wait_ge(chosen_done, 1)
                    e = EXPERTS
                    pe.matmul(dst[:, 0:e], before, chosen3[:, 0, :], start=True, stop=True)
                    pe.matmul(dst[:, e:2 * e], before, chosen3[:, 1, :], start=True, stop=False)
                    pe.matmul(dst[:, e:2 * e], ones, chosen3[:, 0, :], start=False, stop=True)
                    pe.matmul(dst[:, 2 * e:3 * e], ones, chosen3[:, 0, :], start=True, stop=False)
                    mm = pe.matmul(dst[:, 2 * e:3 * e], ones, chosen3[:, 1, :], start=False, stop=True)
                elif kind == "xt2":
                    pe.wait_ge(x_scaled, 2 * job[1] + 2)
                    mm = turn4(dst, xn4, job[2])
                elif kind == "tile2":
                    l, n = job[1:]
                    from_act(("xt2", l, 3))
                    mm = project(dst[:, 0:T], slot(item_of(job)[0]), P * (n % 2), P * (n % 2) + P)
                elif kind == "vn":
                    l, n = job[1:]
                    from_act(("tile2", l, n))
                    for tt in range(2):
                        mm = pe.transpose(dst[:, P * tt:P * tt + P], tile3[:, n, P * tt:P * tt + P], ident)
                elif kind == "swap":
                    l, n = job[1:]
                    from_act(("tile2", l, n))
                    mm = pe.matmul(dst[:, 0:T], swap, tile3[:, n, :], start=True, stop=True)
                elif kind == "hsq":
                    pe.wait_ge(squared, hsq_nth(*job[1:]))
                    mm = pe.matmul(dst[:, 0:T], headsum, sq_tile(job[2]), start=True, stop=True)
                elif kind == "hso":
                    l, n = job[1:]
                    pe.wait_ge(o_squared, 3 * l + n + 1)
                    mm = pe.matmul(dst[:, 0:T], headsum, sq_tile(n), start=True, stop=True)
                elif kind == "y2":
                    l, s, tt = job[1:]
                    pe.wait_ge(gated, KC * (l + 1))
                    mm = natural(dst[:, 0:256], mix3, tt, slot(f"out{l}_{s}"), 0, 256)
                mm.then_inc(p_ready, 1)

            def s_bank(n):
                if n >= 3:
                    owner = S_OWNER[n - 3]
                    if STEPS[owner][0] in "AB":
                        pe.wait_ge(maxed, owner + 1)
                    else:
                        pe.wait_ge(exped, owner + 1)
                return bank(n % 3)

            def run_scores(step):
                kind, l, h = STEPS[step]
                n = s_first(step)
                if kind == "A":
                    for tile in (h % 2, 2):
                        from_act(("tile1", tile))
                    base = HD * (h // 2)
                    q, k = tile3[base:base + HD, h % 2, :], tile3[base:base + HD, 2, :]
                    s = s_bank(n)
                    pe.matmul(s[:, 0:P], q[:, 0:P], k[:, 0:P], start=True, stop=True)
                    pe.matmul(s[:, P:3 * P], q[:, P:T], k[:, 0:T], start=True, stop=True).then_inc(scores, 1)
                elif kind == "C":
                    from_act(("cqt", 3))
                    pe.wait_ge(setup, 2)
                    q, k = qc3[0:C_QK, h, :], kc3[0:C_QK, h, :]
                    s = s_bank(n)
                    pe.matmul(s[:, 0:P], q[:, 0:P], k[:, 0:P], start=True, stop=False)
                    pe.matmul(s[:, 0:P], ident_b[:, :], causal_b[:, :], start=False, stop=True)
                    pe.matmul(s[:, P:3 * P], q[:, P:T], k[:, 0:T], start=True, stop=False)
                    pe.matmul(s[:, 2 * P:3 * P], ident_b[:, :], causal_b[:, :], start=False, stop=True
                              ).then_inc(scores, 1)
                elif kind == "B":
                    for g in range(B_GROUPS):
                        from_act(("tile1", 10 + 2 * g + 1))
                    base = HD * (h % 2)

                    def qk(g):
                        return (tile3[base:base + HD, 4 + 2 * g + h // 2, :],
                                tile3[base:base + HD, 10 + 2 * g + h // 2, :])

                    s = s_bank(n)
                    for g in range(B_GROUPS):
                        q, k = qk(g)
                        mm = pe.matmul(s[:, P * g:P * g + P], q[:, 0:P], k[:, 0:P], start=True, stop=True)
                    mm.then_inc(scores, 1)
                    s = s_bank(n + 1)
                    for g in range(2):
                        q, k = qk(g)
                        mm = pe.matmul(s[:, T * g:T * g + T], q[:, P:T], k[:, 0:T], start=True, stop=True)
                    mm.then_inc(scores, 1)
                    s = s_bank(n + 2)
                    q, k = qk(2)
                    pe.matmul(s[:, 0:T], q[:, P:T], k[:, 0:T], start=True, stop=True).then_inc(scores, 1)
                elif kind == "D":
                    pe.wait_ge(roped, max(rope_nth(l, h // 2), rope_nth(l, 3 + h // 2)))
                    banks = [s_bank(n), s_bank(n + 1)]
                    for tt in range(2):
                        for m in range(2):
                            base = HD * (h % 2) + 32 * m
                            q, k = tile3[base:base + 32, h // 2, :], tile3[base:base + 32, 3 + h // 2, :]
                            mm = pe.matmul(banks[m][:, T * tt:T * tt + T], q[:, P * tt:P * tt + P], k,
                                           start=True, stop=True)
                            if tt == 1:
                                mm.then_inc(scores, 1)
                else:
                    base = HD * (h % 2)
                    if kind == "G":
                        pe.wait_ge(k_copied, l + 1)
                        q = tile3[base:base + HD, 12 + h // 2, :]
                        same = base == HD * (h // 3)
                        k = tile3[base:base + HD, 15 if same else 16, :]
                    else:
                        from_act(("tile2", l, 20 + h // 2))
                        q = tile3[base:base + HD, 20 + h // 2, :]
                        k = mem_k[base:base + HD, l, h // 2, :]
                    s = s_bank(n)
                    for tt in range(2):
                        mm = pe.matmul(s[:, T * tt:T * tt + T], q[:, P * tt:P * tt + P], k, start=True, stop=True)
                    mm.then_inc(scores, 1)

            def run_turn(step):
                kind, l, h = STEPS[step]
                pe.wait_ge(normed, step + 1)
                pr = probs[:, 1152 * (step % 2):1152 * (step % 2) + 1152]
                for m in range(T_JOBS[kind]):
                    n = t_first(step) + m
                    if n >= 2:
                        pe.wait_ge(turned_out, n - 1)
                    dst = bank(3 + n % 2)
                    if kind in "AC":
                        at = [0, P, 2 * P]
                    elif kind == "B":
                        at = [P * m, 3 * P + T * m, 3 * P + T * m + P]
                    else:
                        at = [0, T, P, T + P]
                    for c, a in enumerate(at):
                        mm = pe.transpose(dst[:, P * c:P * c + P], pr[:, a:a + P], ident)
                    mm.then_inc(turned, 1)

            def run_out(step):
                kind, l, h = STEPS[step]
                par = h % 2
                if step >= 2:
                    pe.wait_ge(o_out, step - 1)
                o = bank(5)[HD * par:HD * par + HD, T * (step % 2):T * (step % 2) + T]
                if kind == "B":
                    from_act(("bv", B_GROUPS - 1, 1))
                elif kind == "A":
                    from_act(("avn",))
                elif kind == "C":
                    from_act(("cv", 1))
                elif kind == "D":
                    from_act(("vn", l, 6 + h // 2))
                elif kind == "G":
                    from_act(("vn", l, 16))
                for m in range(T_JOBS[kind]):
                    n = t_first(step) + m
                    pe.wait_ge(turned_out, n + 1)
                    pt = probsT[:, 512 * (n % 4):512 * (n % 4) + 512]
                    if kind == "A":
                        v = [va[:, tt, HD * (h // 2):HD * (h // 2) + HD] for tt in range(2)]
                    elif kind == "B":
                        v = [vb[:, tt, m, HD * h:HD * h + HD] for tt in range(2)]
                    elif kind == "C":
                        v = [vc3[:, tt, HD * h:HD * h + HD] for tt in range(2)]
                    elif kind == "D":
                        v = [v2[:, tt, h // 2, HD * par:HD * par + HD] for tt in range(2)]
                    elif kind == "G":
                        v = [v2[:, tt, 3, HD * (h // 3):HD * (h // 3) + HD] for tt in range(2)]
                    else:
                        v = [mem_v[:, l, tt, HD * h:HD * h + HD] for tt in range(2)]
                    last = m == T_JOBS[kind] - 1
                    pe.matmul(o, v[0], pt[:, 0:T], start=(m == 0), stop=False)
                    if kind in "ABC":
                        mm = pe.matmul(o[:, P:T], v[1], pt[:, T:T + P], start=False, stop=last)
                    else:
                        mm = pe.matmul(o, v[1], pt[:, T:2 * T], start=False, stop=last)
                mm.then_inc(o_ready, 1)

            def bunch(i, more, n):
                pe.wait_ge(placed, i + 1)
                for half in range(2):
                    dst = bank(4 + half)
                    for c in range(4):
                        k = 4 * half + c
                        for tt in range(2):
                            mm = pe.matmul(dst[:, P * c:P * c + P],
                                           x2[:, tt, :].rearrange("p (q k) -> p k q", k=KC)[:, k, :],
                                           places2[:, tt, :], start=(tt == 0), stop=(tt == 1))
                    mm.then_inc(gathered_ready, 1)
                for tt in range(2):
                    mm = pe.transpose(bank(7)[:, P * tt:P * tt + P], weighed2[:, tt, :], ident)
                mm.then_inc(back_ready, 1)
                pe.wait_ge(gathered_out, 2 * i + 2)
                if not more:
                    for k in range(2 * AT_ONCE):
                        pe.wait_ge(loaded[k], loaded_at(k, i))
                    for k in range(KC):
                        for e in range(AT_ONCE):
                            w = slots[:, 2 * e:2 * e + 2, k, :]
                            mm = pe.matmul(bank(6)[PLACES * e:PLACES * e + PLACES, :],
                                           gathered[:, k, PLACES * e:PLACES * e + PLACES], w,
                                           start=(k == 0), stop=(k == KC - 1))
                else:
                    for e in range(AT_ONCE):
                        pe.wait_ge(more_in, n * (32 * AT_ONCE) + 32 * (e + 1))
                        for m, w in enumerate((more_g, more_u)):
                            for k in range(KC):
                                mm = pe.matmul(bank(6)[PLACES * e:PLACES * e + PLACES, DE * m:DE * m + DE],
                                               gathered[:, k, PLACES * e:PLACES * e + PLACES],
                                               w[:, DE * k:DE * k + DE], start=(k == 0), stop=(k == KC - 1))
                        if e < AT_ONCE - 1:
                            mm.then_inc(more_used, 1)
                mm.then_inc(gu_ready, 1)
                pe.wait_ge(hidden_done, i + 1)
                for k in range(2):
                    mm = pe.transpose(bank(4)[:, P * k:P * k + P],
                                      hidden.rearrange("p (q k) -> p k q", k=2)[:, k, :], ident)
                mm.then_inc(hT_ready, 1)
                pe.wait_ge(hT_out, i + 1)
                pe.wait_ge(back_out, i + 1)
                if not more:
                    for k in range(AT_ONCE):
                        pe.wait_ge(loaded[2 * AT_ONCE + k], loaded_at(2 * AT_ONCE + k, i))
                    for half in range(2):
                        for k in range(2):
                            for e in range(AT_ONCE):
                                a = (2 * AT_ONCE + e) * SLOT + D * k + 512 * half
                                mm = pe.matmul(bank((7, 5)[half])[PLACES * e:PLACES * e + PLACES, :],
                                               hiddenT[:, k, PLACES * e:PLACES * e + PLACES], ring[:, a:a + 512],
                                               start=(k == 0), stop=(k == 1))
                        mm.then_inc(y_ready, 1)
                else:
                    for e in range(AT_ONCE):
                        pe.wait_ge(more_down_in, n * (16 * AT_ONCE) + 16 * (e + 1))
                        for half in range(2):
                            for k in range(2):
                                a = D * k + 512 * half
                                mm = pe.matmul(bank((7, 5)[half])[PLACES * e:PLACES * e + PLACES, :],
                                               hiddenT[:, k, PLACES * e:PLACES * e + PLACES], more_d[:, a:a + 512],
                                               start=(k == 0), stop=(k == 1))
                            if e == AT_ONCE - 1:
                                mm.then_inc(y_ready, 1)
                        if e < AT_ONCE - 1:
                            mm.then_inc(more_used, 1)
                pe.wait_ge(y0_out, i + 1)
                pe.wait_ge(y1_out, i + 1)
                for tt in range(2):
                    for half in range(2):
                        mm = pe.matmul(bank(2 * tt + half), back[:, P * tt:P * tt + P],
                                       y_e[:, 512 * half:512 * half + 512], start=False, stop=False,
                                       skip_group_check=True)
                mm.then_inc(summed, 1)

            def loaded_at(k, i):
                return all_loaded(FIRST_EXPERT + k) + i * 16

            def experts():
                pe.wait_ge(p_act, taken(JOB[("mv", 1, 1)]))
                pe.wait_ge(p_dve, taken(JOB[("rank",)]))
                pe.wait_ge(setup, 2)
                for b in range(4):
                    pe.matmul(bank(b), zeros_b[:, 0:P], zeros_b[:, :], start=True, stop=False, skip_group_check=True)
                bunch(0, False, None)
                with pe.Fori(1, BUNCHES) as i:
                    bunch(i, False, None)
                pe.wait_ge(routed, 1)
                some = pe.value_load(flags[0:1, 112:113], min_val=0, max_val=1)
                with pe.If(some):
                    with pe.Fori(0, ROUNDS - 1) as r:
                        with pe.Fori(0, BUNCHES) as g:
                            flag = pe.value_load(flags[0:1, bass.ds(r * BUNCHES + g, 1)], min_val=0, max_val=1)
                            with pe.If(flag):
                                n = pe.value_load(flags[0:1, bass.ds(r * BUNCHES + g + 56, 1)], min_val=0, max_val=55)
                                bunch(n + BUNCHES, True, n)
                for b in range(4):
                    mm = pe.matmul(bank(b), zeros_b[:, 0:P], zeros_b[:, :], start=False, stop=True, skip_group_check=True)
                mm.then_inc(moe_done, 1)

            j = step = drained = 0
            for jobs, what in TURNS:
                if what in STEP:
                    step = STEP[what]
                    run_scores(step)
                    if not opens(step) and not opens(step - 1):
                        run_out(step - 2)
                    drained = 0
                for job in jobs:
                    run(job, j)
                    j += 1
                if what == "experts":
                    experts()
                elif what is not None:
                    if not opens(step):
                        run_turn(step - 1)
                elif jobs == []:
                    if drained == 0:
                        run_out(step - 1)
                        run_turn(step)
                    else:
                        run_out(step)
                    drained += 1

        @block.scalar
        def _(act):
            chain = [0]

            def link(ins_):
                chain[0] += 1
                ins_.then_inc(act_chain, 1)
                act.wait_ge(act_chain, chain[0])

            act.preload_act_table_set("natural_log_exp_and_others")
            act.dma_start(bucket_sb[:, 0:VALS], ins["const_bucket"]).then_inc(table_in, 16)
            act.dma_start(rel_sb, ins["rel_bias"]).then_inc(table_in, 16)
            act.dma_start(unseen_sb, ins["const_unseen"]).then_inc(table_in, 16)

            def take(job, j):
                kind = job[0]
                src = bank(6 + j % 2)
                act.wait_ge(p_ready, j + 1)
                if kind == "vec":
                    op = act.activation(vecs[:, :], src[:, 0:41], ACT.Copy)
                elif kind in ("xt", "x1t"):
                    k = job[1]
                    op = act.activation(xT3[:, 2 * k:2 * k + 2, :], src.rearrange("p (c t) -> p c t", c=2), ACT.Copy)
                elif kind == "cnat":
                    op = act.activation(c_nat[:, job[1], :], src[:, 0:C_COLS], ACT.Copy)
                elif kind == "tile1":
                    n = job[1]
                    q = n < 2 or 4 <= n < 10
                    op = act.activation(tile3[:, n, :], src[:, 0:T], ACT.Copy, scale=(HD ** -0.5 if q else 1.0))
                elif kind == "avn":
                    op = act.activation(va, src[:, 0:256].rearrange("p (t n) -> p t n", t=2), ACT.Copy)
                elif kind == "ct":
                    for c in range(2):
                        op = act.activation(c_qT[:, c, :], src[:, T * c:T * c + T], ACT.Copy,
                                            scale=vecs[:, 32 + c:33 + c])
                elif kind == "ckt":
                    act.activation(c_kvT, src[:, 0:T], ACT.Copy, scale=vecs[:, 34:35])
                    op = act.activation(kc3[C_NOPE:C_QK, :, :],
                                        src[0:C_ROPE, T:2 * T].unsqueeze(1).to_broadcast([C_ROPE, C_HEADS, T]),
                                        ACT.Copy)
                elif kind == "cq":
                    tt, half = job[1:]
                    op = act.activation(qc_nat[:, tt, 384 * half:384 * half + 384], src[:, 0:384], ACT.Copy)
                elif kind == "ck":
                    k = job[1]
                    op = act.activation(kc3[0:C_NOPE, 2 * k:2 * k + 2, :],
                                        src[0:C_NOPE, :].rearrange("p (c t) -> p c t", c=2), ACT.Copy)
                elif kind == "cv":
                    op = act.activation(vc3[:, job[1], :], src, ACT.Copy)
                elif kind == "cqt":
                    k = job[1]
                    op = act.activation(qc3[0:C_QK, 2 * k:2 * k + 2, :],
                                        src[0:C_QK, :].rearrange("p (c t) -> p c t", c=2), ACT.Copy)
                elif kind == "bv":
                    g, tt = job[1:]
                    op = act.activation(vb[:, tt, g, :], src[:, 0:256], ACT.Copy)
                elif kind == "mt":
                    k = job[1]
                    for l in range(LAYERS):
                        for c in range(2):
                            at = 16 + 8 * l + 2 * k + c
                            op = act.activation(memT[:, l, 2 * k + c, :], src[:, T * c:T * c + T], ACT.Copy,
                                                scale=vecs[:, at:at + 1])
                elif kind == "mk":
                    l, n = job[1:]
                    op = act.activation(mem_k[:, l, n, :], src[:, 0:T], ACT.Copy)
                elif kind == "mv":
                    l, tt = job[1:]
                    op = act.activation(mem_v[:, l, tt, :], src[:, 0:256], ACT.Copy)
                elif kind == "xt2":
                    l, k = job[1:]
                    for c in range(2):
                        at = 8 * l + 2 * k + c
                        op = act.activation(xT3[:, 2 * k + c, :], src[:, T * c:T * c + T], ACT.Copy,
                                            scale=vecs[:, at:at + 1])
                elif kind == "tile2":
                    l, n = job[1:]
                    if 12 <= n <= 15:
                        act.activation(sq_tile(n), src[:, 0:T], ACT.Square).then_inc(squared, 1)
                        at = (37 if n < 15 else 39) + l
                        op = act.activation(tile3[:, n, :], src[:, 0:T], ACT.Copy, scale=vecs[:, at:at + 1])
                    elif n in GATE_TILES:
                        act.activation(exp_tile(n), src[:, 0:T], ACT.Exp, scale=-1.0)
                        op = act.activation(tile3[:, n, :], src[:, 0:T], ACT.Copy)
                    else:
                        op = act.activation(tile3[:, n, :], src[:, 0:T], ACT.Copy)
                elif kind == "vn":
                    l, n = job[1:]
                    op = act.activation(v2[:, :, V_TILES.index(n), :], src[:, 0:256].rearrange("p (t n) -> p t n", t=2),
                                        ACT.Copy)
                elif kind in ("hsq", "hso"):
                    dst = sq_tile(job[2])
                    link(act.activation(dst, src[:, 0:T], ACT.Ln, scale=1.0 / HD, bias=eps6))
                    op = act.activation(dst, dst, ACT.Exp, scale=-0.5)
                elif kind == "y2":
                    l, s, tt = job[1:]
                    op = act.activation(y_nat[:, tt, 256 * s:256 * s + 256], src[:, 0:256], ACT.Copy)
                op.then_inc(p_act, 1)

            def exps(step):
                kind, l, h = STEPS[step]
                act.wait_ge(maxed, step + 1)
                pr = probs[:, 1152 * (step % 2):1152 * (step % 2) + 1152]
                par = step % 2
                n_, s_ = nm[:, 4 * par:4 * par + 4], sm[:, 4 * par:4 * par + 4]
                if step >= 2:
                    act.wait_ge(turned, t_first(step - 1))
                b0 = s_first(step)
                if kind == "A":
                    act.activation(sink_e[:, 2 * par:2 * par + 2], n_[:, 0:2], ACT.Exp, bias=sink[:, h:h + 1])
                    act.activation(pr[:, 0:P], pr[:, 0:P], ACT.Exp, bias=n_[:, 0:1], accum_out=s_[:, 0:1])
                    op = act.activation(pr[:, P:3 * P], pr[:, P:3 * P], ACT.Exp, bias=n_[:, 1:2],
                                        accum_out=s_[:, 1:2])
                elif kind == "B":
                    act.activation(pr[:, 0:384], pr[:, 0:384], ACT.Exp, bias=n_[:, 0:1], accum_out=s_[:, 0:1])
                    op = act.activation(pr[:, 384:1152], pr[:, 384:1152], ACT.Exp, bias=n_[:, 1:2],
                                        accum_out=s_[:, 1:2])
                elif kind == "C":
                    s = bank(b0 % 3)
                    sc = C_QK ** -0.5
                    act.activation(pr[:, 0:P], s[:, 0:P], ACT.Exp, bias=n_[:, 0:1], scale=sc, accum_out=s_[:, 0:1])
                    op = act.activation(pr[:, P:3 * P], s[:, P:3 * P], ACT.Exp, bias=n_[:, 1:2], scale=sc,
                                        accum_out=s_[:, 1:2])
                elif kind == "D":
                    for m in range(2):
                        for tt in range(2):
                            c = 2 * m + tt
                            op = act.activation(pr[:, T * c:T * c + T], bank((b0 + m) % 3)[:, T * tt:T * tt + T],
                                                ACT.Exp, bias=n_[:, c:c + 1], scale=32 ** -0.5,
                                                accum_out=s_[:, c:c + 1])
                else:
                    s = bank(b0 % 3)
                    for tt in range(2):
                        op = act.activation(pr[:, T * tt:T * tt + T], s[:, T * tt:T * tt + T], ACT.Exp,
                                            bias=n_[:, tt:tt + 1], scale=HD ** -0.5, accum_out=s_[:, tt:tt + 1])
                op.then_inc(exped, 1)

            def take_turned(step):
                kind = STEPS[step][0]
                w = 3 * P if kind in "ABC" else 4 * P
                for m in range(T_JOBS[kind]):
                    n = t_first(step) + m
                    if n >= 4:
                        owner = max(s for s in range(len(STEPS)) if t_first(s) <= n - 4)
                        act.wait_ge(o_ready, owner + 1)
                    act.wait_ge(turned, n + 1)
                    act.activation(probsT[:, 512 * (n % 4):512 * (n % 4) + w], bank(3 + n % 2)[:, 0:w], ACT.Copy
                                   ).then_inc(turned_out, 1)

            def memory():
                act.wait_ge(mem_rstd, 1)
                for tt in range(2):
                    act.activation(mem_nat[:, tt, :], mem_nat[:, tt, :], ACT.Copy, scale=mem_rs[:, tt:tt + 1]
                                   ).then_inc(mem_scaled, 1)

            def bunch(i):
                for half in range(2):
                    act.wait_ge(gathered_ready, 2 * i + half + 1)
                    act.activation(gathered[:, 4 * half:4 * half + 4, :],
                                   bank(4 + half).rearrange("p (k s) -> p k s", k=4), ACT.Copy
                                   ).then_inc(gathered_out, 1)
                act.wait_ge(gu_ready, i + 1)
                act.activation(gate_e, bank(6)[:, 0:DE], ACT.Exp, scale=-1.0).then_inc(gate_exped, 1)
                act.wait_ge(hT_ready, i + 1)
                act.activation(hiddenT, bank(4)[:, 0:256].rearrange("p (k s) -> p k s", k=2), ACT.Copy
                               ).then_inc(hT_out, 1)
                act.wait_ge(y_ready, 2 * i + 1)
                if not isinstance(i, int):
                    act.wait_ge(summed, i)
                act.activation(y_e[:, 0:512], bank(7), ACT.Copy).then_inc(y0_out, 1)

            def experts():
                bunch(0)
                with act.Fori(1, BUNCHES) as i:
                    bunch(i)
                act.wait_ge(routed, 1)
                some = act.value_load(flags[0:1, 112:113], min_val=0, max_val=1)
                with act.If(some):
                    with act.Fori(0, ROUNDS - 1) as r:
                        with act.Fori(0, BUNCHES) as g:
                            flag = act.value_load(flags[0:1, bass.ds(r * BUNCHES + g, 1)], min_val=0, max_val=1)
                            with act.If(flag):
                                n = act.value_load(flags[0:1, bass.ds(r * BUNCHES + g + 56, 1)], min_val=0, max_val=55)
                                bunch(n + BUNCHES)

            j = step = drained = 0
            for jobs, what in TURNS:
                if what in STEP:
                    step = STEP[what]
                    exps(step)
                    drained = 0
                for job in jobs:
                    if job[0] == "mt" and job[1] == 0:
                        memory()
                    if not BY_DVE[j]:
                        take(job, j)
                        if job[0] == "tile2" and job[2] == 9 and job[1] == 0:
                            act.wait_ge(lam_sum, 1)
                            act.activation(lam_e, lam_s, ACT.Exp).then_inc(lam_exp, 1)
                    elif job[0] == "logitT":
                        act.wait_ge(route_dif, 1)
                        act.activation(g_exp, g_dif, ACT.Exp).then_inc(route_exp, 1)
                        act.wait_ge(route_m, 1)
                        act.activation(e_x, e_t, ACT.Exp).then_inc(route_x, 1)
                    j += 1
                if what == "experts":
                    experts()
                elif what is not None:
                    if not opens(step):
                        take_turned(step - 1)
                    if what[0] in "DG" and STEP[what] - STEP[("D", what[1], 0)] in (4, 6, 8):
                        n = (STEP[what] - STEP[("D", what[1], 0)]) // 2 - 2
                        act.wait_ge(o_out, step - 2)
                        act.activation(sq_tile(n), mix3[:, n, :], ACT.Square).then_inc(o_squared, 1)
                elif jobs == []:
                    if drained == 0:
                        take_turned(step)
                    drained += 1

        @block.vector
        def _(dve):
            chain = [0]

            def link(ins_):
                chain[0] += 1
                ins_.then_inc(dve_chain, 1)
                dve.wait_ge(dve_chain, chain[0])

            def rope4(dst1, dst2, cos, sin, t, last=None):
                t1, t2, t3, t4 = t
                dve.tensor_tensor(t1, dst1, cos, ALU.mult)
                dve.tensor_tensor(t2, dst2, sin, ALU.mult)
                dve.tensor_tensor(t3, dst1, sin, ALU.mult)
                link(dve.tensor_tensor(t4, dst2, cos, ALU.mult))
                link(dve.tensor_tensor(dst1, t1, t2, ALU.subtract))
                return dve.tensor_tensor(dst2, t3, t4, ALU.add)

            dve.memset(eps6, 1e-6)
            dve.memset(eps5, 1e-5)
            dve.memset(minus_half, -0.5).then_inc(setup, 1)
            dve.memset(bucket_sb[:, VALS:VALS + 1], 0.0)
            dve.memset(zeros_b[:, :], 0.0)
            dve.wait_ge(const_in, 16)
            dve.tensor_copy(ident_b[:, :], ident)
            dve.tensor_copy(causal_b[:, :], c_("causal")).then_inc(setup, 1)
            dve.wait_ge(small_in, 64)
            lp = lam_p.rearrange("p (l a b d) -> p l a b d", l=2, a=2, b=2)
            for l in range(LAYERS):
                link(dve.tensor_tensor(lp[:, l, :, 0, :], lp[:, l, :, 0, :], lp[:, l, :, 1, :], ALU.mult))
            for l in range(LAYERS):
                op = dve.tensor_reduce(lam_s[:, 2 * l:2 * l + 2], lp[:, l, :, 0, :], X, ALU.add)
            op.then_inc(lam_sum, 1)

            def rms(dst, src, n, junk, eps):
                link(dve.tensor_tensor_reduce(out=junk, in0=src, in1=src, scale=1.0, scalar=0.0,
                                              op0=ALU.mult, op1=ALU.add, accum_out=dst))
                return dve.tensor_scalar(dst, dst, 1.0 / n, eps, ALU.mult, ALU.add)

            def latent_norm():
                dve.wait_ge(p_act, taken(JOB[("cnat", 1)]))
                for tt in range(2):
                    link(rms(c_sq[:, tt:tt + 1], c_nat[:, tt, 0:Q_LORA], Q_LORA, rope_t[:, 0:Q_LORA], 1e-6))
                    op = rms(c_sq[:, 2 + tt:3 + tt], c_nat[:, tt, Q_LORA:Q_LORA + KV_LORA], KV_LORA,
                             rope_t[:, 256:256 + KV_LORA], 1e-6)
                    if tt == 0:
                        link(op)
                op.then_inc(c_sums, 1)
                dve.wait_ge(c_rstd, 1)
                for tt in range(2):
                    op = dve.tensor_scalar(c_nat[:, tt, 0:Q_LORA], c_nat[:, tt, 0:Q_LORA], c_rs[:, tt:tt + 1], None,
                                           ALU.mult)
                op.then_inc(c_scaled, 1)
                for tt in range(2):
                    op = dve.tensor_scalar(c_nat[:, tt, Q_LORA:Q_LORA + KV_LORA],
                                           c_nat[:, tt, Q_LORA:Q_LORA + KV_LORA], c_rs[:, 2 + tt:3 + tt], None,
                                           ALU.mult)
                link(op)
                a = Q_LORA + KV_LORA
                t = [rope_t[:, 32 * m:32 * m + 32].rearrange("p (t n) -> p t n", t=2) for m in range(4)]
                rope4(c_nat[:, :, a:a + HALF], c_nat[:, :, a + HALF:a + 2 * HALF],
                      c_("cos_c").rearrange("p (t n) -> p t n", t=2), c_("sin_c").rearrange("p (t n) -> p t n", t=2),
                      t).then_inc(kc_roped, 1)

            def latent_rope():
                dve.wait_ge(p_act, taken(JOB[("cq", 1, 1)]))
                for tt in range(2):
                    q = qc_nat[:, tt, :].rearrange("p (h n) -> p h n", h=C_HEADS)
                    a, b = (c_(n)[:, HALF * tt:HALF * tt + HALF].unsqueeze(1).to_broadcast([P, C_HEADS, HALF])
                            for n in ("cos_c", "sin_c"))
                    t = [rope_s[:, P * m:P * m + P].rearrange("p (h n) -> p h n", h=C_HEADS) for m in range(4)]
                    op = rope4(q[:, :, C_NOPE:C_NOPE + HALF], q[:, :, C_NOPE + HALF:C_QK], a, b, t)
                    if tt == 0:
                        link(op)
                op.then_inc(qc_roped, 1)

            def take(job, j):
                kind = job[0]
                src = bank(6 + j % 2)
                dve.wait_ge(p_ready, j + 1)
                if kind == "bias":
                    dve.wait_ge(table_in, 48)
                    dve.tensor_tensor(bias_sb, src[0:BIAS_HEADS, 0:VALS], unseen_sb, ALU.add).then_inc(p_dve, 1)
                elif kind == "y1":
                    s, tt = job[1:]
                    xs = x2[:, tt, 256 * s:256 * s + 256]
                    dve.scalar_tensor_tensor(xs, xs, ALPHA, src[:, 0:256], ALU.mult, ALU.add).then_inc(p_dve, 1)
                elif kind == "logit":
                    n = GROUPS + EXPERTS
                    dve.tensor_scalar(logitT_sb[0:n, :], src[0:n, 0:T], route_b[0:n, :], None, ALU.add
                                      ).then_inc(p_dve, 1)
                elif kind == "logitT":
                    dve.tensor_copy(lg, src[:, 0:72].rearrange("p (t n) -> p t n", t=2)).then_inc(p_dve, 1)
                elif kind == "rank":
                    e = EXPERTS
                    link(dve.tensor_tensor(rank, src[:, 0:2 * e], chosen, ALU.mult))
                    link(dve.tensor_scalar(e_sc, chosen, -ABSENT, ABSENT, ALU.mult, ALU.add))
                    link(dve.tensor_tensor(rank, rank, e_sc, ALU.add))
                    dve.tensor_reduce(cnt_b, src[:, 2 * e:3 * e].rearrange("p (b e) -> p b e", b=BUNCHES), X, ALU.max
                                      ).then_inc(p_dve, 1)
                elif kind == "swap":
                    l, n = job[1:]
                    cos, sin = (("cos_lin", "sin_lin") if n < 6 else ("cos_ax", "sin_ax"))
                    tl = tile3[:, n, :]
                    if n >= 12:
                        dve.wait_ge(p_act, taken(JOB[("hsq", l, n)]))
                    else:
                        dve.wait_ge(p_act, taken(JOB[("tile2", l, n)]))
                    if rope_nth(l, n) > 1:
                        dve.wait_ge(roped, rope_nth(l, n) - 1)
                    link(dve.tensor_tensor(rope_a, src[:, 0:T], c_(sin), ALU.mult))
                    op = dve.tensor_tensor(tl, tl, c_(cos), ALU.mult)
                    op.then_inc(p_dve, 1)
                    dve.wait_ge(p_dve, taken(j))
                    op = dve.tensor_tensor(tl, tl, rope_a, ALU.add)
                    if n >= 12:
                        link(op)
                        op = dve.tensor_tensor(tl, tl, sq_tile(n), ALU.mult)
                    op.then_inc(roped, 1)

            def exchange(l):
                dve.wait_ge(roped, rope_nth(l, 15))
                dve.wait_ge(p_act, taken(JOB[("vn", l, 16)]))
                link(dve.tensor_copy(tile3[0:HD, 16, :], tile3[HD:P, 15, :]))
                dve.tensor_copy(tile3[HD:P, 16, :], tile3[0:HD, 15, :]).then_inc(k_copied, 1)

            def maxes(step):
                kind, l, h = STEPS[step]
                par = step % 2
                m_, n_ = mx[:, 8 * par:8 * par + 8], nm[:, 4 * par:4 * par + 4]
                pr = probs[:, 1152 * par:1152 * par + 1152]
                b0 = s_first(step)
                if kind in "AB" and step >= 2:
                    dve.wait_ge(turned, t_first(step - 1))

                def biased(dst, s, b, m):
                    return dve.tensor_tensor_reduce(out=dst, in0=s, in1=b, scale=1.0, scalar=LOW, op0=ALU.add,
                                                    op1=ALU.max, accum_out=m)

                if kind == "A":
                    dve.wait_ge(scores, b0 + 1)
                    s = bank(b0 % 3)
                    biased(pr[:, 0:P], s[:, 0:P], bias3[:, h, P:T], m_[:, 0:1])
                    link(biased(pr[:, P:3 * P], s[:, P:3 * P], bias3[:, h, :], m_[:, 1:2]))
                    dve.tensor_scalar(n_[:, 0:2], m_[:, 0:2], sink[:, h:h + 1], -1.0, ALU.max, ALU.mult
                                      ).then_inc(maxed, 1)
                elif kind == "B":
                    heads = A_HEADS + h
                    dve.wait_ge(scores, b0 + 1)
                    biased(pr[:, 0:384].rearrange("p (g t) -> p g t", g=3),
                           bank(b0 % 3)[:, 0:384].rearrange("p (g t) -> p g t", g=3),
                           bias3[:, heads:BIAS_HEADS:B_HEADS, P:T], m_[:, 0:1])
                    dve.wait_ge(scores, b0 + 2)
                    biased(pr[:, 384:896].rearrange("p (g t) -> p g t", g=2),
                           bank((b0 + 1) % 3).rearrange("p (g t) -> p g t", g=2),
                           bias3[:, heads:heads + B_HEADS + 1:B_HEADS, :], m_[:, 1:2])
                    dve.wait_ge(scores, b0 + 3)
                    link(biased(pr[:, 896:1152], bank((b0 + 2) % 3)[:, 0:T], bias3[:, heads + 2 * B_HEADS, :],
                                m_[:, 2:3]))
                    link(dve.tensor_tensor(m_[:, 1:2], m_[:, 1:2], m_[:, 2:3], ALU.max))
                    dve.tensor_scalar(n_[:, 0:2], m_[:, 0:2], -1.0, None, ALU.mult).then_inc(maxed, 1)
                elif kind == "C":
                    dve.wait_ge(scores, b0 + 1)
                    s = bank(b0 % 3)
                    dve.tensor_reduce(m_[:, 0:1], s[:, 0:P], X, ALU.max)
                    link(dve.tensor_reduce(m_[:, 1:2], s[:, P:3 * P], X, ALU.max))
                    dve.tensor_scalar(n_[:, 0:2], m_[:, 0:2], -(C_QK ** -0.5), None, ALU.mult).then_inc(maxed, 1)
                elif kind == "D":
                    for tt in range(2):
                        dve.wait_ge(scores, b0 + tt + 1)
                        op = dve.tensor_reduce(m_[:, 2 * tt:2 * tt + 2],
                                               bank((b0 + tt) % 3).rearrange("p (m t) -> p m t", m=2), X, ALU.max)
                    link(op)
                    dve.tensor_scalar(n_[:, 0:4], m_[:, 0:4], -(32 ** -0.5), None, ALU.mult).then_inc(maxed, 1)
                else:
                    dve.wait_ge(scores, b0 + 1)
                    link(dve.tensor_reduce(m_[:, 0:2], bank(b0 % 3).rearrange("p (m t) -> p m t", m=2), X, ALU.max))
                    dve.tensor_scalar(n_[:, 0:2], m_[:, 0:2], -(HD ** -0.5), None, ALU.mult).then_inc(maxed, 1)

            def norms(step):
                kind, l, h = STEPS[step]
                par = step % 2
                s_ = sm[:, 4 * par:4 * par + 4]
                pr = probs[:, 1152 * par:1152 * par + 1152]
                dve.wait_ge(exped, step + 1)
                w = 4 if kind == "D" else 2
                if kind == "A":
                    link(dve.tensor_tensor(s_[:, 0:2], s_[:, 0:2], sink_e[:, 2 * par:2 * par + 2], ALU.add))
                link(dve.reciprocal(s_[:, 0:w], s_[:, 0:w]))
                if kind == "D":
                    dve.tensor_scalar(s_[:, 2:4], s_[:, 2:4], neg_lam[:, l:l + 1], None, ALU.mult)
                    for tt in range(2):
                        op = dve.tensor_scalar(pr[:, T * tt:T * tt + T], pr[:, T * tt:T * tt + T],
                                               s_[:, tt:tt + 1], None, ALU.mult)
                    link(op)
                    for tt in range(2):
                        op = dve.scalar_tensor_tensor(pr[:, T * tt:T * tt + T], pr[:, 512 + T * tt:512 + T * tt + T],
                                                      s_[:, 2 + tt:3 + tt], pr[:, T * tt:T * tt + T],
                                                      ALU.mult, ALU.add)
                else:
                    cut = {"A": (P, 3 * P), "C": (P, 3 * P), "B": (384, 1152)}.get(kind, (T, 2 * T))
                    dve.tensor_scalar(pr[:, 0:cut[0]], pr[:, 0:cut[0]], s_[:, 0:1], None, ALU.mult)
                    op = dve.tensor_scalar(pr[:, cut[0]:cut[1]], pr[:, cut[0]:cut[1]], s_[:, 1:2], None, ALU.mult)
                op.then_inc(normed, 1)

            def outs(step):
                kind, l, h = STEPS[step]
                par = h % 2
                chunk = {"A": 0, "B": 2, "C": 4, "D": 0, "G": 3, "M": 6}[kind] + h // 2
                dve.wait_ge(o_ready, step + 1)
                dve.tensor_copy(mix3[HD * par:HD * par + HD, chunk, :],
                                bank(5)[HD * par:HD * par + HD, T * (step % 2):T * (step % 2) + T]
                                ).then_inc(o_out, 1)

            def moments(tt):
                for c in range(2):
                    op = dve.bn_stats(stats4[:, tt, c, :], x2[:, tt, 512 * c:512 * c + 512])
                link(op)
                link(dve.bn_aggr(mv3[:, tt, :], stats4[:, tt, :, :].rearrange("p c s -> p (c s)")))
                dve.tensor_scalar(mv3[:, tt, 1:2], mv3[:, tt, 1:2], 1e-5, None, ALU.add).then_inc(ln_var, 1)

            def layer_norm(n, ready):
                dve.wait_ge(ready, 32)
                for tt in range(2):
                    dve.wait_ge(ln_rstd, 2 * n + tt + 1)
                    xs = x2[:, tt, :]
                    link(dve.tensor_scalar(xs, xs, mv3[:, tt, 0:1], ln_rs[:, tt:tt + 1], ALU.subtract, ALU.mult))
                    link(dve.tensor_tensor(xs, xs, ln_row[:, 0, :], ALU.mult))
                    dve.tensor_tensor(xs, xs, ln_row[:, 1, :], ALU.add).then_inc(ln_done, 1)

            def first_of(one, score, best, values3, n):
                def wide(a):
                    return a.unsqueeze(2).to_broadcast([P, 2, n])

                order = c_("first32")[:, EXPERTS - n:EXPERTS].unsqueeze(1).to_broadcast([P, 2, n])
                one3, score3 = (a.rearrange("p (t n) -> p t n", t=2) for a in (one, score))
                link(dve.tensor_reduce(best, values3, X, ALU.max))
                link(dve.tensor_tensor(score3, values3, wide(best), ALU.is_equal))
                link(dve.tensor_tensor(score3, score3, order, ALU.mult))
                link(dve.tensor_reduce(e_t, score3, X, ALU.max))
                link(dve.tensor_tensor(one3, score3, wide(e_t), ALU.is_equal))

            def route():
                dve.memset(ones, 1.0)
                dve.wait_ge(p_dve, taken(JOB[("logitT",)]))
                g3, e3 = lg[:, :, 0:GROUPS], lg[:, :, GROUPS:GROUPS + EXPERTS]
                first_of(g_one, g_sc, g_mx, g3, GROUPS)
                gw = g_mx.unsqueeze(2).to_broadcast([P, 2, GROUPS])
                dve.tensor_tensor(g_dif.rearrange("p (t n) -> p t n", t=2), g3, gw, ALU.subtract
                                  ).then_inc(route_dif, 1)
                m4 = e_m.rearrange("p (t g e) -> p t g e", t=2, g=GROUPS)
                s4 = e_sc.rearrange("p (t g e) -> p t g e", t=2, g=GROUPS)
                one = g_one.rearrange("p (t g) -> p t g", t=2)
                for tt in range(2):
                    ow = one[:, tt, :].unsqueeze(2).to_broadcast([P, GROUPS, PER_GROUP])
                    ev = e3[:, tt, :].rearrange("p (g e) -> p g e", g=GROUPS)
                    dve.tensor_tensor(m4[:, tt], ev, ow, ALU.mult)
                    link(dve.tensor_scalar(s4[:, tt], ow, -NEG, NEG, ALU.mult, ALU.add))
                link(dve.tensor_tensor(e_m, e_m, e_sc, ALU.add))
                m3 = e_m.rearrange("p (t n) -> p t n", t=2)
                first_of(e_one1, e_sc, e_mx1, m3, EXPERTS)
                link(dve.scalar_tensor_tensor(e_m, e_one1, 3.0 * NEG, e_m, ALU.mult, ALU.add))
                first_of(e_one2, e_sc, e_mx2, m3, EXPERTS)
                dve.tensor_tensor(chosen, e_one1, e_one2, ALU.add).then_inc(chosen_done, 1)
                dve.tensor_tensor(e_t, e_mx2, e_mx1, ALU.subtract).then_inc(route_m, 1)
                dve.wait_ge(route_exp, 1)
                link(dve.tensor_reduce(g_sum, g_exp.rearrange("p (t n) -> p t n", t=2), X, ALU.add))
                dve.wait_ge(route_x, 1)
                link(dve.tensor_scalar(w_1, e_x, 1.0, None, ALU.add))
                link(dve.tensor_tensor(w_1, w_1, g_sum, ALU.mult))
                link(dve.reciprocal(w_1, w_1))
                link(dve.tensor_tensor(w_2, w_1, e_x, ALU.mult))
                ww = [a.unsqueeze(2).to_broadcast([P, 2, EXPERTS]) for a in (w_1, w_2)]
                one1, one2 = (a.rearrange("p (t n) -> p t n", t=2) for a in (e_one1, e_one2))
                link(dve.tensor_tensor(gates3, one1, ww[0], ALU.mult))
                link(dve.tensor_tensor(m3, one2, ww[1], ALU.mult))
                link(dve.tensor_tensor(gates, gates, e_m, ALU.add))

            def more_rounds():
                dve.wait_ge(p_dve, taken(JOB[("rank",)]))
                n = (ROUNDS - 1) * BUNCHES
                cw = cnt_b.unsqueeze(1).to_broadcast([P, ROUNDS - 1, BUNCHES])
                link(dve.tensor_tensor(more_f.rearrange("p (r b) -> p r b", r=ROUNDS - 1), cw,
                                       c_("round_from").rearrange("p (r b) -> p r b", r=ROUNDS - 1), ALU.is_gt))
                link(dve.tensor_reduce(any_more, more_f, X, ALU.max))
                a, b = scan, e_sc[:, 0:n]
                link(dve.memset(a[:, 0:1], 0.0))
                link(dve.tensor_copy(a[:, 1:n], more_f[:, 0:n - 1]))
                d = 1
                while d < n:
                    link(dve.tensor_copy(b[:, 0:d], a[:, 0:d]))
                    link(dve.tensor_tensor(b[:, d:n], a[:, d:n], a[:, 0:n - d], ALU.add))
                    a, b = b, a
                    d *= 2
                link(dve.tensor_copy(flags[:, 0:n], more_f))
                link(dve.tensor_copy(flags[:, n:2 * n], a))
                dve.tensor_copy(flags[:, 2 * n:2 * n + 1], any_more).then_inc(routed, 1)

            LINKS = 4

            def bunch(i, g, r):
                def mlink(ins_, n):
                    ins_.then_inc(moe_chain, 1)
                    dve.wait_ge(moe_chain, i * LINKS + n)

                if isinstance(g, int):
                    rk, gt = (a[:, :, AT_ONCE * g:AT_ONCE * g + AT_ONCE] for a in (rank3, gates3))
                    pl = c_("places")[:, 0:PLACES]
                else:
                    rk, gt = (a[:, :, bass.ds(g * AT_ONCE, AT_ONCE)] for a in (rank3, gates3))
                    if r is None:
                        pl = c_("places")[:, 0:PLACES]
                    else:
                        at = CONST["places"][0] + PLACES
                        pl = const[:, bass.ds(r * PLACES + at, PLACES)]
                pw = pl.unsqueeze(1).to_broadcast([P, AT_ONCE, PLACES])
                for tt in range(2):
                    rw = rk[:, tt, :].unsqueeze(2).to_broadcast([P, AT_ONCE, PLACES])
                    op = dve.tensor_tensor(places4[:, tt], rw, pw, ALU.is_equal)
                mlink(op, 1)
                for tt in range(2):
                    gw = gt[:, tt, :].unsqueeze(2).to_broadcast([P, AT_ONCE, PLACES])
                    op = dve.tensor_tensor(weighed4[:, tt], places4[:, tt], gw, ALU.mult)
                op.then_inc(placed, 1)
                dve.wait_ge(back_ready, i + 1)
                if not isinstance(i, int):
                    dve.wait_ge(summed, i)
                dve.tensor_copy(back, bank(7)[:, 0:256]).then_inc(back_out, 1)
                dve.wait_ge(gate_exped, i + 1)
                mlink(dve.tensor_scalar(gate_e, gate_e, 1.0, None, ALU.add), 2)
                mlink(dve.reciprocal(gate_e, gate_e), 3)
                mlink(dve.tensor_tensor(gate_e, gate_e, bank(6)[:, 0:DE], ALU.mult), 4)
                dve.tensor_tensor(hidden, gate_e, bank(6)[:, DE:2 * DE], ALU.mult).then_inc(hidden_done, 1)
                dve.wait_ge(y_ready, 2 * i + 2)
                dve.tensor_copy(y_e[:, 512:1024], bank(5)).then_inc(y1_out, 1)

            def experts():
                more_rounds()
                bunch(0, 0, None)
                with dve.Fori(1, BUNCHES) as i:
                    bunch(i, i, None)
                some = dve.value_load(flags[0:1, 112:113], min_val=0, max_val=1)
                with dve.If(some):
                    with dve.Fori(0, ROUNDS - 1) as r:
                        with dve.Fori(0, BUNCHES) as g:
                            flag = dve.value_load(flags[0:1, bass.ds(r * BUNCHES + g, 1)], min_val=0, max_val=1)
                            with dve.If(flag):
                                n = dve.value_load(flags[0:1, bass.ds(r * BUNCHES + g + 56, 1)], min_val=0, max_val=55)
                                bunch(n + BUNCHES, g, r)
                dve.wait_ge(moe_done, 1)
                for tt in range(2):
                    for half in range(2):
                        xs = x2[:, tt, 512 * half:512 * half + 512]
                        op = dve.scalar_tensor_tensor(xs, xs, ALPHA, bank(2 * tt + half), ALU.mult, ALU.add)
                    link(op)
                    moments(tt)
                layer_norm(1, ln2_in)
                dve.wait_ge(ln_done, 4)

            def start_layer(l):
                for tt in range(2):
                    op = rms(x_sq[:, tt:tt + 1], x2[:, tt, :], D, xn2[:, tt, :], 1e-6)
                    if tt == 0:
                        link(op)
                op.then_inc(x_sum, 1)
                dve.wait_ge(x_rstd, l + 1)
                for tt in range(2):
                    dve.tensor_scalar(xn2[:, tt, :], x2[:, tt, :], x_rs[:, tt:tt + 1], None, ALU.mult
                                      ).then_inc(x_scaled, 1)

            def silu(l, n):
                e, tl = exp_tile(n), tile3[:, n, :]
                link(dve.tensor_scalar(e, e, 1.0, None, ALU.add))
                link(dve.reciprocal(e, e))
                dve.tensor_tensor(tl, tl, e, ALU.mult).then_inc(gate_silu, 1)

            def sub_norm(l, n):
                dve.wait_ge(p_act, taken(JOB[("hso", l, n)]))
                dve.scalar_tensor_tensor(mix3[:, n, :], mix3[:, n, :], sub_g[:, l:l + 1], sq_tile(n),
                                         ALU.mult, ALU.mult).then_inc(sub_done, 1)

            def gate_all(l):
                dve.wait_ge(gate_silu, len(GATE_TILES) * (l + 1))
                dve.wait_ge(sub_done, 3 * (l + 1))
                dve.wait_ge(o_out, STEP[("M", l, M_HEADS - 1)] + 1)
                for c in range(KC):
                    dve.tensor_tensor(mix3[:, c, :], mix3[:, c, :], tile3[:, GATE_TILES[c], :], ALU.mult
                                      ).then_inc(gated, 1)

            def end_layer(l, tt):
                dve.wait_ge(post_in, 32)
                dve.wait_ge(p_act, taken(JOB[("y2", l, 3, tt)]))
                rms(y_sq[:, tt:tt + 1], y_nat[:, tt, :], D, xn2[:, tt, :], 1e-6).then_inc(y_sum, 1)
                dve.wait_ge(y_rstd, 2 * l + tt + 1)
                link(dve.scalar_tensor_tensor(y_nat[:, tt, :], y_nat[:, tt, :], y_rs[:, tt:tt + 1],
                                              post_row[:, l, :], ALU.mult, ALU.mult))
                dve.tensor_tensor(x2[:, tt, :], x2[:, tt, :], y_nat[:, tt, :], ALU.add).then_inc(x_done, 1)
                dve.wait_ge(x_done, 2 * l + tt + 1)

            j = step = drained = 0
            for jobs, what in TURNS:
                if jobs and jobs[0][0] == "xt2":
                    start_layer(jobs[0][1])
                if what in STEP:
                    step = STEP[what]
                    if step == 0:
                        dve.wait_ge(bias_in, 16)
                    if not opens(step):
                        norms(step - 1)
                    maxes(step)
                    if not opens(step) and not opens(step - 1):
                        outs(step - 2)
                    drained = 0
                for job in jobs:
                    if job[0] == "ct":
                        latent_norm()
                    if BY_DVE[j]:
                        take(job, j)
                    if job == ("cq", 1, 1):
                        latent_rope()
                    if job[:2] == ("y1", 3):
                        dve.wait_ge(p_dve, taken(j))
                        moments(job[2])
                        if job[2] == 1:
                            layer_norm(0, ln1_in)
                    if job == ("logitT",):
                        route()
                    if job[0] == "tile2" and job[2] in GATE_TILES:
                        dve.wait_ge(p_act, taken(j))
                        silu(job[1], job[2])
                    if job == ("tile2", 0, 9):
                        dve.wait_ge(lam_exp, 1)
                        le = lam_e.rearrange("p (l a) -> p l a", l=2)
                        link(dve.tensor_tensor(neg_lam, le[:, :, 1], le[:, :, 0], ALU.subtract))
                        for l in range(LAYERS):
                            dve.tensor_scalar(neg_lam[:, l:l + 1], neg_lam[:, l:l + 1], -LAMBDA_INIT[l], None, ALU.add)
                            op = dve.tensor_scalar(sub_g[:, l:l + 1], vecs[:, 35 + l:36 + l], 1.0 - LAMBDA_INIT[l],
                                                   None, ALU.mult)
                        link(op)
                    if job[0] == "hso":
                        sub_norm(job[1], job[2])
                    if job[0] == "vn" and job[2] == 16:
                        exchange(job[1])
                    if job[0] == "y2" and job[2] == 3:
                        end_layer(job[1], job[3])
                    j += 1
                if what == "experts":
                    experts()
                elif what is not None:
                    if what == ("B", 0, 1):
                        dve.wait_ge(mem_in, 16)
                        link(rms(mem_sq[:, 0:1], mem_nat[:, 0, :], D, mem_junk, 1e-6))
                        rms(mem_sq[:, 1:2], mem_nat[:, 1, :], D, mem_junk, 1e-6).then_inc(mem_sum, 1)
                elif jobs == []:
                    if drained == 0:
                        norms(step)
                        outs(step - 1)
                    else:
                        outs(step)
                        if STEPS[step][0] == "M":
                            gate_all(STEPS[step][1])
                    drained += 1


_INS = ["x", "w_in", "w_out", "sinks", "rel_bias", "mla_q_norm", "mla_kv_norm", "w_uq", "w_ukv", "ln1_g", "ln1_b",
        "w_route_group", "b_route_group", "w_route_expert", "b_route_expert", "w_expert_gate", "w_expert_up",
        "w_expert_down", "ln2_g", "ln2_b", "mem_2", "pre_norm_2", "w_in_2", "diff_lambda_2", "diff_subln_2",
        "gqa_q_norm_2", "gqa_k_norm_2", "mem_norm_2", "w_mem_kv_2", "w_out_2", "post_norm_2"]


def kernel(**inputs):
    import numpy as _np
    import concourse.bacc as _bacc
    from concourse import mybir as _mybir
    from concourse.bass_utils import run_bass_kernel_spmd as _run

    nc = _bacc.Bacc("TRN2", target_bir_lowering=False, num_devices=1, dynamic_dma_scratch_size=4096)
    arrays, args = {}, {}
    given = {name: _np.ascontiguousarray(inputs[name]) for name in _INS}
    given.update(constants())
    for name, a in given.items():
        arrays[f"in_{name}_dram"] = a
        args[name] = nc.dram_tensor(f"in_{name}_dram", a.shape, _mybir.dt.from_np(a.dtype), kind="ExternalInput").ap()
    out = nc.dram_tensor("out_0_dram", (1, T, D), F32, kind="ExternalOutput").ap()
    build(nc, args, out)
    r = _run(nc, [arrays], core_ids=[0])
    return r.results[0]["out_0_dram"]
```

```python
import math
from contextlib import ExitStack

import numpy as np
import concourse.bass as bass
from concourse import mybir

F32 = mybir.dt.float32
BF16 = mybir.dt.bfloat16
F32R = mybir.dt.float32r
I32 = mybir.dt.int32
ALU = mybir.AluOpType
ACT = mybir.ActivationFunctionType
X = mybir.AxisListType.X

P = 128
T = 256
D = 1024
KC = D // P
COLS = 256
SLOT = KC * COLS
RING = 12
NEG = -1.0e30
LOW = -3.0e38
HD = 64

A_HEADS, B_HEADS, B_GROUPS, C_HEADS = 4, 4, 3, 8
DILATIONS = (1, 4, 16)
C_QK, C_NOPE, C_ROPE = 96, 64, 32
Q_LORA, KV_LORA = 256, 128
C_COLS = Q_LORA + KV_LORA + C_ROPE
A_COLS, B_COLS = 512, 2304
N_BUCKETS = 32
BIAS_HEADS = A_HEADS + B_HEADS * B_GROUPS
VALS = 3 * P - 1
GROUPS, PER_GROUP = 4, 8
EXPERTS = GROUPS * PER_GROUP
DE = 256
ALPHA = 2.0 ** 0.25
HALF = C_ROPE // 2

AT_ONCE = 4
PLACES = P // AT_ONCE
BUNCHES = EXPERTS // AT_ONCE
ROUNDS = T // PLACES
ABSENT = -1024.0

LAYERS = 2
D_HEADS, G_HEADS, M_HEADS = 6, 6, 4
TILES2 = 24
V_TILES = (6, 7, 8, 16)
GATE_TILES = (9, 10, 11, 17, 18, 19, 22, 23)
LAMBDA_INIT = [0.8 - 0.6 * math.exp(-0.3 * l) for l in range(LAYERS)]

_WIDTHS = [("ident", P), ("swap", P), ("headsum", P), ("before", P), ("cos_lin", T), ("sin_lin", T),
           ("cos_ax", T), ("sin_ax", T), ("causal", P), ("cos_c", 2 * HALF), ("sin_c", 2 * HALF),
           ("places", T), ("first32", EXPERTS), ("round_from", (ROUNDS - 1) * BUNCHES)]
CONST = {}
_at = 0
for _name, _w in _WIDTHS:
    CONST[_name] = (_at, _at + _w)
    _at += _w
N_CONST = _at


def constants():
    f = np.float32
    c = {}
    p = np.arange(P)
    c["ident"] = np.eye(P)
    partner = (p // 32) * 32 + (p + 16) % 32
    c["swap"] = (partner[:, None] == p[None, :]).astype(f)
    c["headsum"] = (p[:, None] // HD == p[None, :] // HD).astype(f)
    c["before"] = (p[:, None] < p[None, :]).astype(f)
    inv = (f(10000.0) ** (-np.arange(0, 32, 2, dtype=f) / f(32))).astype(f)
    t = np.arange(T)
    own = inv[p % 16][:, None]
    sign = np.where(p % 32 < 16, -1.0, 1.0)[:, None]
    lin = (t[None, :].astype(f) * own).astype(f)
    c["cos_lin"], c["sin_lin"] = np.cos(lin), np.sin(lin) * sign
    place = np.where((p % HD < 32)[:, None], (t // 64)[None, :], (t % 64)[None, :]).astype(f)
    ax = (place * own).astype(f)
    c["cos_ax"], c["sin_ax"] = np.cos(ax), np.sin(ax) * sign
    c["causal"] = np.where(p[None, :] <= p[:, None], 0.0, NEG)
    tok = p[:, None, None] + P * np.arange(2)[None, :, None]
    ang = (tok.astype(f) * inv[None, None, :]).astype(f)
    c["cos_c"], c["sin_c"] = np.cos(ang).reshape(P, -1), np.sin(ang).reshape(P, -1)
    c["places"] = np.broadcast_to(t[None, :], (P, T))
    c["first32"] = np.broadcast_to(EXPERTS - np.arange(EXPERTS)[None, :], (P, EXPERTS))
    c["round_from"] = np.broadcast_to(
        np.repeat(PLACES * np.arange(1, ROUNDS), BUNCHES)[None, :], (P, (ROUNDS - 1) * BUNCHES))
    table = np.concatenate([np.asarray(c[n], f).reshape(P, -1) for n, _ in _WIDTHS], axis=1)

    dist = 2 * P - 1 - np.arange(VALS)
    d = np.maximum(dist, 0)
    exact = N_BUCKETS // 2
    large = exact + (np.log(np.maximum(d, 1).astype(f) / f(exact)) / f(math.log(2048 / exact))
                     * f(N_BUCKETS - exact)).astype(np.int32)
    bucket = np.where(d < exact, d, np.minimum(large, N_BUCKETS - 1))
    of_bucket = (bucket[None, :] == np.arange(N_BUCKETS)[:, None]).astype(f)
    seen = np.zeros((BIAS_HEADS, VALS), bool)
    seen[:A_HEADS] = (dist >= 0) & (dist <= P - 1)
    for g, dil in enumerate(DILATIONS):
        at = A_HEADS + g * B_HEADS
        seen[at:at + B_HEADS] = (dist >= 0) & (dist % dil == 0) & (dist // dil <= P)
    return {"const_table": np.ascontiguousarray(table, dtype=f), "const_bucket": of_bucket,
            "const_unseen": np.where(seen, 0.0, NEG).astype(f)}


ITEMS = (["c_q", "c_kv", "w_uq", "w_ukv", "a_q", "a_kv"]
         + [f"b_{x}{g}" for g in range(B_GROUPS) for x in "qkv"]
         + [f"w_out{s}" for s in range(4)] + ["router"]
         + [f"mem_{x}{l}" for l in range(LAYERS) for x in "kv"])
FIRST_EXPERT = len(ITEMS)
assert FIRST_EXPERT % RING == 0
ITEMS += [f"expert{e}{y}" for b in range(BUNCHES) for x in ("gu", "d")
          for e in range(AT_ONCE * b, AT_ONCE * (b + 1)) for y in (("g", "u") if x == "gu" else ("d",))]
LOAD_ORDER2 = [0, 1, 2, 3, 4, 7, 8, 6, 9, 10, 5, 11]
for _l in range(LAYERS):
    ITEMS += [f"in{_l}_{n}" for n in LOAD_ORDER2] + [f"out{_l}_{s}" for s in range(4)]
ITEM = {name: n for n, name in enumerate(ITEMS)}
FIRST2 = FIRST_EXPERT + RING * BUNCHES
RING2 = 5
PIECES = {"router": 1 + GROUPS, "a_q": A_HEADS}


def slot_of(n):
    return n % RING if n < FIRST2 else (n - FIRST2) % RING2


def all_loaded(n):
    return 16 * sum(PIECES.get(ITEMS[m], 1) for m in range(n + 1) if slot_of(m) == slot_of(n))


TAKEN_BY_DVE = ("bias", "xt2", "y1", "logit", "logitT", "rank", "swap")


def schedule():
    turns = []
    jobs = [("xt", k) for k in range(4)] + [("cnat", 0), ("cnat", 1), ("bias",), ("vec",), ("tile1", 0), ("tile1", 1), ("tile1", 2), ("ct",), ("ckt",), ("tile1", 3),
             ("cq", 0, 0), ("cq", 0, 1), ("cq", 1, 0), ("cq", 1, 1), ("avn",)]
    jobs += [("ck", k) for k in range(4)] + [("cv", 0), ("cv", 1)] + [("cqt", k) for k in range(4)]
    turns.append((jobs, None))
    fill = []
    for g in range(B_GROUPS):
        fill += [("tile1", 4 + 2 * g), ("tile1", 5 + 2 * g), ("tile1", 10 + 2 * g), ("tile1", 11 + 2 * g),
                 ("bv", g, 0), ("bv", g, 1)]
    steps = [("A", 0, h) for h in range(A_HEADS)] + [("C", 0, h) for h in range(C_HEADS)]
    for n, s in enumerate(steps):
        turns.append((fill[n * len(fill) // 12:(n + 1) * len(fill) // 12], s))
    of_b = [[("mt", 0), ("mt", 1)], [("mt", 2), ("mt", 3)], [("mk", 0, 0), ("mk", 0, 1)], [("mk", 1, 0), ("mk", 1, 1)]]
    for h in range(B_HEADS):
        turns.append((of_b[h], ("B", 0, h)))
    turns += [([], None), ([], None)]
    jobs = [("y1", s, tt) for tt in range(2) for s in range(4)]
    jobs += [("mv", 0, 0), ("mv", 0, 1), ("mv", 1, 0)]
    jobs += [("x1t", k) for k in range(4)] + [("logit",), ("logitT",), ("mv", 1, 1), ("rank",)]
    turns.append((jobs, None))
    turns.append(([], "experts"))
    for l in range(LAYERS):
        jobs = [("xt2", l, tt, half) for tt in range(2) for half in range(2)]
        for n in range(6):
            jobs.append(("tile2", l, n))
            if n >= 1:
                jobs.append(("swap", l, n - 1))
        jobs += [("tile2", l, 6), ("swap", l, 5), ("tile2", l, 7), ("vn", l, 6), ("tile2", l, 8), ("vn", l, 7),
                 ("tile2", l, 9), ("vn", l, 8)]
        turns.append((jobs, None))
        steps = ([("D", l, h) for h in range(D_HEADS)] + [("G", l, h) for h in range(G_HEADS)]
                 + [("M", l, h) for h in range(M_HEADS)])
        tiles = [15, 16, 12, 13, 14, 17, 18, 20, 19, 10, 22, 21, 11, 23]
        later = [[] for _ in range(len(steps) + 3)]
        for n, t in enumerate(tiles):
            if 12 <= t <= 15:
                later[n + 1].append(("hsq", l, t))
                later[n + 2].insert(0, ("swap", l, t))
            if t == 16:
                later[n + 1].append(("vn", l, t))
        for n in range(3):
            later[5 + 2 * n].append(("hso", l, n))
        for n, s in enumerate(steps):
            first = [job for job in later[n] if job[0] == "swap"]
            last = [job for job in later[n] if job[0] != "swap"]
            tile = [("tile2", l, tiles[n])] if n < len(tiles) else []
            turns.append((first + tile + last, s))
        turns += [([], None), ([], None)]
        turns.append(([("y2", l, s, tt) for s, tt in ((0, 0), (0, 1), (1, 0), (1, 1), (2, 0), (3, 0), (2, 1), (3, 1))],
                      None))
    return turns


TURNS = schedule()
JOBS = [job for jobs, _ in TURNS for job in jobs]
JOB = {job: n for n, job in enumerate(JOBS)}
BY_DVE = [job[0] in TAKEN_BY_DVE for job in JOBS]


def taken(n):
    return sum(BY_DVE[m] == BY_DVE[n] for m in range(n + 1))


STEPS = [s for _, s in TURNS if isinstance(s, tuple)]
STEP = {s: n for n, s in enumerate(STEPS)}
S_JOBS = {"A": 1, "B": 3, "C": 1, "D": 2, "G": 1, "M": 1}
T_JOBS = {"A": 1, "B": 3, "C": 1, "D": 1, "G": 1, "M": 1}


def s_first(step):
    return sum(S_JOBS[s[0]] for s in STEPS[:step])


def t_first(step):
    return sum(T_JOBS[s[0]] for s in STEPS[:step])



def opens(step):
    return STEPS[step] in (("A", 0, 0), ("D", 0, 0), ("D", 1, 0))


S_OWNER = [n for n, s in enumerate(STEPS) for _ in range(S_JOBS[s[0]])]


def item_of(job):
    kind = job[0]
    if kind == "cnat":
        return ["c_q", "c_kv"]
    if kind == "cq":
        return ["w_uq"]
    if kind in ("ck", "cv"):
        return ["w_ukv"]
    if kind == "tile1":
        n = job[1]
        return ["a_q"] if n < 2 else ["a_kv"] if n < 4 else [f"b_q{(n - 4) // 2}"] if n < 10 else [f"b_k{(n - 10) // 2}"]
    if kind == "bv":
        return [f"b_v{job[1]}"]
    if kind == "y1":
        return [f"w_out{job[1]}"]
    if kind == "logit":
        return ["router"]
    if kind in ("mk", "mv"):
        return [f"mem_{kind[1]}{job[1]}"]
    if kind == "tile2":
        return [f"in{job[1]}_{job[2] // 2}"]
    if kind == "y2":
        return [f"out{job[1]}_{job[2]}"]
    return []


LAST_JOB = {}
for _n, _job in enumerate(JOBS):
    for _name in item_of(_job):
        LAST_JOB[_name] = _n

UNITS = 6
TILES_OF = [[job[2] for job in JOBS if job[0] == "tile2" and job[1] == l] for l in range(LAYERS)]
SPLITS = []
for _l in range(LAYERS):
    SPLITS += [("tile2", _l, _n) for _n in TILES_OF[_l]] + [("y2", _l, _s) for _s in range(4)]
SPLIT = {what: n for n, what in enumerate(SPLITS)}


def units_before(split):
    return sum(1 if what[0] == "tile2" else 2 for what in SPLITS[:split])


def users(split):
    what = SPLITS[split]
    return [JOB[what]] if what[0] == "tile2" else [JOB[what + (tt,)] for tt in range(2)]


UNIT_OWNER = [n for n, what in enumerate(SPLITS) for _ in range(1 if what[0] == "tile2" else 2)]


def freed_by(split):
    first = units_before(split)
    before = [UNIT_OWNER[u - UNITS] for u in range(first, len(UNIT_OWNER)) if UNIT_OWNER[u] == split and u >= UNITS]
    return max((max(users(b)) for b in before), default=-1)


SPLIT_AT = {}
_at = 0
for _n, _what in enumerate(SPLITS):
    _at = max(_at, freed_by(_n) + 1)
    if _what[0] == "tile2":
        _i = TILES_OF[_what[1]].index(_what[2])
        if _i >= 2:
            _at = max(_at, JOB[("tile2", _what[1], TILES_OF[_what[1]][max(_i - 3, 0)])])
    if _n >= 3:
        SPLIT_AT.setdefault(_at, []).append(_n)
FIRST_SPLITS = range(3)


def build(nc, ins, out):
    ctx = ExitStack()
    with ctx:
        def sb(name, shape, dt=F32):
            return ctx.enter_context(nc.sbuf_tensor(name, shape, dt))

        def sem(name):
            return ctx.enter_context(nc.semaphore(name))

        with nc.sbuf_tensor("slots_before", [P, RING2 * SLOT], F32), \
                nc.sbuf_tensor("w_high", [P, UNITS * SLOT // 2], F32R) as w_high, \
                nc.sbuf_tensor("w_low", [P, UNITS * SLOT // 2], F32R) as w_low, \
                nc.sbuf_tensor("a_high", [P, KC * T], F32R) as a_high, \
                nc.sbuf_tensor("x_low", [P, KC * T], F32R) as x_low, \
                nc.sbuf_tensor("mix_low", [P, KC * T], F32R) as mix_low:
            pass
        ring = sb("ring", [P, RING * SLOT])
        xT = sb("xT", [P, KC * T])
        mixT = sb("mixT", [P, KC * T])
        const = sb("const", [P, N_CONST])
        x_nat = sb("x_nat", [P, 2 * D])
        tiles = sb("tiles", [P, TILES2 * T])
        v_nat = sb("v_nat", [P, 2048])
        q_c = sb("q_c", [P, C_HEADS * T])
        k_c = sb("k_c", [P, C_HEADS * T])
        v_c = sb("v_c", [P, 1024])
        bias = sb("bias", [P, BIAS_HEADS * T])
        probs = sb("probs", [P, 2 * 1152])
        probsT = sb("probsT", [P, 4 * 512])
        vecs = sb("vecs", [P, 41])
        small = sb("small", [P, 256])
        ident_b = sb("ident_b", [P, P], BF16)
        causal_b = sb("causal_b", [P, P], BF16)
        zeros_b = sb("zeros_b", [P, 512], BF16)
        flags = sb("flags", [P, 2 * (ROUNDS - 1) * BUNCHES + 2], I32)
        psum = ctx.enter_context(nc.psum_tensor("psum", [P, 8, 512], F32))

        def bank(n):
            return psum[:, n, :]

        def c_(name):
            a, b = CONST[name]
            return const[:, a:b]

        ident, swap, headsum, before = c_("ident"), c_("swap"), c_("headsum"), c_("before")
        slots = ring[:, :].rearrange("p (s k n) -> p s k n", s=RING, k=KC)
        x2 = x_nat[:, :].rearrange("p (t d) -> p t d", t=2)
        x4 = x_nat[:, :].rearrange("p (t k q) -> p t k q", t=2, k=KC)
        xT3 = xT[:, :].rearrange("p (k t) -> p k t", k=KC)
        y_nat = tiles[:, 0:2048].rearrange("p (t d) -> p t d", t=2)
        mix3 = mixT[:, :].rearrange("p (k t) -> p k t", k=KC)
        a_high3, x_low3, mix_low3 = (a[:, :].rearrange("p (k t) -> p k t", k=KC) for a in (a_high, x_low, mix_low))

        def split_of(n):
            wide = P if SPLITS[n][0] == "tile2" else COLS
            a = units_before(n) % UNITS * KC * P
            return [w[:, a:a + KC * wide].rearrange("p (k n) -> p k n", k=KC) for w in (w_high, w_low)]

        def raw_of(n):
            kind, l, m = SPLITS[n]
            s = slots[:, slot_of(ITEM[f"in{l}_{m // 2}" if kind == "tile2" else f"out{l}_{m}"])]
            return s[:, :, P * (m % 2):P * (m % 2) + P] if kind == "tile2" else s

        def as_f32(a):
            return a.bitcast(F32)
        tile3 = tiles[:, :].rearrange("p (n t) -> p n t", n=TILES2)
        qc3 = q_c[:, :].rearrange("p (h t) -> p h t", h=C_HEADS)
        kc3 = k_c[:, :].rearrange("p (h t) -> p h t", h=C_HEADS)
        vc3 = v_c[:, :].rearrange("p (t n) -> p t n", t=2)
        bias3 = bias[:, :].rearrange("p (h t) -> p h t", h=BIAS_HEADS)
        va = v_nat[:, 0:256].rearrange("p (t n) -> p t n", t=2)
        vb = v_nat[:, 256:1792].rearrange("p (t g n) -> p t g n", t=2, g=B_GROUPS)
        v2 = v_nat[:, 0:1024].rearrange("p (t n m) -> p t n m", t=2, n=4)
        ln_row = tiles[:, 4096:6144].rearrange("p (n d) -> p n d", n=2)
        post_row = bias[:, 0:2048].rearrange("p (n d) -> p n d", n=2)
        vec_rows = q_c[:, 1024:1024 + P]
        c_nat = mixT[:, 0:2 * C_COLS].rearrange("p (t n) -> p t n", t=2)
        c_qT = mixT[:, 832:832 + 512].rearrange("p (k t) -> p k t", k=2)
        c_kvT = mixT[:, 1344:1600]
        rope_t = mixT[:, 1600:2048]
        qc_nat = probs[:, 0:1536].rearrange("p (t n) -> p t n", t=2)
        mem_nat = tiles[:, 4096:6144].rearrange("p (t d) -> p t d", t=2)
        mem4 = tiles[:, 4096:6144].rearrange("p (t k q) -> p t k q", t=2, k=KC)
        memT = [a[:, :].rearrange("p (k t) -> p k t", k=KC) for a in (xT, k_c)]
        mem_k = v_c[:, :].rearrange("p (l n t) -> p l n t", l=LAYERS, n=2)
        mem_v = v_nat[:, 1024:2048].rearrange("p (l t n) -> p l t n", l=LAYERS, t=2)
        places4 = tiles[:, 0:256].rearrange("p (t e s) -> p t e s", t=2, e=AT_ONCE)
        places2 = tiles[:, 0:256].rearrange("p (t s) -> p t s", t=2)
        weighed4 = tiles[:, 256:512].rearrange("p (t e s) -> p t e s", t=2, e=AT_ONCE)
        weighed2 = tiles[:, 256:512].rearrange("p (t s) -> p t s", t=2)
        back = tiles[:, 512:768]
        gate_e = tiles[:, 768:1024]
        hidden = tiles[:, 1024:1280]
        hiddenT = tiles[:, 1280:1536].rearrange("p (k s) -> p k s", k=2)
        y_e = tiles[:, 1536:2560]
        gathered = q_c[:, 0:1024].rearrange("p (k s) -> p k s", k=KC)
        more_g = xT[:, :]
        more_u = mixT[:, :]
        more_d = k_c[:, :]
        xn2 = probs[:, 0:2048].rearrange("p (t d) -> p t d", t=2)
        xn4 = probs[:, 0:2048].rearrange("p (t k q) -> p t k q", t=2, k=KC)

        used = [0]

        def col(n, rows_=P):
            a = used[0]
            used[0] += n
            assert used[0] <= 256
            return small[0:rows_, a:a + n]

        eps6, eps5 = col(1), col(1)
        sink = col(A_HEADS)
        route_b = col(1)
        c_sq, c_rs = col(4), col(4)
        mx, nm, sm, sink_e = col(2 * 8), col(2 * 4), col(2 * 4), col(2 * 2)
        ln_stats, ln_mv, ln_rs = col(2 * 12), col(4), col(2)
        mem_sq, mem_rs = col(2), col(2)
        x_sq, x_rs = col(2), col(2)
        y_sq, y_ms, y_rs = col(8), col(2), col(2)
        lam_s, lam_e, neg_lam = col(4), col(4), col(2)
        lam_p = v_nat[:, 1024:1280]
        sub_g = col(2)
        stats4 = ln_stats.rearrange("p (t c s) -> p t c s", t=2, c=2)
        mv3 = ln_mv.rearrange("p (t s) -> p t s", t=2)
        bucket_sb, rel_sb = probsT[0:N_BUCKETS, 0:VALS + 1], probsT[0:N_BUCKETS, 384:384 + BIAS_HEADS]
        unseen_sb, bias_sb = probsT[0:BIAS_HEADS, 512:512 + VALS], probsT[0:BIAS_HEADS, 1024:1024 + VALS]
        rope_s = q_c[:, 0:512]
        mem_junk = q_c[:, 0:D]
        rope_a = q_c[:, 7 * T:8 * T]

        def sq_tile(n):
            m = n - 12 if n >= 12 else 4 + n
            return q_c[:, T * m:T * m + T]

        def exp_tile(n):
            m = GATE_TILES.index(n)
            return k_c[:, T * m:T * m + T]

        rt = [0]

        def rcol(n):
            a = rt[0]
            rt[0] += n
            assert rt[0] <= 2048
            return probs[:, a:a + n]

        logitT_sb = rcol(T)
        lg = rcol(72).rearrange("p (t n) -> p t n", t=2)
        g_mx, g_eq, g_sc, g_one, g_dif, g_exp, g_sum, p_grp = (rcol(2), rcol(8), rcol(8), rcol(8), rcol(8), rcol(8),
                                                               rcol(2), rcol(2))
        e_m, e_sc, e_one1, e_one2 = rcol(64), rcol(64), rcol(64), rcol(64)
        e_mx1, e_mx2, e_t, e_x, w_1, w_2 = rcol(2), rcol(2), rcol(2), rcol(2), rcol(2), rcol(2)
        chosen, gates, rank = rcol(64), rcol(64), rcol(64)
        cnt, cnt_b, more_f, scan = rcol(EXPERTS), rcol(BUNCHES), rcol(56), rcol(56)
        any_more = rcol(1)
        ones = rcol(P)
        rank3 = rank.rearrange("p (t e) -> p t e", t=2)
        gates3 = gates.rearrange("p (t e) -> p t e", t=2)
        chosen3 = chosen.rearrange("p (t e) -> p t e", t=2)

        bias_dram = nc.dram_tensor("bias_rows", [BIAS_HEADS, P, VALS], F32, kind="Internal").ap()

        loaded = [sem(f"loaded{s}") for s in range(RING)]
        x_in, const_in, vec_in, small_in = sem("x_in"), sem("const_in"), sem("vec_in"), sem("small_in")
        ln1_in, ln2_in, post_in = sem("ln1_in"), sem("ln2_in"), sem("post_in")
        table_in, bias_out, bias_in, mem_in = sem("table_in"), sem("bias_out"), sem("bias_in"), sem("mem_in")
        p_ready = sem("p_ready")
        p_act, p_dve = sem("p_act"), sem("p_dve")
        setup = sem("setup")
        c_sums, c_rstd, c_scaled = sem("c_sums"), sem("c_rstd"), sem("c_scaled")
        qc_roped, kc_roped = sem("qc_roped"), sem("kc_roped")
        scores, maxed, exped, sink_exped = sem("scores"), sem("maxed"), sem("exped"), sem("sink_exped")
        normed, turned, turned_out = sem("normed"), sem("turned"), sem("turned_out")
        o_ready, o_out = sem("o_ready"), sem("o_out")
        mem_sum, mem_scaled = sem("mem_sum"), sem("mem_scaled")
        ln_var, ln_rstd, ln_done = sem("ln_var"), sem("ln_rstd"), sem("ln_done")
        route_dif, route_exp, route_m, route_x = sem("route_dif"), sem("route_exp"), sem("route_m"), sem("route_x")
        chosen_done, routed = sem("chosen_done"), sem("routed")
        placed, gathered_ready, gathered_out = sem("placed"), sem("gathered_ready"), sem("gathered_out")
        back_ready, back_out = sem("back_ready"), sem("back_out")
        gu_ready, gate_exped, hidden_done = sem("gu_ready"), sem("gate_exped"), sem("hidden_done")
        hT_ready, hT_out = sem("hT_ready"), sem("hT_out")
        y_ready, y0_out, y1_out, summed = sem("y_ready"), sem("y0_out"), sem("y1_out"), sem("summed")
        more_in, more_down_in, more_used = sem("more_in"), sem("more_down_in"), sem("more_used")
        moe_done = sem("moe_done")
        x_scaled = sem("x_scaled")
        y_sum, y_rstd, x_done = sem("y_sum"), sem("y_rstd"), sem("x_done")
        lam_sum, lam_exp = sem("lam_sum"), sem("lam_exp")
        sigmoid = sem("sigmoid")
        roped, squared, gate_silu, gated = sem("roped"), sem("squared"), sem("gate_silu"), sem("gated")
        o_squared, sub_done, k_copied = sem("o_squared"), sem("sub_done"), sem("k_copied")
        highs, lows = sem("highs"), sem("lows")
        x_highs, x_lows, mix_highs, mix_lows = sem("x_highs"), sem("x_lows"), sem("mix_highs"), sem("mix_lows")
        act_chain, dve_chain, moe_chain = sem("act_chain"), sem("dve_chain"), sem("moe_chain")
        stored = sem("stored")

        def rope_nth(l, n):
            order = [j[2] for j in JOBS if j[0] == "swap" and j[1] == l]
            return l * len(order) + order.index(n) + 1

        def silu_nth(l, n):
            order = [j[2] for j in JOBS if j[0] == "tile2" and j[1] == l and j[2] in GATE_TILES]
            return l * len(order) + order.index(n) + 1

        def hsq_nth(l, n):
            order = [j[2] for j in JOBS if j[0] == "hsq" and j[1] == l]
            return l * len(order) + order.index(n) + 1

        block = ctx.enter_context(nc.Block())

        @block.sync
        def _(sp):
            def last_split(n):
                return max(m for m, (kind, l, k) in enumerate(SPLITS)
                           if ITEMS[n] == (f"in{l}_{k // 2}" if kind == "tile2" else f"out{l}_{k}"))

            def source(name):
                w_in, w_out = ins["w_in"][0], ins["w_out"][0]

                def k_rows(w, a, b):
                    return w[:, a:b].rearrange("(k p) n -> p k n", p=P)

                if name == "c_q":
                    return k_rows(w_in, A_COLS + B_COLS, A_COLS + B_COLS + Q_LORA)
                if name == "c_kv":
                    return k_rows(w_in, A_COLS + B_COLS + Q_LORA, A_COLS + B_COLS + C_COLS)
                if name == "a_kv":
                    return k_rows(w_in, 256, 512)
                if name[:2] == "b_":
                    at = A_COLS + 768 * "qkv".index(name[2]) + 256 * int(name[3])
                    return k_rows(w_in, at, at + 256)
                if name[:5] == "w_out":
                    s = int(name[5])
                    return k_rows(w_out, 256 * s, 256 * s + 256)
                if name[:4] == "mem_":
                    at = 256 * "kv".index(name[4])
                    return k_rows(ins["w_mem_kv_2"][int(name[5])], at, at + 256)
                if name[:2] == "in":
                    l, n = int(name[2]), int(name[4:])
                    return k_rows(ins["w_in_2"][l], 256 * n, 256 * n + 256)
                l, s = int(name[3]), int(name[5])
                return k_rows(ins["w_out_2"][l], 256 * s, 256 * s + 256)

            def load(n):
                name, s = ITEMS[n], slot_of(n)
                if name == "w_uq":
                    sp.dma_start(ring[:, s * SLOT:s * SLOT + 1536].rearrange("p (k n) -> p k n", k=2),
                                 ins["w_uq"][0].rearrange("(k p) n -> p k n", p=P)).then_inc(loaded[s], 16)
                elif name == "w_ukv":
                    sp.dma_start(ring[:, s * SLOT:s * SLOT + 1024], ins["w_ukv"][0]).then_inc(loaded[s], 16)
                elif name == "a_q":
                    for m, h in enumerate((0, 2, 1, 3)):
                        sp.dma_start(slots[:, s, :, HD * m:HD * m + HD],
                                     ins["w_in"][0, :, HD * h:HD * h + HD].rearrange("(k p) n -> p k n", p=P)
                                     ).then_inc(loaded[s], 16)
                elif name == "router":
                    sp.dma_start(slots[:, s, :, 0:GROUPS],
                                 ins["w_route_group"][0].rearrange("(k p) n -> p k n", p=P)).then_inc(loaded[s], 16)
                    for g in range(GROUPS):
                        sp.dma_start(slots[:, s, :, GROUPS + PER_GROUP * g:GROUPS + PER_GROUP * (g + 1)],
                                     ins["w_route_expert"][0, g].rearrange("(k p) n -> p k n", p=P)
                                     ).then_inc(loaded[s], 16)
                else:
                    src = source(name)
                    sp.dma_start(slots[:, s, :, 0:src.shape[2]], src).then_inc(loaded[s], 16)

            def load_bunch(b, first):
                for k in range(RING):
                    if not first:
                        if k == 0:
                            sp.wait_ge(gu_ready, b)
                        if k == 2 * AT_ONCE:
                            sp.wait_ge(y_ready, 2 * b)
                    elif FIRST_EXPERT + k >= RING:
                        sp.wait_ge(p_ready, LAST_JOB[ITEMS[FIRST_EXPERT + k - RING]] + 1)
                    name = ("w_expert_gate", "w_expert_up")[k % 2] if k < 2 * AT_ONCE else "w_expert_down"
                    e = k // 2 if k < 2 * AT_ONCE else k - 2 * AT_ONCE
                    w = ins[name][0, bass.ds(b * AT_ONCE + e, 1)]
                    sp.dma_start(ring[:, k * SLOT:(k + 1) * SLOT],
                                 w.rearrange("o (p k) n -> p (o k n)", p=P)).then_inc(loaded[k], 16)

            def small_loads():
                def vec(at, n, src):
                    sp.dma_start(vec_rows[at:at + n, 0:src.shape[1]], src).then_inc(vec_in, 16)

                vec(0, 16, ins["pre_norm_2"].rearrange("l (k q) -> (l k) q", q=P))
                vec(16, 16, ins["mem_norm_2"].rearrange("l (k q) -> (l k) q", q=P))
                vec(32, 2, ins["mla_q_norm"].rearrange("l (k q) -> (l k) q", q=P))
                vec(34, 1, ins["mla_kv_norm"])
                for at, name in ((35, "diff_subln_2"), (37, "gqa_q_norm_2"), (39, "gqa_k_norm_2")):
                    for j in range(2):
                        sp.dma_start(vec_rows[at:at + 2, HD * j:HD * j + HD], ins[name]).then_inc(vec_in, 16)
                sp.dma_start(sink, ins["sinks"][0].partition_broadcast(P)).then_inc(small_in, 16)
                sp.dma_start(route_b[0:GROUPS, :], ins["b_route_group"].rearrange("o g -> g o")).then_inc(small_in, 16)
                sp.dma_start(route_b[GROUPS:GROUPS + EXPERTS, :],
                               ins["b_route_expert"].rearrange("o g e -> (g e) o")).then_inc(small_in, 16)
                sp.dma_start(lam_p, ins["diff_lambda_2"].rearrange("l a d -> (l a d)").partition_broadcast(P)
                               ).then_inc(small_in, 16)

            sp.dma_start(x2, ins["x"][0].rearrange("(t p) d -> p t d", p=P)).then_inc(x_in, 16)
            sp.dma_start(const[:, :], ins["const_table"]).then_inc(const_in, 16)
            for n in range(FIRST_EXPERT):
                if n >= RING:
                    sp.wait_ge(p_ready, LAST_JOB[ITEMS[n - RING]] + 1)
                load(n)
                if n == 2:
                    small_loads()
                if n == 4:
                    sp.dma_start(mem_nat, ins["mem_2"][0].rearrange("(t p) d -> p t d", p=P)).then_inc(mem_in, 16)
                if n == RING - 1:
                    sp.wait_ge(p_dve, taken(JOB[("bias",)]))
                    sp.dma_start(bias_dram, bias_sb.unsqueeze(1).to_broadcast([BIAS_HEADS, P, VALS])
                                 ).then_inc(bias_out, 16)
                    sp.wait_ge(bias_out, 16)
                    shifted = bass.AP(tensor=bias_dram.tensor, offset=P - 1,
                                      ap=[[VALS - 1, P], [P * VALS, BIAS_HEADS], [1, T]])
                    sp.dma_start(bias3, shifted).then_inc(bias_in, 16)
            load_bunch(0, True)
            with sp.Fori(1, BUNCHES) as b:
                load_bunch(b, False)

            sp.wait_ge(routed, 1)
            some = sp.value_load(flags[0:1, 112:113], min_val=0, max_val=1)
            with sp.If(some):
                with sp.Fori(0, ROUNDS - 1) as r:
                    with sp.Fori(0, BUNCHES) as g:
                        flag = sp.value_load(flags[0:1, bass.ds(r * BUNCHES + g, 1)], min_val=0, max_val=1)
                        with sp.If(flag):
                            n = sp.value_load(flags[0:1, bass.ds(r * BUNCHES + g + 56, 1)], min_val=0, max_val=55)
                            sp.wait_ge(y_ready, n * 2 + 2 * BUNCHES)
                            for e in range(AT_ONCE):
                                if e:
                                    sp.wait_ge(more_used, n * 6 + e)
                                for dst, w in ((more_g, ins["w_expert_gate"]), (more_u, ins["w_expert_up"])):
                                    sp.dma_start(dst, w[0, bass.ds(g * AT_ONCE + e, 1)].rearrange(
                                        "o (p k) n -> p (o k n)", p=P)).then_inc(more_in, 16)
                            for e in range(AT_ONCE):
                                if e:
                                    sp.wait_ge(more_used, n * 6 + 3 + e)
                                sp.dma_start(more_d, ins["w_expert_down"][0, bass.ds(g * AT_ONCE + e, 1)].rearrange(
                                    "o (p k) n -> p (o k n)", p=P)).then_inc(more_down_in, 16)

            for n in range(FIRST2, len(ITEMS)):
                if n == FIRST2:
                    sp.wait_ge(gu_ready, BUNCHES)
                elif n >= FIRST2 + RING2:
                    sp.wait_ge(lows, last_split(n - RING2) + 1)
                load(n)
            out2 = out[0].rearrange("(t p) d -> p t d", p=P)
            for tt in range(2):
                sp.wait_ge(x_done, 2 * LAYERS - 1 + tt)
                sp.dma_start(out2[:, tt, :], x2[:, tt, :]).then_inc(stored, 16)
            sp.wait_ge(stored, 32)

        @block.gpsimd
        def _(pool):
            pool.wait_ge(p_ready, JOB[("mt", 3)] + 1)
            for n, name in enumerate(("ln1_g", "ln1_b")):
                pool.dma_start(ln_row[:, n, :], ins[name][0].partition_broadcast(P)).then_inc(ln1_in, 16)
            pool.wait_ge(ln_done, 2)
            for n, name in enumerate(("ln2_g", "ln2_b")):
                pool.dma_start(ln_row[:, n, :], ins[name][0].partition_broadcast(P)).then_inc(ln2_in, 16)
            for n in range(LAYERS):
                pool.dma_start(post_row[:, n, :], ins["post_norm_2"][n].partition_broadcast(P)
                               ).then_inc(post_in, 16)

        @block.tensor
        def _(pe):
            def arrived(name):
                if ITEM[name] < FIRST2:
                    pe.wait_ge(loaded[slot_of(ITEM[name])], all_loaded(ITEM[name]))

            def product(dst, left, right, first, last):
                pe.matmul(dst, left[0], right[0], start=first, stop=False)
                pe.matmul(dst, left[0], right[1], start=False, stop=False)
                return pe.matmul(dst, left[1], right[0], start=False, stop=last)

            def from_act(job):
                pe.wait_ge(p_act, taken(JOB[job]))

            def from_dve(job):
                pe.wait_ge(p_dve, taken(JOB[job]))

            def slot(name):
                return slots[:, ITEM[name] % RING]

            def flat(name, n):
                s = ITEM[name] % RING
                return ring[:, s * SLOT:s * SLOT + n]

            def project(dst, w, a, b):
                for k in range(KC):
                    mm = pe.matmul(dst, w[:, k, a:b], xT3[:, k, :], start=(k == 0), stop=(k == KC - 1))
                return mm

            def natural(dst, src, tt, w, a, b):
                for k in range(KC):
                    mm = pe.matmul(dst, src[:, k, P * tt:P * tt + P], w[:, k, a:b], start=(k == 0), stop=(k == KC - 1))
                return mm

            def turn4(dst, src4, k):
                for c in range(2):
                    for tt in range(2):
                        mm = pe.transpose(dst[:, c * T + tt * P:c * T + tt * P + P], src4[:, tt, 2 * k + c, :], ident)
                return mm

            def run(job, j):
                kind = job[0]
                dst = bank(6 + j % 2)
                if j >= 2:
                    if BY_DVE[j - 2]:
                        pe.wait_ge(p_dve, taken(j - 2))
                    else:
                        pe.wait_ge(p_act, taken(j - 2))
                for name in item_of(job):
                    arrived(name)
                if kind == "vec":
                    pe.wait_ge(const_in, 16)
                    pe.wait_ge(vec_in, 16 * 10)
                    mm = pe.transpose(dst[:, 0:41], vec_rows[0:41, :], ident[0:41, 0:41])
                elif kind == "xt":
                    pe.wait_ge(x_in, 16)
                    pe.wait_ge(const_in, 16)
                    mm = turn4(dst, x4, job[1])
                elif kind == "bias":
                    pe.wait_ge(table_in, 48)
                    pe.wait_ge(setup, 2)
                    mm = pe.matmul(dst[0:BIAS_HEADS, 0:VALS + 1], rel_sb, bucket_sb, start=True, stop=True)
                elif kind == "cnat":
                    from_act(("xt", 3))
                    tt = job[1]
                    natural(dst[:, 0:Q_LORA], xT3, tt, slot("c_q"), 0, 256)
                    mm = natural(dst[:, Q_LORA:C_COLS], xT3, tt, slot("c_kv"), 0, C_COLS - Q_LORA)
                elif kind == "tile1":
                    from_act(("xt", 3))
                    n = job[1]
                    w = slot(item_of(job)[0])
                    mm = project(dst[:, 0:T], w, P * (n % 2), P * (n % 2) + P)
                elif kind == "avn":
                    from_act(("tile1", 3))
                    for tt in range(2):
                        mm = pe.transpose(dst[:, P * tt:P * tt + P], tile3[:, 3, P * tt:P * tt + P], ident)
                elif kind == "ct":
                    pe.wait_ge(c_scaled, 1)
                    for c in range(2):
                        for tt in range(2):
                            mm = pe.transpose(dst[:, c * T + tt * P:c * T + tt * P + P],
                                              c_nat[:, tt, P * c:P * c + P], ident)
                elif kind == "ckt":
                    pe.wait_ge(kc_roped, 1)
                    for tt in range(2):
                        pe.transpose(dst[:, P * tt:P * tt + P], c_nat[:, tt, Q_LORA:Q_LORA + KV_LORA], ident)
                    for tt in range(2):
                        mm = pe.transpose(dst[0:C_ROPE, T + P * tt:T + P * tt + P],
                                          c_nat[:, tt, Q_LORA + KV_LORA:C_COLS], ident)
                elif kind == "cq":
                    from_act(("ct",))
                    tt, half = job[1:]
                    w = flat("w_uq", 1536).rearrange("p (k n) -> p k n", k=2)
                    for k in range(2):
                        mm = pe.matmul(dst[:, 0:384], c_qT[:, k, P * tt:P * tt + P],
                                       w[:, k, 384 * half:384 * half + 384], start=(k == 0), stop=(k == 1))
                elif kind == "ck":
                    from_act(("ckt",))
                    w = flat("w_ukv", 1024)
                    for m in range(2):
                        h = 2 * job[1] + m
                        mm = pe.matmul(dst[0:C_NOPE, T * m:T * m + T], w[:, P * h:P * h + C_NOPE], c_kvT,
                                       start=True, stop=True)
                elif kind == "cv":
                    from_act(("ckt",))
                    tt = job[1]
                    w = flat("w_ukv", 1024).rearrange("p (h n) -> p h n", h=C_HEADS)[:, :, C_NOPE:P]
                    mm = pe.matmul(dst, c_kvT[:, P * tt:P * tt + P], w, start=True, stop=True)
                elif kind == "cqt":
                    pe.wait_ge(qc_roped, 1)
                    for m in range(2):
                        h = 2 * job[1] + m
                        for tt in range(2):
                            mm = pe.transpose(dst[0:C_QK, T * m + P * tt:T * m + P * tt + P],
                                              qc_nat[:, tt, C_QK * h:C_QK * h + C_QK], ident)
                elif kind == "bv":
                    g, tt = job[1:]
                    mm = natural(dst[:, 0:256], xT3, tt, slot(f"b_v{g}"), 0, 256)
                elif kind == "y1":
                    pe.wait_ge(o_out, STEP[("B", 0, B_HEADS - 1)] + 1)
                    mm = natural(dst[:, 0:256], mix3, job[2], slot(item_of(job)[0]), 0, 256)
                elif kind == "mt":
                    pe.wait_ge(mem_scaled, 2)
                    mm = turn4(dst, mem4, job[1])
                elif kind == "mk":
                    l, n = job[1:]
                    from_act(("mt", 3))
                    w = slot(f"mem_k{l}")
                    for k in range(KC):
                        mm = pe.matmul(dst[:, 0:T], w[:, k, P * n:P * n + P], memT[l][:, k, :],
                                       start=(k == 0), stop=(k == KC - 1))
                elif kind == "mv":
                    l, tt = job[1:]
                    mm = natural(dst[:, 0:256], memT[l], tt, slot(f"mem_v{l}"), 0, 256)
                elif kind == "x1t":
                    pe.wait_ge(ln_done, 2)
                    mm = turn4(dst, x4, job[1])
                elif kind == "logit":
                    from_act(("x1t", 3))
                    w = slot("router")
                    for k in range(KC):
                        mm = pe.matmul(dst[0:GROUPS + EXPERTS, 0:T], w[:, k, 0:GROUPS + EXPERTS], xT3[:, k, :],
                                       start=(k == 0), stop=(k == KC - 1))
                elif kind == "logitT":
                    from_dve(("logit",))
                    n = GROUPS + EXPERTS
                    for tt in range(2):
                        mm = pe.transpose(dst[:, n * tt:n * tt + n], logitT_sb[0:n, P * tt:P * tt + P],
                                          ident[0:n, 0:n])
                elif kind == "rank":
                    pe.wait_ge(chosen_done, 1)
                    e = EXPERTS
                    pe.matmul(dst[:, 0:e], before, chosen3[:, 0, :], start=True, stop=True)
                    pe.matmul(dst[:, e:2 * e], before, chosen3[:, 1, :], start=True, stop=False)
                    pe.matmul(dst[:, e:2 * e], ones, chosen3[:, 0, :], start=False, stop=True)
                    pe.matmul(dst[:, 2 * e:3 * e], ones, chosen3[:, 0, :], start=True, stop=False)
                    mm = pe.matmul(dst[:, 2 * e:3 * e], ones, chosen3[:, 1, :], start=False, stop=True)
                elif kind == "xt2":
                    l, tt, half = job[1:]
                    pe.wait_ge(x_scaled, 2 * l + tt + 1)
                    for c in range(4):
                        mm = pe.transpose(dst[:, P * c:P * c + P], xn4[:, tt, 4 * half + c, :], ident)
                elif kind == "tile2":
                    l, n = job[1:]
                    pe.wait_ge(lows, SPLIT[job] + 1)
                    w = split_of(SPLIT[job])
                    for k in range(KC):
                        if k in (0, 4) and n == TILES_OF[l][0]:
                            pe.wait_ge(x_lows, 2 * l + 1 + k // 4)
                        mm = product(dst[:, 0:T], [a[:, k, :] for a in w], (a_high3[:, k, :], x_low3[:, k, :]),
                                     k == 0, k == KC - 1)
                elif kind == "vn":
                    l, n = job[1:]
                    from_act(("tile2", l, n))
                    for tt in range(2):
                        mm = pe.transpose(dst[:, P * tt:P * tt + P], tile3[:, n, P * tt:P * tt + P], ident)
                elif kind == "swap":
                    l, n = job[1:]
                    from_act(("tile2", l, n))
                    mm = pe.matmul(dst[:, 0:T], swap, tile3[:, n, :], start=True, stop=True)
                elif kind == "hsq":
                    pe.wait_ge(squared, hsq_nth(*job[1:]))
                    mm = pe.matmul(dst[:, 0:T], headsum, sq_tile(job[2]), start=True, stop=True)
                elif kind == "hso":
                    l, n = job[1:]
                    pe.wait_ge(o_squared, 3 * l + n + 1)
                    mm = pe.matmul(dst[:, 0:T], headsum, sq_tile(n), start=True, stop=True)
                elif kind == "y2":
                    l, s, tt = job[1:]
                    w = split_of(SPLIT[("y2", l, s)])
                    pe.wait_ge(lows, SPLIT[("y2", l, s)] + 1)
                    own = slice(P * tt, P * tt + P)
                    for k in range(KC):
                        if k in (0, KC - 2):
                            pe.wait_ge(mix_lows, 2 * l + (1 if k == 0 else 2))
                        mm = product(dst[:, 0:256], (a_high3[:, k, own], mix_low3[:, k, own]), [a[:, k, :] for a in w],
                                     k == 0, k == KC - 1)
                mm.then_inc(p_ready, 1)

            def s_bank(n):
                if n >= 3:
                    owner = S_OWNER[n - 3]
                    if STEPS[owner][0] in "AB":
                        pe.wait_ge(maxed, owner + 1)
                    else:
                        pe.wait_ge(exped, owner + 1)
                return bank(n % 3)

            def run_scores(step):
                kind, l, h = STEPS[step]
                n = s_first(step)
                if kind == "A":
                    for tile in (h % 2, 2):
                        from_act(("tile1", tile))
                    base = HD * (h // 2)
                    q, k = tile3[base:base + HD, h % 2, :], tile3[base:base + HD, 2, :]
                    s = s_bank(n)
                    pe.matmul(s[:, 0:P], q[:, 0:P], k[:, 0:P], start=True, stop=True)
                    pe.matmul(s[:, P:3 * P], q[:, P:T], k[:, 0:T], start=True, stop=True).then_inc(scores, 1)
                elif kind == "C":
                    from_act(("cqt", 3))
                    pe.wait_ge(setup, 2)
                    q, k = qc3[0:C_QK, h, :], kc3[0:C_QK, h, :]
                    s = s_bank(n)
                    pe.matmul(s[:, 0:P], q[:, 0:P], k[:, 0:P], start=True, stop=False)
                    pe.matmul(s[:, 0:P], ident_b[:, :], causal_b[:, :], start=False, stop=True)
                    pe.matmul(s[:, P:3 * P], q[:, P:T], k[:, 0:T], start=True, stop=False)
                    pe.matmul(s[:, 2 * P:3 * P], ident_b[:, :], causal_b[:, :], start=False, stop=True
                              ).then_inc(scores, 1)
                elif kind == "B":
                    for g in range(B_GROUPS):
                        from_act(("tile1", 10 + 2 * g + 1))
                    base = HD * (h % 2)

                    def qk(g):
                        return (tile3[base:base + HD, 4 + 2 * g + h // 2, :],
                                tile3[base:base + HD, 10 + 2 * g + h // 2, :])

                    s = s_bank(n)
                    for g in range(B_GROUPS):
                        q, k = qk(g)
                        mm = pe.matmul(s[:, P * g:P * g + P], q[:, 0:P], k[:, 0:P], start=True, stop=True)
                    mm.then_inc(scores, 1)
                    s = s_bank(n + 1)
                    for g in range(2):
                        q, k = qk(g)
                        mm = pe.matmul(s[:, T * g:T * g + T], q[:, P:T], k[:, 0:T], start=True, stop=True)
                    mm.then_inc(scores, 1)
                    s = s_bank(n + 2)
                    q, k = qk(2)
                    pe.matmul(s[:, 0:T], q[:, P:T], k[:, 0:T], start=True, stop=True).then_inc(scores, 1)
                elif kind == "D":
                    pe.wait_ge(roped, max(rope_nth(l, h // 2), rope_nth(l, 3 + h // 2)))
                    banks = [s_bank(n), s_bank(n + 1)]
                    for tt in range(2):
                        for m in range(2):
                            base = HD * (h % 2) + 32 * m
                            q, k = tile3[base:base + 32, h // 2, :], tile3[base:base + 32, 3 + h // 2, :]
                            mm = pe.matmul(banks[m][:, T * tt:T * tt + T], q[:, P * tt:P * tt + P], k,
                                           start=True, stop=True)
                            if tt == 1:
                                mm.then_inc(scores, 1)
                else:
                    base = HD * (h % 2)
                    if kind == "G":
                        pe.wait_ge(k_copied, l + 1)
                        q = tile3[base:base + HD, 12 + h // 2, :]
                        same = base == HD * (h // 3)
                        k = tile3[base:base + HD, 15 if same else 16, :]
                    else:
                        from_act(("tile2", l, 20 + h // 2))
                        q = tile3[base:base + HD, 20 + h // 2, :]
                        k = mem_k[base:base + HD, l, h // 2, :]
                    s = s_bank(n)
                    for tt in range(2):
                        mm = pe.matmul(s[:, T * tt:T * tt + T], q[:, P * tt:P * tt + P], k, start=True, stop=True)
                    mm.then_inc(scores, 1)

            def run_turn(step):
                kind, l, h = STEPS[step]
                pe.wait_ge(normed, step + 1)
                pr = probs[:, 1152 * (step % 2):1152 * (step % 2) + 1152]
                for m in range(T_JOBS[kind]):
                    n = t_first(step) + m
                    if n >= 2:
                        pe.wait_ge(turned_out, n - 1)
                    dst = bank(3 + n % 2)
                    if kind in "AC":
                        at = [0, P, 2 * P]
                    elif kind == "B":
                        at = [P * m, 3 * P + T * m, 3 * P + T * m + P]
                    else:
                        at = [0, T, P, T + P]
                    for c, a in enumerate(at):
                        mm = pe.transpose(dst[:, P * c:P * c + P], pr[:, a:a + P], ident)
                    mm.then_inc(turned, 1)

            def run_out(step):
                kind, l, h = STEPS[step]
                par = h % 2
                if step >= 2:
                    pe.wait_ge(o_out, step - 1)
                o = bank(5)[HD * par:HD * par + HD, T * (step % 2):T * (step % 2) + T]
                if kind == "B":
                    from_act(("bv", B_GROUPS - 1, 1))
                elif kind == "A":
                    from_act(("avn",))
                elif kind == "C":
                    from_act(("cv", 1))
                elif kind == "D":
                    from_act(("vn", l, 6 + h // 2))
                elif kind == "G":
                    from_act(("vn", l, 16))
                for m in range(T_JOBS[kind]):
                    n = t_first(step) + m
                    pe.wait_ge(turned_out, n + 1)
                    pt = probsT[:, 512 * (n % 4):512 * (n % 4) + 512]
                    if kind == "A":
                        v = [va[:, tt, HD * (h // 2):HD * (h // 2) + HD] for tt in range(2)]
                    elif kind == "B":
                        v = [vb[:, tt, m, HD * h:HD * h + HD] for tt in range(2)]
                    elif kind == "C":
                        v = [vc3[:, tt, HD * h:HD * h + HD] for tt in range(2)]
                    elif kind == "D":
                        v = [v2[:, tt, h // 2, HD * par:HD * par + HD] for tt in range(2)]
                    elif kind == "G":
                        v = [v2[:, tt, 3, HD * (h // 3):HD * (h // 3) + HD] for tt in range(2)]
                    else:
                        v = [mem_v[:, l, tt, HD * h:HD * h + HD] for tt in range(2)]
                    last = m == T_JOBS[kind] - 1
                    pe.matmul(o, v[0], pt[:, 0:T], start=(m == 0), stop=False)
                    if kind in "ABC":
                        mm = pe.matmul(o[:, P:T], v[1], pt[:, T:T + P], start=False, stop=last)
                    else:
                        mm = pe.matmul(o, v[1], pt[:, T:2 * T], start=False, stop=last)
                mm.then_inc(o_ready, 1)

            def bunch(i, more, n):
                pe.wait_ge(placed, i + 1)
                for half in range(2):
                    dst = bank(4 + half)
                    for c in range(4):
                        k = 4 * half + c
                        for tt in range(2):
                            mm = pe.matmul(dst[:, P * c:P * c + P],
                                           x2[:, tt, :].rearrange("p (q k) -> p k q", k=KC)[:, k, :],
                                           places2[:, tt, :], start=(tt == 0), stop=(tt == 1))
                    mm.then_inc(gathered_ready, 1)
                for tt in range(2):
                    mm = pe.transpose(bank(7)[:, P * tt:P * tt + P], weighed2[:, tt, :], ident)
                mm.then_inc(back_ready, 1)
                pe.wait_ge(gathered_out, 2 * i + 2)
                if not more:
                    for k in range(2 * AT_ONCE):
                        pe.wait_ge(loaded[k], loaded_at(k, i))
                    for k in range(KC):
                        for e in range(AT_ONCE):
                            w = slots[:, 2 * e:2 * e + 2, k, :]
                            mm = pe.matmul(bank(6)[PLACES * e:PLACES * e + PLACES, :],
                                           gathered[:, k, PLACES * e:PLACES * e + PLACES], w,
                                           start=(k == 0), stop=(k == KC - 1))
                else:
                    for e in range(AT_ONCE):
                        pe.wait_ge(more_in, n * (32 * AT_ONCE) + 32 * (e + 1))
                        for m, w in enumerate((more_g, more_u)):
                            for k in range(KC):
                                mm = pe.matmul(bank(6)[PLACES * e:PLACES * e + PLACES, DE * m:DE * m + DE],
                                               gathered[:, k, PLACES * e:PLACES * e + PLACES],
                                               w[:, DE * k:DE * k + DE], start=(k == 0), stop=(k == KC - 1))
                        if e < AT_ONCE - 1:
                            mm.then_inc(more_used, 1)
                mm.then_inc(gu_ready, 1)
                pe.wait_ge(hidden_done, i + 1)
                for k in range(2):
                    mm = pe.transpose(bank(4)[:, P * k:P * k + P],
                                      hidden.rearrange("p (q k) -> p k q", k=2)[:, k, :], ident)
                mm.then_inc(hT_ready, 1)
                pe.wait_ge(hT_out, i + 1)
                pe.wait_ge(back_out, i + 1)
                if not more:
                    for k in range(AT_ONCE):
                        pe.wait_ge(loaded[2 * AT_ONCE + k], loaded_at(2 * AT_ONCE + k, i))
                    for half in range(2):
                        for k in range(2):
                            for e in range(AT_ONCE):
                                a = (2 * AT_ONCE + e) * SLOT + D * k + 512 * half
                                mm = pe.matmul(bank((7, 5)[half])[PLACES * e:PLACES * e + PLACES, :],
                                               hiddenT[:, k, PLACES * e:PLACES * e + PLACES], ring[:, a:a + 512],
                                               start=(k == 0), stop=(k == 1))
                        mm.then_inc(y_ready, 1)
                else:
                    for e in range(AT_ONCE):
                        pe.wait_ge(more_down_in, n * (16 * AT_ONCE) + 16 * (e + 1))
                        for half in range(2):
                            for k in range(2):
                                a = D * k + 512 * half
                                mm = pe.matmul(bank((7, 5)[half])[PLACES * e:PLACES * e + PLACES, :],
                                               hiddenT[:, k, PLACES * e:PLACES * e + PLACES], more_d[:, a:a + 512],
                                               start=(k == 0), stop=(k == 1))
                            if e == AT_ONCE - 1:
                                mm.then_inc(y_ready, 1)
                        if e < AT_ONCE - 1:
                            mm.then_inc(more_used, 1)
                pe.wait_ge(y0_out, i + 1)
                pe.wait_ge(y1_out, i + 1)
                for tt in range(2):
                    for half in range(2):
                        mm = pe.matmul(bank(2 * tt + half), back[:, P * tt:P * tt + P],
                                       y_e[:, 512 * half:512 * half + 512], start=False, stop=False,
                                       skip_group_check=True)
                mm.then_inc(summed, 1)

            def loaded_at(k, i):
                return all_loaded(FIRST_EXPERT + k) + i * 16

            def experts():
                pe.wait_ge(p_act, taken(JOB[("mv", 1, 1)]))
                pe.wait_ge(p_dve, taken(JOB[("rank",)]))
                pe.wait_ge(setup, 2)
                for b in range(4):
                    pe.matmul(bank(b), zeros_b[:, 0:P], zeros_b[:, :], start=True, stop=False, skip_group_check=True)
                bunch(0, False, None)
                with pe.Fori(1, BUNCHES) as i:
                    bunch(i, False, None)
                pe.wait_ge(routed, 1)
                some = pe.value_load(flags[0:1, 112:113], min_val=0, max_val=1)
                with pe.If(some):
                    with pe.Fori(0, ROUNDS - 1) as r:
                        with pe.Fori(0, BUNCHES) as g:
                            flag = pe.value_load(flags[0:1, bass.ds(r * BUNCHES + g, 1)], min_val=0, max_val=1)
                            with pe.If(flag):
                                n = pe.value_load(flags[0:1, bass.ds(r * BUNCHES + g + 56, 1)], min_val=0, max_val=55)
                                bunch(n + BUNCHES, True, n)
                for b in range(4):
                    mm = pe.matmul(bank(b), zeros_b[:, 0:P], zeros_b[:, :], start=False, stop=True, skip_group_check=True)
                    if b % 2 == 1:
                        mm.then_inc(moe_done, 1)

            j = step = drained = 0
            for jobs, what in TURNS:
                if what in STEP:
                    step = STEP[what]
                    run_scores(step)
                    if not opens(step) and not opens(step - 1):
                        run_out(step - 2)
                    drained = 0
                for job in jobs:
                    run(job, j)
                    j += 1
                if what == "experts":
                    experts()
                elif what is not None:
                    if not opens(step):
                        run_turn(step - 1)
                elif jobs == []:
                    if drained == 0:
                        run_out(step - 1)
                        run_turn(step)
                    else:
                        run_out(step)
                    drained += 1

        @block.scalar
        def _(act):
            chain = [0]

            def link(ins_):
                chain[0] += 1
                ins_.then_inc(act_chain, 1)
                act.wait_ge(act_chain, chain[0])

            act.preload_act_table_set("natural_log_exp_and_others")
            act.dma_start(bucket_sb[:, 0:VALS], ins["const_bucket"]).then_inc(table_in, 16)
            act.dma_start(rel_sb, ins["rel_bias"]).then_inc(table_in, 16)
            act.dma_start(unseen_sb, ins["const_unseen"]).then_inc(table_in, 16)

            def take(job, j):
                kind = job[0]
                src = bank(6 + j % 2)
                act.wait_ge(p_ready, j + 1)
                if kind == "vec":
                    op = act.activation(vecs[:, :], src[:, 0:41], ACT.Copy)
                elif kind in ("xt", "x1t"):
                    k = job[1]
                    op = act.activation(xT3[:, 2 * k:2 * k + 2, :], src.rearrange("p (c t) -> p c t", c=2), ACT.Copy)
                elif kind == "cnat":
                    op = act.activation(c_nat[:, job[1], :], src[:, 0:C_COLS], ACT.Copy)
                elif kind == "tile1":
                    n = job[1]
                    q = n < 2 or 4 <= n < 10
                    op = act.activation(tile3[:, n, :], src[:, 0:T], ACT.Copy, scale=(HD ** -0.5 if q else 1.0))
                elif kind == "avn":
                    op = act.activation(va, src[:, 0:256].rearrange("p (t n) -> p t n", t=2), ACT.Copy)
                elif kind == "ct":
                    for c in range(2):
                        op = act.activation(c_qT[:, c, :], src[:, T * c:T * c + T], ACT.Copy,
                                            scale=vecs[:, 32 + c:33 + c])
                elif kind == "ckt":
                    act.activation(c_kvT, src[:, 0:T], ACT.Copy, scale=vecs[:, 34:35])
                    op = act.activation(kc3[C_NOPE:C_QK, :, :],
                                        src[0:C_ROPE, T:2 * T].unsqueeze(1).to_broadcast([C_ROPE, C_HEADS, T]),
                                        ACT.Copy)
                elif kind == "cq":
                    tt, half = job[1:]
                    op = act.activation(qc_nat[:, tt, 384 * half:384 * half + 384], src[:, 0:384], ACT.Copy)
                elif kind == "ck":
                    k = job[1]
                    op = act.activation(kc3[0:C_NOPE, 2 * k:2 * k + 2, :],
                                        src[0:C_NOPE, :].rearrange("p (c t) -> p c t", c=2), ACT.Copy)
                elif kind == "cv":
                    op = act.activation(vc3[:, job[1], :], src, ACT.Copy)
                elif kind == "cqt":
                    k = job[1]
                    op = act.activation(qc3[0:C_QK, 2 * k:2 * k + 2, :],
                                        src[0:C_QK, :].rearrange("p (c t) -> p c t", c=2), ACT.Copy)
                elif kind == "bv":
                    g, tt = job[1:]
                    op = act.activation(vb[:, tt, g, :], src[:, 0:256], ACT.Copy)
                elif kind == "mt":
                    k = job[1]
                    for l in range(LAYERS):
                        for c in range(2):
                            at = 16 + 8 * l + 2 * k + c
                            op = act.activation(memT[l][:, 2 * k + c, :], src[:, T * c:T * c + T], ACT.Copy,
                                                scale=vecs[:, at:at + 1])
                elif kind == "mk":
                    l, n = job[1:]
                    op = act.activation(mem_k[:, l, n, :], src[:, 0:T], ACT.Copy)
                elif kind == "mv":
                    l, tt = job[1:]
                    op = act.activation(mem_v[:, l, tt, :], src[:, 0:256], ACT.Copy)
                elif kind == "tile2":
                    l, n = job[1:]
                    if 12 <= n <= 15:
                        act.activation(sq_tile(n), src[:, 0:T], ACT.Square).then_inc(squared, 1)
                        at = (37 if n < 15 else 39) + l
                        op = act.activation(tile3[:, n, :], src[:, 0:T], ACT.Copy, scale=vecs[:, at:at + 1])
                    elif n in GATE_TILES:
                        act.activation(exp_tile(n), src[:, 0:T], ACT.Exp, scale=-1.0)
                        op = act.activation(tile3[:, n, :], src[:, 0:T], ACT.Copy)
                    else:
                        op = act.activation(tile3[:, n, :], src[:, 0:T], ACT.Copy)
                elif kind == "vn":
                    l, n = job[1:]
                    op = act.activation(v2[:, :, V_TILES.index(n), :], src[:, 0:256].rearrange("p (t n) -> p t n", t=2),
                                        ACT.Copy)
                elif kind in ("hsq", "hso"):
                    dst = sq_tile(job[2])
                    link(act.activation(dst, src[:, 0:T], ACT.Ln, scale=1.0 / HD, bias=eps6))
                    op = act.activation(dst, dst, ACT.Exp, scale=-0.5)
                elif kind == "y2":
                    l, s, tt = job[1:]
                    act.activation(xn2[:, tt, 256 * s:256 * s + 256], src[:, 0:256], ACT.Square,
                                   accum_out=y_sq[:, 4 * tt + s:4 * tt + s + 1])
                    op = act.activation(y_nat[:, tt, 256 * s:256 * s + 256], src[:, 0:256], ACT.Copy)
                op.then_inc(p_act, 1)

            def gate_sigmoid(l, n):
                e = exp_tile(n)
                act.wait_ge(p_act, taken(JOB[("tile2", l, n)]))
                link(act.activation(e, e, ACT.Ln, bias=1.0))
                act.activation(e, e, ACT.Exp, scale=-1.0).then_inc(sigmoid, 1)

            def exps(step):
                kind, l, h = STEPS[step]
                act.wait_ge(maxed, step + 1)
                pr = probs[:, 1152 * (step % 2):1152 * (step % 2) + 1152]
                par = step % 2
                n_, s_ = nm[:, 4 * par:4 * par + 4], sm[:, 4 * par:4 * par + 4]
                if step >= 2:
                    act.wait_ge(turned, t_first(step - 1))
                b0 = s_first(step)
                if kind == "A":
                    act.activation(sink_e[:, 2 * par:2 * par + 2], n_[:, 0:2], ACT.Exp, bias=sink[:, h:h + 1])
                    act.activation(pr[:, 0:P], pr[:, 0:P], ACT.Exp, bias=n_[:, 0:1], accum_out=s_[:, 0:1])
                    op = act.activation(pr[:, P:3 * P], pr[:, P:3 * P], ACT.Exp, bias=n_[:, 1:2],
                                        accum_out=s_[:, 1:2])
                elif kind == "B":
                    act.activation(pr[:, 0:384], pr[:, 0:384], ACT.Exp, bias=n_[:, 0:1], accum_out=s_[:, 0:1])
                    op = act.activation(pr[:, 384:1152], pr[:, 384:1152], ACT.Exp, bias=n_[:, 1:2],
                                        accum_out=s_[:, 1:2])
                elif kind == "C":
                    s = bank(b0 % 3)
                    sc = C_QK ** -0.5
                    act.activation(pr[:, 0:P], s[:, 0:P], ACT.Exp, bias=n_[:, 0:1], scale=sc, accum_out=s_[:, 0:1])
                    op = act.activation(pr[:, P:3 * P], s[:, P:3 * P], ACT.Exp, bias=n_[:, 1:2], scale=sc,
                                        accum_out=s_[:, 1:2])
                elif kind == "D":
                    for m in range(2):
                        for tt in range(2):
                            c = 2 * m + tt
                            op = act.activation(pr[:, T * c:T * c + T], bank((b0 + m) % 3)[:, T * tt:T * tt + T],
                                                ACT.Exp, bias=n_[:, c:c + 1], scale=32 ** -0.5,
                                                accum_out=s_[:, c:c + 1])
                else:
                    s = bank(b0 % 3)
                    for tt in range(2):
                        op = act.activation(pr[:, T * tt:T * tt + T], s[:, T * tt:T * tt + T], ACT.Exp,
                                            bias=n_[:, tt:tt + 1], scale=HD ** -0.5, accum_out=s_[:, tt:tt + 1])
                op.then_inc(exped, 1)

            def take_turned(step):
                kind = STEPS[step][0]
                w = 3 * P if kind in "ABC" else 4 * P
                for m in range(T_JOBS[kind]):
                    n = t_first(step) + m
                    if n >= 4:
                        owner = max(s for s in range(len(STEPS)) if t_first(s) <= n - 4)
                        act.wait_ge(o_ready, owner + 1)
                    act.wait_ge(turned, n + 1)
                    act.activation(probsT[:, 512 * (n % 4):512 * (n % 4) + w], bank(3 + n % 2)[:, 0:w], ACT.Copy
                                   ).then_inc(turned_out, 1)

            def inverse_root(dst, src, scale=1.0, bias=0.0):
                link(act.activation(dst, src, ACT.Ln, scale=scale, bias=bias))
                return act.activation(dst, dst, ACT.Exp, scale=-0.5)

            def layer_stats(n, tt):
                act.wait_ge(ln_var, 2 * n + tt + 1)
                inverse_root(ln_rs[:, tt:tt + 1], mv3[:, tt, 1:2], bias=eps5).then_inc(ln_rstd, 1)

            def start_layer(l, tt):
                if l == 0:
                    act.wait_ge(ln_done, 2 + tt + 1)
                else:
                    act.wait_ge(x_done, 2 * (l - 1) + tt + 1)
                link(act.activation(xn2[:, tt, :], x2[:, tt, :], ACT.Square, accum_out=x_sq[:, tt:tt + 1]))
                link(inverse_root(x_rs[:, tt:tt + 1], x_sq[:, tt:tt + 1], 1.0 / D, eps6))
                act.activation(xn2[:, tt, :], x2[:, tt, :], ACT.Copy, scale=x_rs[:, tt:tt + 1]).then_inc(x_scaled, 1)

            def high(n):
                kind, l, m = SPLITS[n]
                item = ITEM[f"in{l}_{m // 2}" if kind == "tile2" else f"out{l}_{m}"]
                act.wait_ge(loaded[slot_of(item)], all_loaded(item))
                if freed_by(n) >= 0:
                    act.wait_ge(p_ready, freed_by(n) + 1)
                act.activation(split_of(n)[0], raw_of(n), ACT.Copy).then_inc(highs, 1)

            def x_high(l, half):
                act.wait_ge(p_dve, taken(JOB[("xt2", l, 1, half)]))
                own = slice(4 * half, 4 * half + 4)
                act.activation(a_high3[:, own, :], xT3[:, own, :], ACT.Copy).then_inc(x_highs, 1)

            def mix_high(l, part):
                if part == 0:
                    act.wait_ge(p_ready, JOB[("tile2", l, TILES_OF[l][-1])] + 1)
                    act.wait_ge(gated, D_HEADS // 2 * (l + 1))
                act.wait_ge(o_out, STEP[("G", l, G_HEADS - 1) if part == 0 else ("M", l, M_HEADS - 1)] + 1)
                own = slice(0, KC - 2) if part == 0 else slice(KC - 2, KC)
                act.activation(a_high3[:, own, :], mix3[:, own, :], ACT.Copy).then_inc(mix_highs, 1)

            def memory():
                act.wait_ge(mem_sum, 1)
                link(inverse_root(mem_rs, mem_sq))
                for tt in range(2):
                    act.activation(mem_nat[:, tt, :], mem_nat[:, tt, :], ACT.Copy, scale=mem_rs[:, tt:tt + 1]
                                   ).then_inc(mem_scaled, 1)

            def bunch(i):
                for half in range(2):
                    act.wait_ge(gathered_ready, 2 * i + half + 1)
                    act.activation(gathered[:, 4 * half:4 * half + 4, :],
                                   bank(4 + half).rearrange("p (k s) -> p k s", k=4), ACT.Copy
                                   ).then_inc(gathered_out, 1)
                act.wait_ge(gu_ready, i + 1)
                act.activation(gate_e, bank(6)[:, 0:DE], ACT.Exp, scale=-1.0).then_inc(gate_exped, 1)
                act.wait_ge(hT_ready, i + 1)
                act.activation(hiddenT, bank(4)[:, 0:256].rearrange("p (k s) -> p k s", k=2), ACT.Copy
                               ).then_inc(hT_out, 1)
                act.wait_ge(y_ready, 2 * i + 1)
                if not isinstance(i, int):
                    act.wait_ge(summed, i)
                act.activation(y_e[:, 0:512], bank(7), ACT.Copy).then_inc(y0_out, 1)

            def experts():
                bunch(0)
                with act.Fori(1, BUNCHES) as i:
                    bunch(i)
                act.wait_ge(routed, 1)
                some = act.value_load(flags[0:1, 112:113], min_val=0, max_val=1)
                with act.If(some):
                    with act.Fori(0, ROUNDS - 1) as r:
                        with act.Fori(0, BUNCHES) as g:
                            flag = act.value_load(flags[0:1, bass.ds(r * BUNCHES + g, 1)], min_val=0, max_val=1)
                            with act.If(flag):
                                n = act.value_load(flags[0:1, bass.ds(r * BUNCHES + g + 56, 1)], min_val=0, max_val=55)
                                bunch(n + BUNCHES)
                for n in FIRST_SPLITS:
                    high(n)
                for tt in range(2):
                    layer_stats(1, tt)

            j = step = drained = 0
            gates_due = []
            for jobs, what in TURNS:
                if what in STEP:
                    step = STEP[what]
                    exps(step)
                    if what == ("C", 0, 0):
                        memory()
                    drained = 0
                for job in jobs:
                    for n in SPLIT_AT.get(j, ()):
                        high(n)
                    if job[0] == "xt2" and job[3] == 0 and job[1:3] != (1, 0):
                        start_layer(*job[1:3])
                    if job[0] == "xt2" and job[2] == 1:
                        x_high(job[1], job[3])
                    if not BY_DVE[j]:
                        take(job, j)
                        if job == ("tile1", 0):
                            act.wait_ge(c_sums, 1)
                            inverse_root(c_rs, c_sq).then_inc(c_rstd, 1)
                        if job[0] == "y2" and job[2] == 3:
                            l, tt = job[1], job[3]
                            act.wait_ge(y_sum, 2 * l + tt + 1)
                            inverse_root(y_rs[:, tt:tt + 1], y_ms[:, tt:tt + 1], 1.0 / D, eps6).then_inc(y_rstd, 1)
                        if job == ("y2", 0, 2, 1):
                            start_layer(1, 0)
                        if job[0] == "tile2" and job[2] == 9 and job[1] == 0:
                            act.wait_ge(lam_sum, 1)
                            act.activation(lam_e, lam_s, ACT.Exp).then_inc(lam_exp, 1)
                    elif job[:2] == ("y1", 3):
                        layer_stats(0, job[2])
                    elif job[0] == "logitT":
                        act.wait_ge(route_dif, 1)
                        act.activation(g_exp, g_dif, ACT.Exp).then_inc(route_exp, 1)
                        act.wait_ge(route_m, 1)
                        act.activation(e_x, e_t, ACT.Exp).then_inc(route_x, 1)
                    if job[0] == "tile2" and job[2] in GATE_TILES:
                        gates_due.append(job[1:])
                    j += 1
                if what == "experts":
                    experts()
                elif what is not None:
                    if not opens(step):
                        take_turned(step - 1)
                    for due in gates_due:
                        gate_sigmoid(*due)
                    gates_due = []
                    if what[0] in "DG" and STEP[what] - STEP[("D", what[1], 0)] in (4, 6, 8):
                        n = (STEP[what] - STEP[("D", what[1], 0)]) // 2 - 2
                        act.wait_ge(o_out, step - 2)
                        act.activation(sq_tile(n), mix3[:, n, :], ACT.Square).then_inc(o_squared, 1)
                elif jobs == []:
                    if drained == 0:
                        if STEPS[step][0] == "M":
                            mix_high(STEPS[step][1], 0)
                        take_turned(step)
                    elif STEPS[step][0] == "M":
                        mix_high(STEPS[step][1], 1)
                    drained += 1

        @block.vector
        def _(dve):
            chain = [0]

            def link(ins_):
                chain[0] += 1
                ins_.then_inc(dve_chain, 1)
                dve.wait_ge(dve_chain, chain[0])

            def rope4(dst1, dst2, cos, sin, t, last=None):
                t1, t2, t3, t4 = t
                dve.tensor_tensor(t1, dst1, cos, ALU.mult)
                dve.tensor_tensor(t2, dst2, sin, ALU.mult)
                dve.tensor_tensor(t3, dst1, sin, ALU.mult)
                link(dve.tensor_tensor(t4, dst2, cos, ALU.mult))
                link(dve.tensor_tensor(dst1, t1, t2, ALU.subtract))
                return dve.tensor_tensor(dst2, t3, t4, ALU.add)

            dve.memset(eps6, 1e-6)
            dve.memset(eps5, 1e-5)
            dve.memset(bucket_sb[:, VALS:VALS + 1], 0.0)
            dve.memset(zeros_b[:, :], 0.0).then_inc(setup, 1)
            dve.wait_ge(const_in, 16)
            dve.tensor_copy(ident_b[:, :], ident)
            dve.tensor_copy(causal_b[:, :], c_("causal")).then_inc(setup, 1)
            def rms(dst, src, n, junk, eps):
                link(dve.tensor_tensor_reduce(out=junk, in0=src, in1=src, scale=1.0, scalar=0.0,
                                              op0=ALU.mult, op1=ALU.add, accum_out=dst))
                return dve.tensor_scalar(dst, dst, 1.0 / n, eps, ALU.mult, ALU.add)

            def lambda_sums():
                dve.wait_ge(small_in, 64)
                lp = lam_p.rearrange("p (l a b d) -> p l a b d", l=2, a=2, b=2)
                for l in range(LAYERS):
                    link(dve.tensor_tensor(lp[:, l, :, 0, :], lp[:, l, :, 0, :], lp[:, l, :, 1, :], ALU.mult))
                for l in range(LAYERS):
                    op = dve.tensor_reduce(lam_s[:, 2 * l:2 * l + 2], lp[:, l, :, 0, :], X, ALU.add)
                op.then_inc(lam_sum, 1)

            def latent_norm():
                dve.wait_ge(p_act, taken(JOB[("cnat", 1)]))
                for tt in range(2):
                    link(rms(c_sq[:, tt:tt + 1], c_nat[:, tt, 0:Q_LORA], Q_LORA, rope_t[:, 0:Q_LORA], 1e-6))
                    op = rms(c_sq[:, 2 + tt:3 + tt], c_nat[:, tt, Q_LORA:Q_LORA + KV_LORA], KV_LORA,
                             rope_t[:, 256:256 + KV_LORA], 1e-6)
                    if tt == 0:
                        link(op)
                op.then_inc(c_sums, 1)
                dve.wait_ge(c_rstd, 1)
                for tt in range(2):
                    op = dve.tensor_scalar(c_nat[:, tt, 0:Q_LORA], c_nat[:, tt, 0:Q_LORA], c_rs[:, tt:tt + 1], None,
                                           ALU.mult)
                op.then_inc(c_scaled, 1)
                for tt in range(2):
                    op = dve.tensor_scalar(c_nat[:, tt, Q_LORA:Q_LORA + KV_LORA],
                                           c_nat[:, tt, Q_LORA:Q_LORA + KV_LORA], c_rs[:, 2 + tt:3 + tt], None,
                                           ALU.mult)
                link(op)
                a = Q_LORA + KV_LORA
                t = [rope_t[:, 32 * m:32 * m + 32].rearrange("p (t n) -> p t n", t=2) for m in range(4)]
                rope4(c_nat[:, :, a:a + HALF], c_nat[:, :, a + HALF:a + 2 * HALF],
                      c_("cos_c").rearrange("p (t n) -> p t n", t=2), c_("sin_c").rearrange("p (t n) -> p t n", t=2),
                      t).then_inc(kc_roped, 1)

            def latent_rope():
                dve.wait_ge(p_act, taken(JOB[("cq", 1, 1)]))
                for tt in range(2):
                    q = qc_nat[:, tt, :].rearrange("p (h n) -> p h n", h=C_HEADS)
                    a, b = (c_(n)[:, HALF * tt:HALF * tt + HALF].unsqueeze(1).to_broadcast([P, C_HEADS, HALF])
                            for n in ("cos_c", "sin_c"))
                    t = [rope_s[:, P * m:P * m + P].rearrange("p (h n) -> p h n", h=C_HEADS) for m in range(4)]
                    op = rope4(q[:, :, C_NOPE:C_NOPE + HALF], q[:, :, C_NOPE + HALF:C_QK], a, b, t)
                    if tt == 0:
                        link(op)
                op.then_inc(qc_roped, 1)

            def take(job, j):
                kind = job[0]
                src = bank(6 + j % 2)
                dve.wait_ge(p_ready, j + 1)
                if kind == "bias":
                    dve.wait_ge(table_in, 48)
                    dve.tensor_tensor(bias_sb, src[0:BIAS_HEADS, 0:VALS], unseen_sb, ALU.add).then_inc(p_dve, 1)
                elif kind == "y1":
                    s, tt = job[1:]
                    xs = x2[:, tt, 256 * s:256 * s + 256]
                    dve.scalar_tensor_tensor(xs, xs, ALPHA, src[:, 0:256], ALU.mult, ALU.add).then_inc(p_dve, 1)
                elif kind == "logit":
                    n = GROUPS + EXPERTS
                    dve.tensor_scalar(logitT_sb[0:n, :], src[0:n, 0:T], route_b[0:n, :], None, ALU.add
                                      ).then_inc(p_dve, 1)
                elif kind == "logitT":
                    dve.tensor_copy(lg, src[:, 0:72].rearrange("p (t n) -> p t n", t=2)).then_inc(p_dve, 1)
                elif kind == "xt2":
                    l, tt, half = job[1:]
                    g = vecs[:, 8 * l + 4 * half:8 * l + 4 * half + 4].unsqueeze(2).to_broadcast([P, 4, P])
                    dve.tensor_tensor(xT3[:, 4 * half:4 * half + 4, P * tt:P * tt + P],
                                      src.rearrange("p (c t) -> p c t", c=4), g, ALU.mult).then_inc(p_dve, 1)
                elif kind == "rank":
                    e = EXPERTS
                    link(dve.tensor_tensor(rank, src[:, 0:2 * e], chosen, ALU.mult))
                    link(dve.tensor_scalar(e_sc, chosen, -ABSENT, ABSENT, ALU.mult, ALU.add))
                    link(dve.tensor_tensor(rank, rank, e_sc, ALU.add))
                    dve.tensor_reduce(cnt_b, src[:, 2 * e:3 * e].rearrange("p (b e) -> p b e", b=BUNCHES), X, ALU.max
                                      ).then_inc(p_dve, 1)
                elif kind == "swap":
                    l, n = job[1:]
                    cos, sin = (("cos_lin", "sin_lin") if n < 6 else ("cos_ax", "sin_ax"))
                    tl = tile3[:, n, :]
                    if n >= 12:
                        dve.wait_ge(p_act, taken(JOB[("hsq", l, n)]))
                    else:
                        dve.wait_ge(p_act, taken(JOB[("tile2", l, n)]))
                    if rope_nth(l, n) > 1:
                        dve.wait_ge(roped, rope_nth(l, n) - 1)
                    link(dve.tensor_tensor(rope_a, src[:, 0:T], c_(sin), ALU.mult))
                    op = dve.tensor_tensor(tl, tl, c_(cos), ALU.mult)
                    op.then_inc(p_dve, 1)
                    dve.wait_ge(p_dve, taken(j))
                    op = dve.tensor_tensor(tl, tl, rope_a, ALU.add)
                    if n >= 12:
                        link(op)
                        op = dve.tensor_tensor(tl, tl, sq_tile(n), ALU.mult)
                    op.then_inc(roped, 1)

            def exchange(l):
                dve.wait_ge(roped, rope_nth(l, 15))
                dve.wait_ge(p_act, taken(JOB[("vn", l, 16)]))
                link(dve.tensor_copy(tile3[0:HD, 16, :], tile3[HD:P, 15, :]))
                dve.tensor_copy(tile3[HD:P, 16, :], tile3[0:HD, 15, :]).then_inc(k_copied, 1)

            def maxes(step):
                kind, l, h = STEPS[step]
                par = step % 2
                m_, n_ = mx[:, 8 * par:8 * par + 8], nm[:, 4 * par:4 * par + 4]
                pr = probs[:, 1152 * par:1152 * par + 1152]
                b0 = s_first(step)
                if kind in "AB" and step >= 2:
                    dve.wait_ge(turned, t_first(step - 1))

                def biased(dst, s, b, m):
                    return dve.tensor_tensor_reduce(out=dst, in0=s, in1=b, scale=1.0, scalar=LOW, op0=ALU.add,
                                                    op1=ALU.max, accum_out=m)

                if kind == "A":
                    dve.wait_ge(scores, b0 + 1)
                    s = bank(b0 % 3)
                    biased(pr[:, 0:P], s[:, 0:P], bias3[:, h, P:T], m_[:, 0:1])
                    link(biased(pr[:, P:3 * P], s[:, P:3 * P], bias3[:, h, :], m_[:, 1:2]))
                    dve.tensor_scalar(n_[:, 0:2], m_[:, 0:2], sink[:, h:h + 1], -1.0, ALU.max, ALU.mult
                                      ).then_inc(maxed, 1)
                elif kind == "B":
                    heads = A_HEADS + h
                    dve.wait_ge(scores, b0 + 1)
                    biased(pr[:, 0:384].rearrange("p (g t) -> p g t", g=3),
                           bank(b0 % 3)[:, 0:384].rearrange("p (g t) -> p g t", g=3),
                           bias3[:, heads:BIAS_HEADS:B_HEADS, P:T], m_[:, 0:1])
                    dve.wait_ge(scores, b0 + 2)
                    biased(pr[:, 384:896].rearrange("p (g t) -> p g t", g=2),
                           bank((b0 + 1) % 3).rearrange("p (g t) -> p g t", g=2),
                           bias3[:, heads:heads + B_HEADS + 1:B_HEADS, :], m_[:, 1:2])
                    dve.wait_ge(scores, b0 + 3)
                    link(biased(pr[:, 896:1152], bank((b0 + 2) % 3)[:, 0:T], bias3[:, heads + 2 * B_HEADS, :],
                                m_[:, 2:3]))
                    link(dve.tensor_tensor(m_[:, 1:2], m_[:, 1:2], m_[:, 2:3], ALU.max))
                    dve.tensor_scalar(n_[:, 0:2], m_[:, 0:2], -1.0, None, ALU.mult).then_inc(maxed, 1)
                elif kind == "C":
                    dve.wait_ge(scores, b0 + 1)
                    s = bank(b0 % 3)
                    dve.tensor_reduce(m_[:, 0:1], s[:, 0:P], X, ALU.max)
                    link(dve.tensor_reduce(m_[:, 1:2], s[:, P:3 * P], X, ALU.max))
                    dve.tensor_scalar(n_[:, 0:2], m_[:, 0:2], -(C_QK ** -0.5), None, ALU.mult).then_inc(maxed, 1)
                elif kind == "D":
                    for tt in range(2):
                        dve.wait_ge(scores, b0 + tt + 1)
                        op = dve.tensor_reduce(m_[:, 2 * tt:2 * tt + 2],
                                               bank((b0 + tt) % 3).rearrange("p (m t) -> p m t", m=2), X, ALU.max)
                    link(op)
                    dve.tensor_scalar(n_[:, 0:4], m_[:, 0:4], -(32 ** -0.5), None, ALU.mult).then_inc(maxed, 1)
                else:
                    dve.wait_ge(scores, b0 + 1)
                    link(dve.tensor_reduce(m_[:, 0:2], bank(b0 % 3).rearrange("p (m t) -> p m t", m=2), X, ALU.max))
                    dve.tensor_scalar(n_[:, 0:2], m_[:, 0:2], -(HD ** -0.5), None, ALU.mult).then_inc(maxed, 1)

            def norms(step):
                kind, l, h = STEPS[step]
                par = step % 2
                s_ = sm[:, 4 * par:4 * par + 4]
                pr = probs[:, 1152 * par:1152 * par + 1152]
                dve.wait_ge(exped, step + 1)
                w = 4 if kind == "D" else 2
                if kind == "A":
                    link(dve.tensor_tensor(s_[:, 0:2], s_[:, 0:2], sink_e[:, 2 * par:2 * par + 2], ALU.add))
                link(dve.reciprocal(s_[:, 0:w], s_[:, 0:w]))
                if kind == "D":
                    dve.tensor_scalar(s_[:, 2:4], s_[:, 2:4], neg_lam[:, l:l + 1], None, ALU.mult)
                    for tt in range(2):
                        op = dve.tensor_scalar(pr[:, T * tt:T * tt + T], pr[:, T * tt:T * tt + T],
                                               s_[:, tt:tt + 1], None, ALU.mult)
                    link(op)
                    for tt in range(2):
                        op = dve.scalar_tensor_tensor(pr[:, T * tt:T * tt + T], pr[:, 512 + T * tt:512 + T * tt + T],
                                                      s_[:, 2 + tt:3 + tt], pr[:, T * tt:T * tt + T],
                                                      ALU.mult, ALU.add)
                else:
                    cut = {"A": (P, 3 * P), "C": (P, 3 * P), "B": (384, 1152)}.get(kind, (T, 2 * T))
                    dve.tensor_scalar(pr[:, 0:cut[0]], pr[:, 0:cut[0]], s_[:, 0:1], None, ALU.mult)
                    op = dve.tensor_scalar(pr[:, cut[0]:cut[1]], pr[:, cut[0]:cut[1]], s_[:, 1:2], None, ALU.mult)
                op.then_inc(normed, 1)

            def outs(step):
                kind, l, h = STEPS[step]
                par = h % 2
                chunk = {"A": 0, "B": 2, "C": 4, "D": 0, "G": 3, "M": 6}[kind] + h // 2
                dve.wait_ge(o_ready, step + 1)
                rows = slice(HD * par, HD * par + HD)
                src = bank(5)[rows, T * (step % 2):T * (step % 2) + T]
                if kind in "GM":
                    n = GATE_TILES[chunk]
                    dve.wait_ge(gate_silu, silu_nth(l, n))
                    dve.tensor_tensor(mix3[rows, chunk, :], src, tile3[rows, n, :], ALU.mult).then_inc(o_out, 1)
                else:
                    dve.tensor_copy(mix3[rows, chunk, :], src).then_inc(o_out, 1)

            def moments(tt):
                for c in range(2):
                    op = dve.bn_stats(stats4[:, tt, c, :], x2[:, tt, 512 * c:512 * c + 512])
                link(op)
                dve.bn_aggr(mv3[:, tt, :], stats4[:, tt, :, :].rearrange("p c s -> p (c s)")).then_inc(ln_var, 1)

            def centred(n, tt, ready):
                dve.wait_ge(ready, 32)
                dve.wait_ge(ln_var, 2 * n + tt + 1)
                xs = x2[:, tt, :]
                link(dve.scalar_tensor_tensor(xs, xs, mv3[:, tt, 0:1], ln_row[:, 0, :], ALU.subtract, ALU.mult))

            def scaled(n, tt):
                dve.wait_ge(ln_rstd, 2 * n + tt + 1)
                xs = x2[:, tt, :]
                dve.scalar_tensor_tensor(xs, xs, ln_rs[:, tt:tt + 1], ln_row[:, 1, :], ALU.mult, ALU.add
                                         ).then_inc(ln_done, 1)

            def first_of(one, score, best, values3, n):
                def wide(a):
                    return a.unsqueeze(2).to_broadcast([P, 2, n])

                order = c_("first32")[:, EXPERTS - n:EXPERTS].unsqueeze(1).to_broadcast([P, 2, n])
                one3, score3 = (a.rearrange("p (t n) -> p t n", t=2) for a in (one, score))
                link(dve.tensor_reduce(best, values3, X, ALU.max))
                link(dve.tensor_tensor(score3, values3, wide(best), ALU.is_equal))
                link(dve.tensor_tensor(score3, score3, order, ALU.mult))
                link(dve.tensor_reduce(e_t, score3, X, ALU.max))
                link(dve.tensor_tensor(one3, score3, wide(e_t), ALU.is_equal))

            def route():
                dve.memset(ones, 1.0)
                dve.wait_ge(p_dve, taken(JOB[("logitT",)]))
                g3, e3 = lg[:, :, 0:GROUPS], lg[:, :, GROUPS:GROUPS + EXPERTS]
                first_of(g_one, g_sc, g_mx, g3, GROUPS)
                gw = g_mx.unsqueeze(2).to_broadcast([P, 2, GROUPS])
                dve.tensor_tensor(g_dif.rearrange("p (t n) -> p t n", t=2), g3, gw, ALU.subtract
                                  ).then_inc(route_dif, 1)
                m4 = e_m.rearrange("p (t g e) -> p t g e", t=2, g=GROUPS)
                s4 = e_sc.rearrange("p (t g e) -> p t g e", t=2, g=GROUPS)
                one = g_one.rearrange("p (t g) -> p t g", t=2)
                for tt in range(2):
                    ow = one[:, tt, :].unsqueeze(2).to_broadcast([P, GROUPS, PER_GROUP])
                    ev = e3[:, tt, :].rearrange("p (g e) -> p g e", g=GROUPS)
                    dve.tensor_tensor(m4[:, tt], ev, ow, ALU.mult)
                    link(dve.tensor_scalar(s4[:, tt], ow, -NEG, NEG, ALU.mult, ALU.add))
                link(dve.tensor_tensor(e_m, e_m, e_sc, ALU.add))
                m3 = e_m.rearrange("p (t n) -> p t n", t=2)
                first_of(e_one1, e_sc, e_mx1, m3, EXPERTS)
                link(dve.scalar_tensor_tensor(e_m, e_one1, 3.0 * NEG, e_m, ALU.mult, ALU.add))
                first_of(e_one2, e_sc, e_mx2, m3, EXPERTS)
                dve.tensor_tensor(chosen, e_one1, e_one2, ALU.add).then_inc(chosen_done, 1)
                dve.tensor_tensor(e_t, e_mx2, e_mx1, ALU.subtract).then_inc(route_m, 1)
                dve.wait_ge(route_exp, 1)
                link(dve.tensor_reduce(g_sum, g_exp.rearrange("p (t n) -> p t n", t=2), X, ALU.add))
                dve.wait_ge(route_x, 1)
                link(dve.tensor_scalar(w_1, e_x, 1.0, None, ALU.add))
                link(dve.tensor_tensor(w_1, w_1, g_sum, ALU.mult))
                link(dve.reciprocal(w_1, w_1))
                link(dve.tensor_tensor(w_2, w_1, e_x, ALU.mult))
                ww = [a.unsqueeze(2).to_broadcast([P, 2, EXPERTS]) for a in (w_1, w_2)]
                one1, one2 = (a.rearrange("p (t n) -> p t n", t=2) for a in (e_one1, e_one2))
                link(dve.tensor_tensor(gates3, one1, ww[0], ALU.mult))
                link(dve.tensor_tensor(m3, one2, ww[1], ALU.mult))
                link(dve.tensor_tensor(gates, gates, e_m, ALU.add))

            def more_rounds():
                dve.wait_ge(p_dve, taken(JOB[("rank",)]))
                n = (ROUNDS - 1) * BUNCHES
                cw = cnt_b.unsqueeze(1).to_broadcast([P, ROUNDS - 1, BUNCHES])
                link(dve.tensor_tensor(more_f.rearrange("p (r b) -> p r b", r=ROUNDS - 1), cw,
                                       c_("round_from").rearrange("p (r b) -> p r b", r=ROUNDS - 1), ALU.is_gt))
                link(dve.tensor_reduce(any_more, more_f, X, ALU.max))
                a, b = scan, e_sc[:, 0:n]
                link(dve.memset(a[:, 0:1], 0.0))
                link(dve.tensor_copy(a[:, 1:n], more_f[:, 0:n - 1]))
                d = 1
                while d < n:
                    link(dve.tensor_copy(b[:, 0:d], a[:, 0:d]))
                    link(dve.tensor_tensor(b[:, d:n], a[:, d:n], a[:, 0:n - d], ALU.add))
                    a, b = b, a
                    d *= 2
                link(dve.tensor_copy(flags[:, 0:n], more_f))
                link(dve.tensor_copy(flags[:, n:2 * n], a))
                dve.tensor_copy(flags[:, 2 * n:2 * n + 1], any_more).then_inc(routed, 1)

            LINKS = 4

            def bunch(i, g, r):
                def mlink(ins_, n):
                    ins_.then_inc(moe_chain, 1)
                    dve.wait_ge(moe_chain, i * LINKS + n)

                if isinstance(g, int):
                    rk, gt = (a[:, :, AT_ONCE * g:AT_ONCE * g + AT_ONCE] for a in (rank3, gates3))
                    pl = c_("places")[:, 0:PLACES]
                else:
                    rk, gt = (a[:, :, bass.ds(g * AT_ONCE, AT_ONCE)] for a in (rank3, gates3))
                    if r is None:
                        pl = c_("places")[:, 0:PLACES]
                    else:
                        at = CONST["places"][0] + PLACES
                        pl = const[:, bass.ds(r * PLACES + at, PLACES)]
                pw = pl.unsqueeze(1).to_broadcast([P, AT_ONCE, PLACES])
                for tt in range(2):
                    rw = rk[:, tt, :].unsqueeze(2).to_broadcast([P, AT_ONCE, PLACES])
                    op = dve.tensor_tensor(places4[:, tt], rw, pw, ALU.is_equal)
                mlink(op, 1)
                for tt in range(2):
                    gw = gt[:, tt, :].unsqueeze(2).to_broadcast([P, AT_ONCE, PLACES])
                    op = dve.tensor_tensor(weighed4[:, tt], places4[:, tt], gw, ALU.mult)
                op.then_inc(placed, 1)
                dve.wait_ge(back_ready, i + 1)
                if not isinstance(i, int):
                    dve.wait_ge(summed, i)
                dve.tensor_copy(back, bank(7)[:, 0:256]).then_inc(back_out, 1)
                dve.wait_ge(gate_exped, i + 1)
                mlink(dve.tensor_scalar(gate_e, gate_e, 1.0, None, ALU.add), 2)
                mlink(dve.reciprocal(gate_e, gate_e), 3)
                mlink(dve.tensor_tensor(gate_e, gate_e, bank(6)[:, 0:DE], ALU.mult), 4)
                dve.tensor_tensor(hidden, gate_e, bank(6)[:, DE:2 * DE], ALU.mult).then_inc(hidden_done, 1)
                dve.wait_ge(y_ready, 2 * i + 2)
                dve.tensor_copy(y_e[:, 512:1024], bank(5)).then_inc(y1_out, 1)

            def experts():
                bunch(0, 0, None)
                more_rounds()
                with dve.Fori(1, BUNCHES) as i:
                    bunch(i, i, None)
                some = dve.value_load(flags[0:1, 112:113], min_val=0, max_val=1)
                with dve.If(some):
                    with dve.Fori(0, ROUNDS - 1) as r:
                        with dve.Fori(0, BUNCHES) as g:
                            flag = dve.value_load(flags[0:1, bass.ds(r * BUNCHES + g, 1)], min_val=0, max_val=1)
                            with dve.If(flag):
                                n = dve.value_load(flags[0:1, bass.ds(r * BUNCHES + g + 56, 1)], min_val=0, max_val=55)
                                bunch(n + BUNCHES, g, r)
                for n in FIRST_SPLITS:
                    low(n)
                for tt in range(2):
                    dve.wait_ge(moe_done, tt + 1)
                    for half in range(2):
                        xs = x2[:, tt, 512 * half:512 * half + 512]
                        op = dve.scalar_tensor_tensor(xs, xs, ALPHA, bank(2 * tt + half), ALU.mult, ALU.add)
                    link(op)
                    moments(tt)
                    centred(1, tt, ln2_in)
                    if tt:
                        scaled(1, 0)
                scaled(1, 1)

            def low(n):
                dve.wait_ge(highs, n + 1)
                dve.tensor_tensor(split_of(n)[1], raw_of(n), as_f32(split_of(n)[0]), ALU.subtract).then_inc(lows, 1)

            def x_low_part(l, half):
                dve.wait_ge(x_highs, 2 * l + half + 1)
                own = slice(4 * half, 4 * half + 4)
                dve.tensor_tensor(x_low3[:, own, :], xT3[:, own, :], as_f32(a_high3[:, own, :]), ALU.subtract
                                  ).then_inc(x_lows, 1)

            def mix_low_part(l, part):
                dve.wait_ge(mix_highs, 2 * l + part + 1)
                own = slice(0, KC - 2) if part == 0 else slice(KC - 2, KC)
                dve.tensor_tensor(mix_low3[:, own, :], mix3[:, own, :], as_f32(a_high3[:, own, :]), ALU.subtract
                                  ).then_inc(mix_lows, 1)

            def silu(l, n):
                dve.wait_ge(sigmoid, silu_nth(l, n))
                tl = tile3[:, n, :]
                dve.tensor_tensor(tl, tl, exp_tile(n), ALU.mult).then_inc(gate_silu, 1)
                if n in GATE_TILES[1:3]:
                    gate(l, GATE_TILES.index(n))

            def sub_norm(l, n):
                dve.wait_ge(p_act, taken(JOB[("hso", l, n)]))
                dve.scalar_tensor_tensor(mix3[:, n, :], mix3[:, n, :], sub_g[:, l:l + 1], sq_tile(n),
                                         ALU.mult, ALU.mult).then_inc(sub_done, 1)
                if n == 0:
                    gate(l, n)

            def gate(l, c):
                dve.wait_ge(gate_silu, silu_nth(l, GATE_TILES[c]))
                dve.wait_ge(sub_done, 3 * l + c + 1)
                dve.tensor_tensor(mix3[:, c, :], mix3[:, c, :], tile3[:, GATE_TILES[c], :], ALU.mult
                                  ).then_inc(gated, 1)

            def end_layer(l, tt):
                dve.wait_ge(post_in, 32)
                dve.wait_ge(p_act, taken(JOB[("y2", l, 3, tt)]))
                dve.tensor_reduce(y_ms[:, tt:tt + 1], y_sq[:, 4 * tt:4 * tt + 4], X, ALU.add).then_inc(y_sum, 1)
                dve.wait_ge(y_rstd, 2 * l + tt + 1)
                link(dve.scalar_tensor_tensor(y_nat[:, tt, :], y_nat[:, tt, :], y_rs[:, tt:tt + 1],
                                              post_row[:, l, :], ALU.mult, ALU.mult))
                dve.tensor_tensor(x2[:, tt, :], x2[:, tt, :], y_nat[:, tt, :], ALU.add).then_inc(x_done, 1)

            j = step = drained = 0
            subs_due, gates_due, lows_due = [], [], []
            for jobs, what in TURNS:
                if what in STEP:
                    step = STEP[what]
                    if step == 0:
                        dve.wait_ge(bias_in, 16)
                    if not opens(step):
                        norms(step - 1)
                    maxes(step)
                    if not opens(step) and not opens(step - 1):
                        outs(step - 2)
                    for due in subs_due:
                        sub_norm(*due)
                    for due in gates_due:
                        silu(*due)
                    for n in lows_due:
                        low(n)
                    subs_due, gates_due, lows_due = [], [], []
                    if what[0] == "D" and what[2] == 3:
                        exchange(what[1])
                    drained = 0
                for job in jobs:
                    if job[0] in ("xt2", "y2") or what is None and job[0] == "tile2":
                        for n in lows_due:
                            low(n)
                        lows_due = []
                    lows_due = lows_due + SPLIT_AT.get(j, [])
                    if job[0] == "ct":
                        latent_norm()
                        lambda_sums()
                    if BY_DVE[j]:
                        take(job, j)
                    if job[0] == "xt2" and job[2:] == (1, 1):
                        for half in range(2):
                            x_low_part(job[1], half)
                    if job == ("cq", 0, 0):
                        dve.wait_ge(mem_in, 16)
                        link(rms(mem_sq[:, 0:1], mem_nat[:, 0, :], D, mem_junk, 1e-6))
                        rms(mem_sq[:, 1:2], mem_nat[:, 1, :], D, mem_junk, 1e-6).then_inc(mem_sum, 1)
                    if job == ("cq", 1, 1):
                        latent_rope()
                    if job[:2] == ("y1", 3):
                        dve.wait_ge(p_dve, taken(j))
                        moments(job[2])
                        centred(0, job[2], ln1_in)
                        scaled(0, job[2])
                    if job == ("logitT",):
                        route()
                    if job[0] == "tile2" and job[2] in GATE_TILES:
                        gates_due.append(job[1:])
                    if job == ("tile2", 0, 9):
                        dve.wait_ge(lam_exp, 1)
                        le = lam_e.rearrange("p (l a) -> p l a", l=2)
                        link(dve.tensor_tensor(neg_lam, le[:, :, 1], le[:, :, 0], ALU.subtract))
                        for l in range(LAYERS):
                            dve.tensor_scalar(neg_lam[:, l:l + 1], neg_lam[:, l:l + 1], -LAMBDA_INIT[l], None, ALU.add)
                            op = dve.tensor_scalar(sub_g[:, l:l + 1], vecs[:, 35 + l:36 + l], 1.0 - LAMBDA_INIT[l],
                                                   None, ALU.mult)
                        link(op)
                    if job[0] == "hso":
                        subs_due.append(job[1:])
                    if job[0] == "y2" and job[2] == 3:
                        end_layer(job[1], job[3])
                    j += 1
                if what == "experts":
                    experts()
                elif what is None and jobs == []:
                    if drained == 0:
                        norms(step)
                        outs(step - 1)
                    else:
                        outs(step)
                    if STEPS[step][0] == "M":
                        mix_low_part(STEPS[step][1], drained)
                    drained += 1


_INS = ["x", "w_in", "w_out", "sinks", "rel_bias", "mla_q_norm", "mla_kv_norm", "w_uq", "w_ukv", "ln1_g", "ln1_b",
        "w_route_group", "b_route_group", "w_route_expert", "b_route_expert", "w_expert_gate", "w_expert_up",
        "w_expert_down", "ln2_g", "ln2_b", "mem_2", "pre_norm_2", "w_in_2", "diff_lambda_2", "diff_subln_2",
        "gqa_q_norm_2", "gqa_k_norm_2", "mem_norm_2", "w_mem_kv_2", "w_out_2", "post_norm_2"]


def kernel(**inputs):
    import numpy as _np
    import concourse.bacc as _bacc
    from concourse import mybir as _mybir
    from concourse.bass_utils import run_bass_kernel_spmd as _run

    nc = _bacc.Bacc("TRN2", target_bir_lowering=False, num_devices=1, dynamic_dma_scratch_size=4096)
    arrays, args = {}, {}
    given = {name: _np.ascontiguousarray(inputs[name]) for name in _INS}
    given.update(constants())
    for name, a in given.items():
        arrays[f"in_{name}_dram"] = a
        args[name] = nc.dram_tensor(f"in_{name}_dram", a.shape, _mybir.dt.from_np(a.dtype), kind="ExternalInput").ap()
    out = nc.dram_tensor("out_0_dram", (1, T, D), F32, kind="ExternalOutput").ap()
    build(nc, args, out)
    r = _run(nc, [arrays], core_ids=[0])
    return r.results[0]["out_0_dram"]
```

```python
import math
from contextlib import ExitStack

import numpy as np
import concourse.bass as bass
from concourse import mybir

F32 = mybir.dt.float32
BF16 = mybir.dt.bfloat16
F32R = mybir.dt.float32r
I32 = mybir.dt.int32
ALU = mybir.AluOpType
ACT = mybir.ActivationFunctionType
X = mybir.AxisListType.X

P = 128
T = 256
D = 1024
KC = D // P
COLS = 256
SLOT = KC * COLS
RING = 12
NEG = -1.0e30
LOW = -3.0e38
HD = 64

A_HEADS, B_HEADS, B_GROUPS, C_HEADS = 4, 4, 3, 8
DILATIONS = (1, 4, 16)
C_QK, C_NOPE, C_ROPE = 96, 64, 32
Q_LORA, KV_LORA = 256, 128
C_COLS = Q_LORA + KV_LORA + C_ROPE
A_COLS, B_COLS = 512, 2304
N_BUCKETS = 32
BIAS_HEADS = A_HEADS + B_HEADS * B_GROUPS
VALS = 3 * P - 1
GROUPS, PER_GROUP = 4, 8
EXPERTS = GROUPS * PER_GROUP
DE = 256
ALPHA = 2.0 ** 0.25
HALF = C_ROPE // 2

AT_ONCE = 4
PLACES = P // AT_ONCE
BUNCHES = EXPERTS // AT_ONCE
ROUNDS = T // PLACES
ABSENT = -1024.0

LAYERS = 2
D_HEADS, G_HEADS, M_HEADS = 6, 6, 4
TILES2 = 24
V_TILES = (6, 7, 8, 16)
GATE_TILES = (9, 10, 11, 17, 18, 19, 22, 23)
LAMBDA_INIT = [0.8 - 0.6 * math.exp(-0.3 * l) for l in range(LAYERS)]

_WIDTHS = [("ident", P), ("swap", P), ("headsum", P), ("before", P), ("cos_lin", T), ("sin_lin", T),
           ("cos_ax", T), ("sin_ax", T), ("causal", P), ("cos_c", 2 * HALF), ("sin_c", 2 * HALF),
           ("places", T), ("first32", EXPERTS), ("round_from", (ROUNDS - 1) * BUNCHES)]
CONST = {}
_at = 0
for _name, _w in _WIDTHS:
    CONST[_name] = (_at, _at + _w)
    _at += _w
N_CONST = _at


def constants():
    f = np.float32
    c = {}
    p = np.arange(P)
    c["ident"] = np.eye(P)
    partner = (p // 32) * 32 + (p + 16) % 32
    c["swap"] = (partner[:, None] == p[None, :]).astype(f)
    c["headsum"] = (p[:, None] // HD == p[None, :] // HD).astype(f)
    c["before"] = (p[:, None] < p[None, :]).astype(f)
    inv = (f(10000.0) ** (-np.arange(0, 32, 2, dtype=f) / f(32))).astype(f)
    t = np.arange(T)
    own = inv[p % 16][:, None]
    sign = np.where(p % 32 < 16, -1.0, 1.0)[:, None]
    lin = (t[None, :].astype(f) * own).astype(f)
    c["cos_lin"], c["sin_lin"] = np.cos(lin), np.sin(lin) * sign
    place = np.where((p % HD < 32)[:, None], (t // 64)[None, :], (t % 64)[None, :]).astype(f)
    ax = (place * own).astype(f)
    c["cos_ax"], c["sin_ax"] = np.cos(ax), np.sin(ax) * sign
    c["causal"] = np.where(p[None, :] <= p[:, None], 0.0, NEG)
    tok = p[:, None, None] + P * np.arange(2)[None, :, None]
    ang = (tok.astype(f) * inv[None, None, :]).astype(f)
    c["cos_c"], c["sin_c"] = np.cos(ang).reshape(P, -1), np.sin(ang).reshape(P, -1)
    c["places"] = np.broadcast_to(t[None, :], (P, T))
    c["first32"] = np.broadcast_to(EXPERTS - np.arange(EXPERTS)[None, :], (P, EXPERTS))
    c["round_from"] = np.broadcast_to(
        np.repeat(PLACES * np.arange(1, ROUNDS), BUNCHES)[None, :], (P, (ROUNDS - 1) * BUNCHES))
    table = np.concatenate([np.asarray(c[n], f).reshape(P, -1) for n, _ in _WIDTHS], axis=1)

    dist = 2 * P - 1 - np.arange(VALS)
    d = np.maximum(dist, 0)
    exact = N_BUCKETS // 2
    large = exact + (np.log(np.maximum(d, 1).astype(f) / f(exact)) / f(math.log(2048 / exact))
                     * f(N_BUCKETS - exact)).astype(np.int32)
    bucket = np.where(d < exact, d, np.minimum(large, N_BUCKETS - 1))
    of_bucket = (bucket[None, :] == np.arange(N_BUCKETS)[:, None]).astype(f)
    seen = np.zeros((BIAS_HEADS, VALS), bool)
    seen[:A_HEADS] = (dist >= 0) & (dist <= P - 1)
    for g, dil in enumerate(DILATIONS):
        at = A_HEADS + g * B_HEADS
        seen[at:at + B_HEADS] = (dist >= 0) & (dist % dil == 0) & (dist // dil <= P)
    return {"const_table": np.ascontiguousarray(table, dtype=f), "const_bucket": of_bucket,
            "const_unseen": np.where(seen, 0.0, NEG).astype(f)}


ITEMS = (["c_q", "c_kv", "a_q", "a_kv"]
         + [f"b_{x}{g}" for g in range(B_GROUPS) for x in "qkv"]
         + ["mem_k0", "mem_k1"] + [f"w_out{s}" for s in range(4)] + ["mem_v1", "mem_v0"])
FIRST_EXPERT = len(ITEMS)
ITEMS += [f"expert{e}{y}" for b in range(BUNCHES) for x in ("gu", "d")
          for e in range(AT_ONCE * b, AT_ONCE * (b + 1)) for y in (("g", "u") if x == "gu" else ("d",))]
LOAD_ORDER2 = [0, 1, 2, 3, 4, 7, 8, 6, 9, 10, 5, 11]
for _l in range(LAYERS):
    ITEMS += [f"in{_l}_{n}" for n in LOAD_ORDER2] + [f"out{_l}_{s}" for s in range(4)]
ITEM = {name: n for n, name in enumerate(ITEMS)}
FIRST_BUNCH = (1, 2, 3, 5, 6, 7, 0, 8, 9, 4, 10, 11)
FIRST2 = FIRST_EXPERT + RING * BUNCHES
MIXERS_RING = 5
PIECES = {"a_q": A_HEADS}


def slot_of(n):
    if n < FIRST_EXPERT:
        return n % MIXERS_RING
    return (n - FIRST_EXPERT) % RING if n < FIRST2 else (n - FIRST2) % MIXERS_RING


def all_loaded(n):
    return 16 * sum(PIECES.get(ITEMS[m], 1) for m in range(n + 1) if slot_of(m) == slot_of(n))


TAKEN_BY_DVE = ("bias", "xt2", "y1", "logit", "logitT", "rank", "swap")


Y_ORDER = ((0, 0), (0, 1), (1, 0), (1, 1), (2, 0), (3, 0), (2, 1), (3, 1))


def schedule():
    turns = []
    jobs = [("xt", k) for k in range(4)] + [("cnat", 0), ("bias",), ("cnat", 1), ("vec",)]
    jobs += [("tile1", n) for n in range(4)]
    jobs += [("ct",), ("ckt",), ("avn",), ("cq", 0, 0), ("cq", 0, 1), ("cq", 1, 0), ("cq", 1, 1)]
    jobs += [("ck", k) for k in range(4)] + [("cv", 0), ("cv", 1)] + [("cqt", k) for k in range(4)]
    turns.append((jobs, None))
    fill = []
    for g in range(B_GROUPS):
        fill += [("tile1", 4 + 2 * g), ("tile1", 5 + 2 * g), ("tile1", 10 + 2 * g), ("tile1", 11 + 2 * g),
                 ("bv", g, 0), ("bv", g, 1)]
    steps = [("A", 0, h) for h in range(A_HEADS)] + [("C", 0, h) for h in range(C_HEADS)]
    for n, s in enumerate(steps):
        turns.append((fill[n * len(fill) // 12:(n + 1) * len(fill) // 12], s))
    turns[-1][0].append(("mt", 0))
    of_b = [[("mt", 1), ("mt", 2)], [("mt", 3), ("mk", 0, 0)], [("mk", 0, 1), ("mk", 1, 0)], [("mk", 1, 1)]]
    for h in range(B_HEADS):
        turns.append((of_b[h], ("B", 0, h)))
    turns += [([], None), ([], None)]
    jobs = [("y1", s, tt) for s, tt in Y_ORDER]
    jobs += [("mv", 0, 0), ("mv", 0, 1)]
    jobs += [("x1t", k) for k in range(4)] + [("logit",), ("logitT",), ("mv", 1, 0), ("mv", 1, 1), ("rank",)]
    turns.append((jobs, None))
    turns.append(([], "experts"))
    for l in range(LAYERS):
        jobs = [("xt2", l, tt, half) for tt in range(2) for half in range(2)]
        for n in range(6):
            jobs.append(("tile2", l, n))
            if n >= 1:
                jobs.append(("swap", l, n - 1))
        turns.append((jobs, None))
        steps = ([("D", l, h) for h in range(D_HEADS)] + [("G", l, h) for h in range(G_HEADS)]
                 + [("M", l, h) for h in range(M_HEADS)])
        tiles = [[6, 7], [8, 15], [16, 12], [13, 9], [14], [17], [18], [20], [19], [10], [22], [21], [11], [23], [], []]
        before, behind = ([[] for _ in range(len(steps) + 2)] for _ in range(2))
        before[0].append(("swap", l, 5))
        for n, own in enumerate(tiles):
            for t in own:
                if 12 <= t <= 15:
                    behind[n + 1].append(("hsq", l, t))
                    before[n + 2].append(("swap", l, t))
                if t in V_TILES:
                    behind[n + 1].append(("vn", l, t))
        for n in range(3):
            behind[5 + 2 * n].append(("hso", l, n))
        for n, s in enumerate(steps):
            turns.append((before[n] + [("tile2", l, t) for t in tiles[n]] + behind[n], s))
        turns += [([], None), ([], None)]
        turns.append(([("y2", l, s, tt) for s, tt in Y_ORDER], None))
    return turns


TURNS = schedule()
JOBS = [job for jobs, _ in TURNS for job in jobs]
JOB = {job: n for n, job in enumerate(JOBS)}
BY_DVE = [job[0] in TAKEN_BY_DVE for job in JOBS]


def taken(n):
    return sum(BY_DVE[m] == BY_DVE[n] for m in range(n + 1))


STEPS = [s for _, s in TURNS if isinstance(s, tuple)]
STEP = {s: n for n, s in enumerate(STEPS)}
S_JOBS = {"A": 1, "B": 3, "C": 1, "D": 2, "G": 1, "M": 1}
T_JOBS = {"A": 1, "B": 3, "C": 1, "D": 1, "G": 1, "M": 1}


def s_first(step):
    return sum(S_JOBS[s[0]] for s in STEPS[:step])


def t_first(step):
    return sum(T_JOBS[s[0]] for s in STEPS[:step])



def opens(step):
    return STEPS[step] in (("A", 0, 0), ("D", 0, 0), ("D", 1, 0))


S_OWNER = [n for n, s in enumerate(STEPS) for _ in range(S_JOBS[s[0]])]


def item_of(job):
    kind = job[0]
    if kind == "cnat":
        return ["c_q", "c_kv"]
    if kind == "tile1":
        n = job[1]
        return ["a_q"] if n < 2 else ["a_kv"] if n < 4 else [f"b_q{(n - 4) // 2}"] if n < 10 else [f"b_k{(n - 10) // 2}"]
    if kind == "bv":
        return [f"b_v{job[1]}"]
    if kind == "y1":
        return [f"w_out{job[1]}"]
    if kind in ("mk", "mv"):
        return [f"mem_{kind[1]}{job[1]}"]
    if kind == "tile2":
        return [f"in{job[1]}_{job[2] // 2}"]
    if kind == "y2":
        return [f"out{job[1]}_{job[2]}"]
    return []


LAST_JOB = {}
for _n, _job in enumerate(JOBS):
    for _name in item_of(_job):
        LAST_JOB[_name] = _n

UNITS = 6
OF_TILES, OF_ITEMS = ("tile1", "tile2"), ("bv", "y1", "y2")
SPLITS = []
for _job in JOBS:
    _what = _job if _job[0] in OF_TILES else _job[:-1] if _job[0] in OF_ITEMS else None
    if _what and _what not in SPLITS:
        SPLITS.append(_what)
SPLIT = {what: n for n, what in enumerate(SPLITS)}
UNIT_OWNER = [n for n, what in enumerate(SPLITS) for _ in range(1 if what[0] in OF_TILES else 2)]


def units_before(split):
    return UNIT_OWNER.index(split)


def users(split):
    what = SPLITS[split]
    return [JOB[what]] if what[0] in OF_TILES else [JOB[what + (tt,)] for tt in range(2)]


def freed_by(split):
    before = [UNIT_OWNER[u - UNITS] for u, owner in enumerate(UNIT_OWNER) if owner == split and u >= UNITS]
    return max((max(users(b)) for b in before), default=-1)


def item_split(split):
    return ITEM[item_of(SPLITS[split] if SPLITS[split][0] in OF_TILES else SPLITS[split] + (0,))[0]]


LAST_SPLIT = {item_split(n): n for n in range(len(SPLITS))}
OPENING = [SPLIT[("tile1", 0)]] + [SPLIT[("tile2", l, 0)] for l in range(LAYERS)]
AT_EXPERTS = range(OPENING[1], OPENING[1] + 3)
SPLIT_AT = {}
_at = 0
for _n in range(len(SPLITS)):
    _phase = max(p for p in range(len(OPENING)) if OPENING[p] <= _n)
    _ahead = _n - OPENING[_phase]
    if _ahead >= 3:
        _at = max(_at, users(_n - 3)[0])
    elif _phase == 0 or _ahead == 2:
        _at = max(_at, users(OPENING[_phase])[0] + _ahead - 2)
    _at = max(_at, freed_by(_n) + 1)
    if SPLITS[_n] == ("y1", 2):
        _at = max(_at, JOB[("mk", 0, 0)])
    if _n not in AT_EXPERTS:
        SPLIT_AT.setdefault(_at, []).append(_n)

ALL = slice(None)
X_PARTS = [[(ALL, slice(4 * half, 4 * half + 4), ALL) for half in range(2)]] + [
    [(ALL, slice(4 * half, 4 * half + 4), slice(P * tt, P * tt + P)) for tt in range(2) for half in range(2)]] * LAYERS


def x_part(phase, part):
    return sum(len(parts) for parts in X_PARTS[:phase]) + part + 1


MIX_PARTS = [[(4, 8), (0, 3), (3, 4)]] + [[(0, 6), (6, 8)]] * LAYERS
MIX_LAST = [[("C", 0, C_HEADS - 1), ("B", 0, 1), ("B", 0, B_HEADS - 1)]] + [
    [("G", l, G_HEADS - 1), ("M", l, M_HEADS - 1)] for l in range(LAYERS)]


def mix_part(phase, part):
    return sum(len(parts) for parts in MIX_PARTS[:phase]) + part + 1


def build(nc, ins, out):
    ctx = ExitStack()
    with ctx:
        def sb(name, shape, dt=F32):
            return ctx.enter_context(nc.sbuf_tensor(name, shape, dt))

        def sem(name):
            return ctx.enter_context(nc.semaphore(name))

        with nc.sbuf_tensor("slots_before", [P, MIXERS_RING * SLOT], F32), \
                nc.sbuf_tensor("w_high", [P, UNITS * SLOT // 2], F32R) as w_high, \
                nc.sbuf_tensor("w_low", [P, UNITS * SLOT // 2], F32R) as w_low, \
                nc.sbuf_tensor("a_high", [P, KC * T], F32R) as a_high, \
                nc.sbuf_tensor("x_low", [P, KC * T], F32R) as x_low, \
                nc.sbuf_tensor("mix_low", [P, KC * T], F32R) as mix_low:
            pass
        ring = sb("ring", [P, RING * SLOT])
        xT = sb("xT", [P, KC * T])
        mixT = sb("mixT", [P, KC * T])
        const = sb("const", [P, N_CONST])
        x_nat = sb("x_nat", [P, 2 * D])
        tiles = sb("tiles", [P, TILES2 * T])
        v_nat = sb("v_nat", [P, 2048])
        q_c = sb("q_c", [P, C_HEADS * T])
        k_c = sb("k_c", [P, C_HEADS * T])
        v_c = sb("v_c", [P, 1024])
        bias = sb("bias", [P, BIAS_HEADS * T])
        probs = sb("probs", [P, 2 * 1152])
        probsT = sb("probsT", [P, 4 * 512])
        vecs = sb("vecs", [P, 41])
        small = sb("small", [P, 256])
        ident_b = sb("ident_b", [P, P], BF16)
        causal_b = sb("causal_b", [P, P], BF16)
        zeros_b = sb("zeros_b", [P, 512], BF16)
        router_w = sb("router_w", [P, KC * (GROUPS + EXPERTS)])
        router = router_w[:, :].rearrange("p (k n) -> p k n", k=KC)
        flags = sb("flags", [P, 2 * (ROUNDS - 1) * BUNCHES + 2], I32)
        psum = ctx.enter_context(nc.psum_tensor("psum", [P, 8, 512], F32))

        def bank(n):
            return psum[:, n, :]

        def c_(name):
            a, b = CONST[name]
            return const[:, a:b]

        ident, swap, headsum, before = c_("ident"), c_("swap"), c_("headsum"), c_("before")
        slots = ring[:, :].rearrange("p (s k n) -> p s k n", s=RING, k=KC)
        x2 = x_nat[:, :].rearrange("p (t d) -> p t d", t=2)
        x4 = x_nat[:, :].rearrange("p (t k q) -> p t k q", t=2, k=KC)
        xT3 = xT[:, :].rearrange("p (k t) -> p k t", k=KC)
        y_nat = tiles[:, 0:2048].rearrange("p (t d) -> p t d", t=2)
        mix3 = mixT[:, :].rearrange("p (k t) -> p k t", k=KC)
        a_high3, x_low3, mix_low3 = (a[:, :].rearrange("p (k t) -> p k t", k=KC) for a in (a_high, x_low, mix_low))

        def split_of(n):
            wide = P if SPLITS[n][0] in OF_TILES else COLS
            a = units_before(n) % UNITS * KC * P
            return [w[:, a:a + KC * wide].rearrange("p (k n) -> p k n", k=KC) for w in (w_high, w_low)]

        def raw_of(n):
            what, s = SPLITS[n], slots[:, slot_of(item_split(n))]
            return s[:, :, P * (what[-1] % 2):P * (what[-1] % 2) + P] if what[0] in OF_TILES else s

        def as_f32(a):
            return a.bitcast(F32)
        tile3 = tiles[:, :].rearrange("p (n t) -> p n t", n=TILES2)
        qc3 = q_c[:, :].rearrange("p (h t) -> p h t", h=C_HEADS)
        kc3 = k_c[:, :].rearrange("p (h t) -> p h t", h=C_HEADS)
        vc3 = v_c[:, :].rearrange("p (t n) -> p t n", t=2)
        bias3 = bias[:, :].rearrange("p (h t) -> p h t", h=BIAS_HEADS)
        va = v_nat[:, 0:256].rearrange("p (t n) -> p t n", t=2)
        vb = v_nat[:, 256:1792].rearrange("p (t g n) -> p t g n", t=2, g=B_GROUPS)
        v2 = v_nat[:, 0:1024].rearrange("p (t n m) -> p t n m", t=2, n=4)
        ln_row = tiles[:, 4096:6144].rearrange("p (n d) -> p n d", n=2)
        post_row = bias[:, 0:2048].rearrange("p (n d) -> p n d", n=2)
        vec_rows = q_c[:, 1024:1024 + P]
        c_nat = mixT[:, 0:2 * C_COLS].rearrange("p (t n) -> p t n", t=2)
        c_qT = mixT[:, 832:832 + 512].rearrange("p (k t) -> p k t", k=2)
        c_kvT = mixT[:, 1344:1600]
        rope_t = mixT[:, 1600:2048]
        qc_nat = probs[:, 0:1536].rearrange("p (t n) -> p t n", t=2)
        w_uq = tiles[:, 10 * T:10 * T + 1536].rearrange("p (k n) -> p k n", k=2)
        w_ukv = tiles[:, 5 * T:5 * T + 1024]
        mem_nat = tiles[:, 4096:6144].rearrange("p (t d) -> p t d", t=2)
        mem4 = tiles[:, 4096:6144].rearrange("p (t k q) -> p t k q", t=2, k=KC)
        memT = [a[:, :].rearrange("p (k t) -> p k t", k=KC) for a in (xT, k_c)]
        mem_k = v_c[:, :].rearrange("p (l n t) -> p l n t", l=LAYERS, n=2)
        mem_v = v_nat[:, 1024:2048].rearrange("p (l t n) -> p l t n", l=LAYERS, t=2)
        places4 = tiles[:, 0:256].rearrange("p (t e s) -> p t e s", t=2, e=AT_ONCE)
        places2 = tiles[:, 0:256].rearrange("p (t s) -> p t s", t=2)
        weighed4 = tiles[:, 256:512].rearrange("p (t e s) -> p t e s", t=2, e=AT_ONCE)
        weighed2 = tiles[:, 256:512].rearrange("p (t s) -> p t s", t=2)
        back = tiles[:, 512:768]
        gate_e = tiles[:, 768:1024]
        hidden = tiles[:, 1024:1280]
        hiddenT = tiles[:, 1280:1536].rearrange("p (k s) -> p k s", k=2)
        y_e = tiles[:, 1536:2560]
        gathered = q_c[:, 0:1024].rearrange("p (k s) -> p k s", k=KC)
        more_g = xT[:, :]
        more_u = mixT[:, :]
        more_d = k_c[:, :]
        xn2 = probs[:, 0:2048].rearrange("p (t d) -> p t d", t=2)
        xn4 = probs[:, 0:2048].rearrange("p (t k q) -> p t k q", t=2, k=KC)

        used = [0]

        def col(n, rows_=P):
            a = used[0]
            used[0] += n
            assert used[0] <= 256
            return small[0:rows_, a:a + n]

        eps6, eps5 = col(1), col(1)
        sink = col(A_HEADS)
        route_b = col(1)
        c_sq, c_rs = col(4), col(4)
        mx, nm, sm, sink_e = col(2 * 8), col(2 * 4), col(2 * 4), col(2 * 2)
        ln_stats, ln_mv, ln_rs = col(2 * 12), col(4), col(2)
        mem_sq, mem_rs = col(2), col(2)
        x_sq, x_rs = col(2), col(2)
        y_sq, y_ms, y_rs = col(8), col(2), col(2)
        lam_s, lam_e, neg_lam = col(4), col(4), col(2)
        lam_p = v_nat[:, 1024:1280]
        sub_g = col(2)
        stats4 = ln_stats.rearrange("p (t c s) -> p t c s", t=2, c=2)
        mv3 = ln_mv.rearrange("p (t s) -> p t s", t=2)
        bucket_sb, rel_sb = probsT[0:N_BUCKETS, 0:VALS + 1], probsT[0:N_BUCKETS, 384:384 + BIAS_HEADS]
        unseen_sb, bias_sb = probsT[0:BIAS_HEADS, 512:512 + VALS], probsT[0:BIAS_HEADS, 1024:1024 + VALS]
        rope_s = q_c[:, 0:512]
        mem_junk = q_c[:, 0:D]
        rope_a = q_c[:, 7 * T:8 * T]

        def sq_tile(n):
            m = n - 12 if n >= 12 else 4 + n
            return q_c[:, T * m:T * m + T]

        def exp_tile(n):
            m = GATE_TILES.index(n)
            return k_c[:, T * m:T * m + T]

        rt = [0]

        def rcol(n):
            a = rt[0]
            rt[0] += n
            assert rt[0] <= 2048
            return probs[:, a:a + n]

        logitT_sb = rcol(T)
        lg = rcol(72).rearrange("p (t n) -> p t n", t=2)
        g_mx, g_eq, g_sc, g_one, g_dif, g_exp, g_sum, p_grp = (rcol(2), rcol(8), rcol(8), rcol(8), rcol(8), rcol(8),
                                                               rcol(2), rcol(2))
        e_m, e_sc, e_one1, e_one2 = rcol(64), rcol(64), rcol(64), rcol(64)
        e_mx1, e_mx2, e_t, e_x, w_1, w_2 = rcol(2), rcol(2), rcol(2), rcol(2), rcol(2), rcol(2)
        chosen, gates, rank = rcol(64), rcol(64), rcol(64)
        cnt, cnt_b, more_f, scan = rcol(EXPERTS), rcol(BUNCHES), rcol(56), rcol(56)
        any_more = rcol(1)
        ones = rcol(P)
        rank3 = rank.rearrange("p (t e) -> p t e", t=2)
        gates3 = gates.rearrange("p (t e) -> p t e", t=2)
        chosen3 = chosen.rearrange("p (t e) -> p t e", t=2)

        bias_dram = nc.dram_tensor("bias_rows", [BIAS_HEADS, P, VALS], F32, kind="Internal").ap()

        loaded = [sem(f"loaded{s}") for s in range(RING)]
        x_in, const_in, vec_in, small_in = sem("x_in"), sem("const_in"), sem("vec_in"), sem("small_in")
        ln1_in, ln2_in, post_in = sem("ln1_in"), sem("ln2_in"), sem("post_in")
        table_in, bias_out, bias_in, mem_in = sem("table_in"), sem("bias_out"), sem("bias_in"), sem("mem_in")
        p_ready = sem("p_ready")
        p_act, p_dve = sem("p_act"), sem("p_dve")
        setup = sem("setup")
        c_sums, c_rstd, c_scaled = sem("c_sums"), sem("c_rstd"), sem("c_scaled")
        qc_roped, kc_roped = sem("qc_roped"), sem("kc_roped")
        scores, maxed, exped, sink_exped = sem("scores"), sem("maxed"), sem("exped"), sem("sink_exped")
        normed, turned, turned_out = sem("normed"), sem("turned"), sem("turned_out")
        o_ready, o_out = sem("o_ready"), sem("o_out")
        mem_sum, mem_scaled = sem("mem_sum"), sem("mem_scaled")
        ln_var, ln_rstd, ln_done = sem("ln_var"), sem("ln_rstd"), sem("ln_done")
        route_dif, route_exp, route_m, route_x = sem("route_dif"), sem("route_exp"), sem("route_m"), sem("route_x")
        chosen_done, routed = sem("chosen_done"), sem("routed")
        placed, gathered_ready, gathered_out = sem("placed"), sem("gathered_ready"), sem("gathered_out")
        back_ready, back_out = sem("back_ready"), sem("back_out")
        gu_ready, gate_exped, hidden_done = sem("gu_ready"), sem("gate_exped"), sem("hidden_done")
        hT_ready, hT_out = sem("hT_ready"), sem("hT_out")
        y_ready, y0_out, y1_out, summed = sem("y_ready"), sem("y0_out"), sem("y1_out"), sem("summed")
        more_in, more_down_in, more_used = sem("more_in"), sem("more_down_in"), sem("more_used")
        moe_done = sem("moe_done")
        x_rstd, x_scaled = sem("x_rstd"), sem("x_scaled")
        y_sum, y_rstd, x_done = sem("y_sum"), sem("y_rstd"), sem("x_done")
        lam_sum, lam_exp = sem("lam_sum"), sem("lam_exp")
        sigmoid = sem("sigmoid")
        roped, squared, gate_silu, gated = sem("roped"), sem("squared"), sem("gate_silu"), sem("gated")
        o_squared, sub_done, k_copied = sem("o_squared"), sem("sub_done"), sem("k_copied")
        router_in, latent_in = sem("router_in"), sem("latent_in")
        highs, lows = sem("highs"), sem("lows")
        x_highs, x_lows, mix_highs, mix_lows = sem("x_highs"), sem("x_lows"), sem("mix_highs"), sem("mix_lows")
        act_chain, dve_chain, moe_chain = sem("act_chain"), sem("dve_chain"), sem("moe_chain")
        stored = sem("stored")

        def rope_nth(l, n):
            order = [j[2] for j in JOBS if j[0] == "swap" and j[1] == l]
            return l * len(order) + order.index(n) + 1

        def silu_nth(l, n):
            order = [j[2] for j in JOBS if j[0] == "tile2" and j[1] == l and j[2] in GATE_TILES]
            return l * len(order) + order.index(n) + 1

        def hsq_nth(l, n):
            order = [j[2] for j in JOBS if j[0] == "hsq" and j[1] == l]
            return l * len(order) + order.index(n) + 1

        block = ctx.enter_context(nc.Block())

        @block.sync
        def _(sp):
            def source(name):
                w_in, w_out = ins["w_in"][0], ins["w_out"][0]

                def k_rows(w, a, b):
                    return w[:, a:b].rearrange("(k p) n -> p k n", p=P)

                if name == "c_q":
                    return k_rows(w_in, A_COLS + B_COLS, A_COLS + B_COLS + Q_LORA)
                if name == "c_kv":
                    return k_rows(w_in, A_COLS + B_COLS + Q_LORA, A_COLS + B_COLS + C_COLS)
                if name == "a_kv":
                    return k_rows(w_in, 256, 512)
                if name[:2] == "b_":
                    at = A_COLS + 768 * "qkv".index(name[2]) + 256 * int(name[3])
                    return k_rows(w_in, at, at + 256)
                if name[:5] == "w_out":
                    s = int(name[5])
                    return k_rows(w_out, 256 * s, 256 * s + 256)
                if name[:4] == "mem_":
                    at = 256 * "kv".index(name[4])
                    return k_rows(ins["w_mem_kv_2"][int(name[5])], at, at + 256)
                if name[:2] == "in":
                    l, n = int(name[2]), int(name[4:])
                    return k_rows(ins["w_in_2"][l], 256 * n, 256 * n + 256)
                l, s = int(name[3]), int(name[5])
                return k_rows(ins["w_out_2"][l], 256 * s, 256 * s + 256)

            def load(n):
                name, s = ITEMS[n], slot_of(n)
                if name == "a_q":
                    for m, h in enumerate((0, 2, 1, 3)):
                        sp.dma_start(slots[:, s, :, HD * m:HD * m + HD],
                                     ins["w_in"][0, :, HD * h:HD * h + HD].rearrange("(k p) n -> p k n", p=P)
                                     ).then_inc(loaded[s], 16)
                else:
                    src = source(name)
                    sp.dma_start(slots[:, s, :, 0:src.shape[2]], src).then_inc(loaded[s], 16)

            def used_up(n):
                if n in LAST_SPLIT:
                    sp.wait_ge(lows, LAST_SPLIT[n] + 1)
                else:
                    sp.wait_ge(p_ready, LAST_JOB[ITEMS[n]] + 1)

            def load_bunch(b, first):
                for k in FIRST_BUNCH if first else range(RING):
                    if not first:
                        if k == 0:
                            sp.wait_ge(gu_ready, b)
                        if k == 2 * AT_ONCE:
                            sp.wait_ge(y_ready, 2 * b)
                    elif k < MIXERS_RING:
                        used_up(max(n for n in range(FIRST_EXPERT) if slot_of(n) == k))
                    elif k == MIXERS_RING:
                        sp.wait_ge(p_ready, JOB[("y1", 3, 1)] + 1)
                    name = ("w_expert_gate", "w_expert_up")[k % 2] if k < 2 * AT_ONCE else "w_expert_down"
                    e = k // 2 if k < 2 * AT_ONCE else k - 2 * AT_ONCE
                    w = ins[name][0, bass.ds(b * AT_ONCE + e, 1)]
                    sp.dma_start(ring[:, k * SLOT:(k + 1) * SLOT],
                                 w.rearrange("o (p k) n -> p (o k n)", p=P)).then_inc(loaded[k], 16)

            def small_loads():
                def vec(at, n, src):
                    sp.dma_start(vec_rows[at:at + n, 0:src.shape[1]], src).then_inc(vec_in, 16)

                vec(0, 16, ins["pre_norm_2"].rearrange("l (k q) -> (l k) q", q=P))
                vec(16, 16, ins["mem_norm_2"].rearrange("l (k q) -> (l k) q", q=P))
                vec(32, 2, ins["mla_q_norm"].rearrange("l (k q) -> (l k) q", q=P))
                vec(34, 1, ins["mla_kv_norm"])
                for at, name in ((35, "diff_subln_2"), (37, "gqa_q_norm_2"), (39, "gqa_k_norm_2")):
                    for j in range(2):
                        sp.dma_start(vec_rows[at:at + 2, HD * j:HD * j + HD], ins[name]).then_inc(vec_in, 16)
                sp.dma_start(sink, ins["sinks"][0].partition_broadcast(P)).then_inc(small_in, 16)
                sp.dma_start(route_b[0:GROUPS, :], ins["b_route_group"].rearrange("o g -> g o")).then_inc(small_in, 16)
                sp.dma_start(route_b[GROUPS:GROUPS + EXPERTS, :],
                               ins["b_route_expert"].rearrange("o g e -> (g e) o")).then_inc(small_in, 16)
                sp.dma_start(lam_p, ins["diff_lambda_2"].rearrange("l a d -> (l a d)").partition_broadcast(P)
                               ).then_inc(small_in, 16)

            sp.dma_start(x2, ins["x"][0].rearrange("(t p) d -> p t d", p=P)).then_inc(x_in, 16)
            sp.dma_start(const[:, :], ins["const_table"]).then_inc(const_in, 16)
            for n in range(FIRST_EXPERT):
                if n >= MIXERS_RING:
                    used_up(n - MIXERS_RING)
                load(n)
                if n == 2:
                    small_loads()
                    sp.dma_start(w_uq, ins["w_uq"][0].rearrange("(k p) n -> p k n", p=P)).then_inc(latent_in, 16)
                    sp.dma_start(w_ukv, ins["w_ukv"][0]).then_inc(latent_in, 16)
                if n == 4:
                    sp.dma_start(mem_nat, ins["mem_2"][0].rearrange("(t p) d -> p t d", p=P)).then_inc(mem_in, 16)
                if n == MIXERS_RING:
                    sp.wait_ge(p_dve, taken(JOB[("bias",)]))
                    sp.dma_start(bias_dram, bias_sb.unsqueeze(1).to_broadcast([BIAS_HEADS, P, VALS])
                                 ).then_inc(bias_out, 16)
                    sp.wait_ge(bias_out, 16)
                    shifted = bass.AP(tensor=bias_dram.tensor, offset=P - 1,
                                      ap=[[VALS - 1, P], [P * VALS, BIAS_HEADS], [1, T]])
                    sp.dma_start(bias3, shifted).then_inc(bias_in, 16)
                if n == MIXERS_RING + 1:
                    sp.dma_start(router[:, :, 0:GROUPS],
                                 ins["w_route_group"][0].rearrange("(k p) n -> p k n", p=P)).then_inc(router_in, 16)
                    for g in range(GROUPS):
                        sp.dma_start(router[:, :, GROUPS + PER_GROUP * g:GROUPS + PER_GROUP * (g + 1)],
                                     ins["w_route_expert"][0, g].rearrange("(k p) n -> p k n", p=P)
                                     ).then_inc(router_in, 16)
            load_bunch(0, True)
            with sp.Fori(1, BUNCHES) as b:
                load_bunch(b, False)

            sp.wait_ge(routed, 1)
            some = sp.value_load(flags[0:1, 112:113], min_val=0, max_val=1)
            with sp.If(some):
                with sp.Fori(0, ROUNDS - 1) as r:
                    with sp.Fori(0, BUNCHES) as g:
                        flag = sp.value_load(flags[0:1, bass.ds(r * BUNCHES + g, 1)], min_val=0, max_val=1)
                        with sp.If(flag):
                            n = sp.value_load(flags[0:1, bass.ds(r * BUNCHES + g + 56, 1)], min_val=0, max_val=55)
                            sp.wait_ge(y_ready, n * 2 + 2 * BUNCHES)
                            for e in range(AT_ONCE):
                                if e:
                                    sp.wait_ge(more_used, n * 6 + e)
                                for dst, w in ((more_g, ins["w_expert_gate"]), (more_u, ins["w_expert_up"])):
                                    sp.dma_start(dst, w[0, bass.ds(g * AT_ONCE + e, 1)].rearrange(
                                        "o (p k) n -> p (o k n)", p=P)).then_inc(more_in, 16)
                            for e in range(AT_ONCE):
                                if e:
                                    sp.wait_ge(more_used, n * 6 + 3 + e)
                                sp.dma_start(more_d, ins["w_expert_down"][0, bass.ds(g * AT_ONCE + e, 1)].rearrange(
                                    "o (p k) n -> p (o k n)", p=P)).then_inc(more_down_in, 16)

            for n in range(FIRST2, len(ITEMS)):
                if n == FIRST2:
                    sp.wait_ge(gu_ready, BUNCHES)
                elif n >= FIRST2 + MIXERS_RING:
                    used_up(n - MIXERS_RING)
                load(n)
            out2 = out[0].rearrange("(t p) d -> p t d", p=P)
            for tt in range(2):
                sp.wait_ge(x_done, 2 * LAYERS - 1 + tt)
                sp.dma_start(out2[:, tt, :], x2[:, tt, :]).then_inc(stored, 16)
            sp.wait_ge(stored, 32)

        @block.gpsimd
        def _(pool):
            pool.wait_ge(p_ready, JOB[("mt", 3)] + 1)
            for n, name in enumerate(("ln1_g", "ln1_b")):
                pool.dma_start(ln_row[:, n, :], ins[name][0].partition_broadcast(P)).then_inc(ln1_in, 16)
            pool.wait_ge(ln_done, 2)
            for n, name in enumerate(("ln2_g", "ln2_b")):
                pool.dma_start(ln_row[:, n, :], ins[name][0].partition_broadcast(P)).then_inc(ln2_in, 16)
            for n in range(LAYERS):
                pool.dma_start(post_row[:, n, :], ins["post_norm_2"][n].partition_broadcast(P)
                               ).then_inc(post_in, 16)

        @block.tensor
        def _(pe):
            def arrived(name):
                pe.wait_ge(loaded[slot_of(ITEM[name])], all_loaded(ITEM[name]))

            def product(dst, left, right, first, last):
                pe.matmul(dst, left[0], right[0], start=first, stop=False)
                pe.matmul(dst, left[0], right[1], start=False, stop=False)
                return pe.matmul(dst, left[1], right[0], start=False, stop=last)

            def turned_product(dst, job, phase):
                pe.wait_ge(lows, SPLIT[job] + 1)
                w = split_of(SPLIT[job])
                for k in range(KC):
                    if k in (0, 4) and SPLIT[job] == OPENING[phase]:
                        pe.wait_ge(x_lows, x_part(phase, len(X_PARTS[phase]) - 2 + k // 4))
                    mm = product(dst[:, 0:T], [a[:, k, :] for a in w], (a_high3[:, k, :], x_low3[:, k, :]),
                                 k == 0, k == KC - 1)
                return mm

            def natural_product(dst, job, low, order, waits):
                pe.wait_ge(lows, SPLIT[job[:-1]] + 1)
                w = split_of(SPLIT[job[:-1]])
                own = slice(P * job[-1], P * job[-1] + P)
                for k in order:
                    if k in waits:
                        pe.wait_ge(mix_lows, waits[k])
                    mm = product(dst[:, 0:COLS], (a_high3[:, k, own], low[:, k, own]), [a[:, k, :] for a in w],
                                 k == order[0], k == order[-1])
                return mm

            def output_product(dst, job, phase):
                order = [k for a, b in MIX_PARTS[phase] for k in range(a, b)]
                waits = {a: mix_part(phase, n) for n, (a, b) in enumerate(MIX_PARTS[phase])}
                return natural_product(dst, job, mix_low3, order, waits if job[-2:] == (0, 0) else {})

            def from_act(job):
                pe.wait_ge(p_act, taken(JOB[job]))

            def from_dve(job):
                pe.wait_ge(p_dve, taken(JOB[job]))

            def slot(name):
                return slots[:, slot_of(ITEM[name])]

            def natural(dst, src, tt, w, a, b):
                for k in range(KC):
                    mm = pe.matmul(dst, src[:, k, P * tt:P * tt + P], w[:, k, a:b], start=(k == 0), stop=(k == KC - 1))
                return mm

            def turn4(dst, src4, k):
                for c in range(2):
                    for tt in range(2):
                        mm = pe.transpose(dst[:, c * T + tt * P:c * T + tt * P + P], src4[:, tt, 2 * k + c, :], ident)
                return mm

            def run(job, j):
                kind = job[0]
                dst = bank(6 + j % 2)
                if j >= 2:
                    if BY_DVE[j - 2]:
                        pe.wait_ge(p_dve, taken(j - 2))
                    else:
                        pe.wait_ge(p_act, taken(j - 2))
                if kind not in OF_TILES + OF_ITEMS:
                    for name in item_of(job):
                        arrived(name)
                if kind == "vec":
                    pe.wait_ge(const_in, 16)
                    pe.wait_ge(vec_in, 16 * 10)
                    mm = pe.transpose(dst[:, 0:41], vec_rows[0:41, :], ident[0:41, 0:41])
                elif kind == "xt":
                    pe.wait_ge(x_in, 16)
                    pe.wait_ge(const_in, 16)
                    mm = turn4(dst, x4, job[1])
                elif kind == "bias":
                    pe.wait_ge(table_in, 48)
                    pe.wait_ge(setup, 2)
                    mm = pe.matmul(dst[0:BIAS_HEADS, 0:VALS + 1], rel_sb, bucket_sb, start=True, stop=True)
                elif kind == "cnat":
                    from_act(("xt", 3))
                    tt = job[1]
                    natural(dst[:, 0:Q_LORA], xT3, tt, slot("c_q"), 0, 256)
                    mm = natural(dst[:, Q_LORA:C_COLS], xT3, tt, slot("c_kv"), 0, C_COLS - Q_LORA)
                elif kind == "tile1":
                    mm = turned_product(dst, job, 0)
                elif kind == "avn":
                    from_act(("tile1", 3))
                    for tt in range(2):
                        mm = pe.transpose(dst[:, P * tt:P * tt + P], tile3[:, 3, P * tt:P * tt + P], ident)
                elif kind == "ct":
                    pe.wait_ge(c_scaled, 1)
                    for c in range(2):
                        for tt in range(2):
                            mm = pe.transpose(dst[:, c * T + tt * P:c * T + tt * P + P],
                                              c_nat[:, tt, P * c:P * c + P], ident)
                elif kind == "ckt":
                    pe.wait_ge(kc_roped, 1)
                    for tt in range(2):
                        pe.transpose(dst[:, P * tt:P * tt + P], c_nat[:, tt, Q_LORA:Q_LORA + KV_LORA], ident)
                    for tt in range(2):
                        mm = pe.transpose(dst[0:C_ROPE, T + P * tt:T + P * tt + P],
                                          c_nat[:, tt, Q_LORA + KV_LORA:C_COLS], ident)
                elif kind == "cq":
                    from_act(("ct",))
                    tt, half = job[1:]
                    pe.wait_ge(latent_in, 32)
                    for k in range(2):
                        mm = pe.matmul(dst[:, 0:384], c_qT[:, k, P * tt:P * tt + P],
                                       w_uq[:, k, 384 * half:384 * half + 384], start=(k == 0), stop=(k == 1))
                elif kind == "ck":
                    from_act(("ckt",))
                    pe.wait_ge(latent_in, 32)
                    for m in range(2):
                        h = 2 * job[1] + m
                        mm = pe.matmul(dst[0:C_NOPE, T * m:T * m + T], w_ukv[:, P * h:P * h + C_NOPE], c_kvT,
                                       start=True, stop=True)
                elif kind == "cv":
                    from_act(("ckt",))
                    tt = job[1]
                    w = w_ukv.rearrange("p (h n) -> p h n", h=C_HEADS)[:, :, C_NOPE:P]
                    mm = pe.matmul(dst, c_kvT[:, P * tt:P * tt + P], w, start=True, stop=True)
                elif kind == "cqt":
                    pe.wait_ge(qc_roped, 1)
                    for m in range(2):
                        h = 2 * job[1] + m
                        for tt in range(2):
                            mm = pe.transpose(dst[0:C_QK, T * m + P * tt:T * m + P * tt + P],
                                              qc_nat[:, tt, C_QK * h:C_QK * h + C_QK], ident)
                elif kind == "bv":
                    mm = natural_product(dst, job, x_low3, range(KC), {})
                elif kind == "y1":
                    mm = output_product(dst, job, 0)
                elif kind == "mt":
                    pe.wait_ge(mem_scaled, 2)
                    mm = turn4(dst, mem4, job[1])
                elif kind == "mk":
                    l, n = job[1:]
                    from_act(("mt", 3))
                    w = slot(f"mem_k{l}")
                    for k in range(KC):
                        mm = pe.matmul(dst[:, 0:T], w[:, k, P * n:P * n + P], memT[l][:, k, :],
                                       start=(k == 0), stop=(k == KC - 1))
                elif kind == "mv":
                    l, tt = job[1:]
                    mm = natural(dst[:, 0:256], memT[l], tt, slot(f"mem_v{l}"), 0, 256)
                elif kind == "x1t":
                    pe.wait_ge(ln_done, 2)
                    mm = turn4(dst, x4, job[1])
                elif kind == "logit":
                    from_act(("x1t", 3))
                    pe.wait_ge(router_in, 16 * (1 + GROUPS))
                    for k in range(KC):
                        mm = pe.matmul(dst[0:GROUPS + EXPERTS, 0:T], router[:, k, :], xT3[:, k, :],
                                       start=(k == 0), stop=(k == KC - 1))
                elif kind == "logitT":
                    from_dve(("logit",))
                    n = GROUPS + EXPERTS
                    for tt in range(2):
                        mm = pe.transpose(dst[:, n * tt:n * tt + n], logitT_sb[0:n, P * tt:P * tt + P],
                                          ident[0:n, 0:n])
                elif kind == "rank":
                    pe.wait_ge(chosen_done, 1)
                    e = EXPERTS
                    pe.matmul(dst[:, 0:e], before, chosen3[:, 0, :], start=True, stop=True)
                    pe.matmul(dst[:, e:2 * e], before, chosen3[:, 1, :], start=True, stop=False)
                    pe.matmul(dst[:, e:2 * e], ones, chosen3[:, 0, :], start=False, stop=True)
                    pe.matmul(dst[:, 2 * e:3 * e], ones, chosen3[:, 0, :], start=True, stop=False)
                    mm = pe.matmul(dst[:, 2 * e:3 * e], ones, chosen3[:, 1, :], start=False, stop=True)
                elif kind == "xt2":
                    l, tt, half = job[1:]
                    pe.wait_ge(x_scaled, 2 * l + tt + 1)
                    for c in range(4):
                        mm = pe.transpose(dst[:, P * c:P * c + P], xn4[:, tt, 4 * half + c, :], ident)
                elif kind == "tile2":
                    mm = turned_product(dst, job, job[1] + 1)
                elif kind == "vn":
                    l, n = job[1:]
                    from_act(("tile2", l, n))
                    for tt in range(2):
                        mm = pe.transpose(dst[:, P * tt:P * tt + P], tile3[:, n, P * tt:P * tt + P], ident)
                elif kind == "swap":
                    l, n = job[1:]
                    from_act(("tile2", l, n))
                    mm = pe.matmul(dst[:, 0:T], swap, tile3[:, n, :], start=True, stop=True)
                elif kind == "hsq":
                    pe.wait_ge(squared, hsq_nth(*job[1:]))
                    mm = pe.matmul(dst[:, 0:T], headsum, sq_tile(job[2]), start=True, stop=True)
                elif kind == "hso":
                    l, n = job[1:]
                    pe.wait_ge(o_squared, 3 * l + n + 1)
                    mm = pe.matmul(dst[:, 0:T], headsum, sq_tile(n), start=True, stop=True)
                elif kind == "y2":
                    mm = output_product(dst, job, job[1] + 1)
                mm.then_inc(p_ready, 1)

            def s_bank(n):
                if n >= 3:
                    owner = S_OWNER[n - 3]
                    if STEPS[owner][0] in "AB":
                        pe.wait_ge(maxed, owner + 1)
                    else:
                        pe.wait_ge(exped, owner + 1)
                return bank(n % 3)

            def run_scores(step):
                kind, l, h = STEPS[step]
                n = s_first(step)
                if kind == "A":
                    for tile in (h % 2, 2):
                        from_act(("tile1", tile))
                    base = HD * (h // 2)
                    q, k = tile3[base:base + HD, h % 2, :], tile3[base:base + HD, 2, :]
                    s = s_bank(n)
                    pe.matmul(s[:, 0:P], q[:, 0:P], k[:, 0:P], start=True, stop=True)
                    pe.matmul(s[:, P:3 * P], q[:, P:T], k[:, 0:T], start=True, stop=True).then_inc(scores, 1)
                elif kind == "C":
                    from_act(("cqt", 3))
                    pe.wait_ge(setup, 2)
                    q, k = qc3[0:C_QK, h, :], kc3[0:C_QK, h, :]
                    s = s_bank(n)
                    pe.matmul(s[:, 0:P], q[:, 0:P], k[:, 0:P], start=True, stop=False)
                    pe.matmul(s[:, 0:P], ident_b[:, :], causal_b[:, :], start=False, stop=True)
                    pe.matmul(s[:, P:3 * P], q[:, P:T], k[:, 0:T], start=True, stop=False)
                    pe.matmul(s[:, 2 * P:3 * P], ident_b[:, :], causal_b[:, :], start=False, stop=True
                              ).then_inc(scores, 1)
                elif kind == "B":
                    for g in range(B_GROUPS):
                        from_act(("tile1", 10 + 2 * g + 1))
                    base = HD * (h % 2)

                    def qk(g):
                        return (tile3[base:base + HD, 4 + 2 * g + h // 2, :],
                                tile3[base:base + HD, 10 + 2 * g + h // 2, :])

                    s = s_bank(n)
                    for g in range(B_GROUPS):
                        q, k = qk(g)
                        mm = pe.matmul(s[:, P * g:P * g + P], q[:, 0:P], k[:, 0:P], start=True, stop=True)
                    mm.then_inc(scores, 1)
                    s = s_bank(n + 1)
                    for g in range(2):
                        q, k = qk(g)
                        mm = pe.matmul(s[:, T * g:T * g + T], q[:, P:T], k[:, 0:T], start=True, stop=True)
                    mm.then_inc(scores, 1)
                    s = s_bank(n + 2)
                    q, k = qk(2)
                    pe.matmul(s[:, 0:T], q[:, P:T], k[:, 0:T], start=True, stop=True).then_inc(scores, 1)
                elif kind == "D":
                    pe.wait_ge(roped, max(rope_nth(l, h // 2), rope_nth(l, 3 + h // 2)))
                    banks = [s_bank(n), s_bank(n + 1)]
                    for tt in range(2):
                        for m in range(2):
                            base = HD * (h % 2) + 32 * m
                            q, k = tile3[base:base + 32, h // 2, :], tile3[base:base + 32, 3 + h // 2, :]
                            mm = pe.matmul(banks[m][:, T * tt:T * tt + T], q[:, P * tt:P * tt + P], k,
                                           start=True, stop=True)
                            if tt == 1:
                                mm.then_inc(scores, 1)
                else:
                    base = HD * (h % 2)
                    if kind == "G":
                        pe.wait_ge(k_copied, l + 1)
                        q = tile3[base:base + HD, 12 + h // 2, :]
                        same = base == HD * (h // 3)
                        k = tile3[base:base + HD, 15 if same else 16, :]
                    else:
                        from_act(("tile2", l, 20 + h // 2))
                        q = tile3[base:base + HD, 20 + h // 2, :]
                        k = mem_k[base:base + HD, l, h // 2, :]
                    s = s_bank(n)
                    for tt in range(2):
                        mm = pe.matmul(s[:, T * tt:T * tt + T], q[:, P * tt:P * tt + P], k, start=True, stop=True)
                    mm.then_inc(scores, 1)

            def run_turn(step):
                kind, l, h = STEPS[step]
                pe.wait_ge(normed, step + 1)
                pr = probs[:, 1152 * (step % 2):1152 * (step % 2) + 1152]
                for m in range(T_JOBS[kind]):
                    n = t_first(step) + m
                    if n >= 2:
                        pe.wait_ge(turned_out, n - 1)
                    dst = bank(3 + n % 2)
                    if kind in "AC":
                        at = [0, P, 2 * P]
                    elif kind == "B":
                        at = [P * m, 3 * P + T * m, 3 * P + T * m + P]
                    else:
                        at = [0, T, P, T + P]
                    for c, a in enumerate(at):
                        mm = pe.transpose(dst[:, P * c:P * c + P], pr[:, a:a + P], ident)
                    mm.then_inc(turned, 1)

            def run_out(step):
                kind, l, h = STEPS[step]
                par = h % 2
                if step >= 2:
                    pe.wait_ge(o_out, step - 1)
                o = bank(5)[HD * par:HD * par + HD, T * (step % 2):T * (step % 2) + T]
                if kind == "B":
                    from_act(("bv", B_GROUPS - 1, 1))
                elif kind == "A":
                    from_act(("avn",))
                elif kind == "C":
                    from_act(("cv", 1))
                elif kind == "D":
                    from_act(("vn", l, 6 + h // 2))
                elif kind == "G":
                    from_act(("vn", l, 16))
                for m in range(T_JOBS[kind]):
                    n = t_first(step) + m
                    pe.wait_ge(turned_out, n + 1)
                    pt = probsT[:, 512 * (n % 4):512 * (n % 4) + 512]
                    if kind == "A":
                        v = [va[:, tt, HD * (h // 2):HD * (h // 2) + HD] for tt in range(2)]
                    elif kind == "B":
                        v = [vb[:, tt, m, HD * h:HD * h + HD] for tt in range(2)]
                    elif kind == "C":
                        v = [vc3[:, tt, HD * h:HD * h + HD] for tt in range(2)]
                    elif kind == "D":
                        v = [v2[:, tt, h // 2, HD * par:HD * par + HD] for tt in range(2)]
                    elif kind == "G":
                        v = [v2[:, tt, 3, HD * (h // 3):HD * (h // 3) + HD] for tt in range(2)]
                    else:
                        v = [mem_v[:, l, tt, HD * h:HD * h + HD] for tt in range(2)]
                    last = m == T_JOBS[kind] - 1
                    pe.matmul(o, v[0], pt[:, 0:T], start=(m == 0), stop=False)
                    if kind in "ABC":
                        mm = pe.matmul(o[:, P:T], v[1], pt[:, T:T + P], start=False, stop=last)
                    else:
                        mm = pe.matmul(o, v[1], pt[:, T:2 * T], start=False, stop=last)
                mm.then_inc(o_ready, 1)

            def bunch(i, more, n):
                pe.wait_ge(placed, i + 1)
                for half in range(2):
                    dst = bank(4 + half)
                    for c in range(4):
                        k = 4 * half + c
                        for tt in range(2):
                            mm = pe.matmul(dst[:, P * c:P * c + P],
                                           x2[:, tt, :].rearrange("p (q k) -> p k q", k=KC)[:, k, :],
                                           places2[:, tt, :], start=(tt == 0), stop=(tt == 1))
                    mm.then_inc(gathered_ready, 1)
                for tt in range(2):
                    mm = pe.transpose(bank(7)[:, P * tt:P * tt + P], weighed2[:, tt, :], ident)
                mm.then_inc(back_ready, 1)
                pe.wait_ge(gathered_out, 2 * i + 2)
                if not more:
                    for k in range(2 * AT_ONCE):
                        pe.wait_ge(loaded[k], loaded_at(k, i))
                    for k in range(KC):
                        for e in range(AT_ONCE):
                            w = slots[:, 2 * e:2 * e + 2, k, :]
                            mm = pe.matmul(bank(6)[PLACES * e:PLACES * e + PLACES, :],
                                           gathered[:, k, PLACES * e:PLACES * e + PLACES], w,
                                           start=(k == 0), stop=(k == KC - 1))
                else:
                    for e in range(AT_ONCE):
                        pe.wait_ge(more_in, n * (32 * AT_ONCE) + 32 * (e + 1))
                        for m, w in enumerate((more_g, more_u)):
                            for k in range(KC):
                                mm = pe.matmul(bank(6)[PLACES * e:PLACES * e + PLACES, DE * m:DE * m + DE],
                                               gathered[:, k, PLACES * e:PLACES * e + PLACES],
                                               w[:, DE * k:DE * k + DE], start=(k == 0), stop=(k == KC - 1))
                        if e < AT_ONCE - 1:
                            mm.then_inc(more_used, 1)
                mm.then_inc(gu_ready, 1)
                pe.wait_ge(hidden_done, i + 1)
                for k in range(2):
                    mm = pe.transpose(bank(4)[:, P * k:P * k + P],
                                      hidden.rearrange("p (q k) -> p k q", k=2)[:, k, :], ident)
                mm.then_inc(hT_ready, 1)
                pe.wait_ge(hT_out, i + 1)
                pe.wait_ge(back_out, i + 1)
                if not more:
                    for k in range(AT_ONCE):
                        pe.wait_ge(loaded[2 * AT_ONCE + k], loaded_at(2 * AT_ONCE + k, i))
                    for half in range(2):
                        for k in range(2):
                            for e in range(AT_ONCE):
                                a = (2 * AT_ONCE + e) * SLOT + D * k + 512 * half
                                mm = pe.matmul(bank((7, 5)[half])[PLACES * e:PLACES * e + PLACES, :],
                                               hiddenT[:, k, PLACES * e:PLACES * e + PLACES], ring[:, a:a + 512],
                                               start=(k == 0), stop=(k == 1))
                        mm.then_inc(y_ready, 1)
                else:
                    for e in range(AT_ONCE):
                        pe.wait_ge(more_down_in, n * (16 * AT_ONCE) + 16 * (e + 1))
                        for half in range(2):
                            for k in range(2):
                                a = D * k + 512 * half
                                mm = pe.matmul(bank((7, 5)[half])[PLACES * e:PLACES * e + PLACES, :],
                                               hiddenT[:, k, PLACES * e:PLACES * e + PLACES], more_d[:, a:a + 512],
                                               start=(k == 0), stop=(k == 1))
                            if e == AT_ONCE - 1:
                                mm.then_inc(y_ready, 1)
                        if e < AT_ONCE - 1:
                            mm.then_inc(more_used, 1)
                pe.wait_ge(y0_out, i + 1)
                pe.wait_ge(y1_out, i + 1)
                for tt in range(2):
                    for half in range(2):
                        mm = pe.matmul(bank(2 * tt + half), back[:, P * tt:P * tt + P],
                                       y_e[:, 512 * half:512 * half + 512], start=False, stop=False,
                                       skip_group_check=True)
                mm.then_inc(summed, 1)

            def loaded_at(k, i):
                return all_loaded(FIRST_EXPERT + k) + i * 16

            def experts():
                pe.wait_ge(p_act, taken(JOB[("mv", 1, 1)]))
                pe.wait_ge(p_dve, taken(JOB[("rank",)]))
                pe.wait_ge(setup, 2)
                for b in range(4):
                    pe.matmul(bank(b), zeros_b[:, 0:P], zeros_b[:, :], start=True, stop=False, skip_group_check=True)
                bunch(0, False, None)
                with pe.Fori(1, BUNCHES) as i:
                    bunch(i, False, None)
                pe.wait_ge(routed, 1)
                some = pe.value_load(flags[0:1, 112:113], min_val=0, max_val=1)
                with pe.If(some):
                    with pe.Fori(0, ROUNDS - 1) as r:
                        with pe.Fori(0, BUNCHES) as g:
                            flag = pe.value_load(flags[0:1, bass.ds(r * BUNCHES + g, 1)], min_val=0, max_val=1)
                            with pe.If(flag):
                                n = pe.value_load(flags[0:1, bass.ds(r * BUNCHES + g + 56, 1)], min_val=0, max_val=55)
                                bunch(n + BUNCHES, True, n)
                for b in range(4):
                    mm = pe.matmul(bank(b), zeros_b[:, 0:P], zeros_b[:, :], start=False, stop=True, skip_group_check=True)
                    if b % 2 == 1:
                        mm.then_inc(moe_done, 1)

            j = step = drained = 0
            for jobs, what in TURNS:
                if what in STEP:
                    step = STEP[what]
                    run_scores(step)
                    if not opens(step) and not opens(step - 1):
                        run_out(step - 2)
                    drained = 0
                for job in jobs:
                    run(job, j)
                    j += 1
                if what == "experts":
                    experts()
                elif what is not None:
                    if not opens(step):
                        run_turn(step - 1)
                elif jobs == []:
                    if drained == 0:
                        run_out(step - 1)
                        run_turn(step)
                    else:
                        run_out(step)
                    drained += 1

        @block.scalar
        def _(act):
            chain = [0]

            def link(ins_):
                chain[0] += 1
                ins_.then_inc(act_chain, 1)
                act.wait_ge(act_chain, chain[0])

            act.preload_act_table_set("natural_log_exp_and_others")
            act.dma_start(bucket_sb[:, 0:VALS], ins["const_bucket"]).then_inc(table_in, 16)
            act.dma_start(rel_sb, ins["rel_bias"]).then_inc(table_in, 16)
            act.dma_start(unseen_sb, ins["const_unseen"]).then_inc(table_in, 16)

            def take(job, j):
                kind = job[0]
                src = bank(6 + j % 2)
                act.wait_ge(p_ready, j + 1)
                if kind == "vec":
                    op = act.activation(vecs[:, :], src[:, 0:41], ACT.Copy)
                elif kind in ("xt", "x1t"):
                    k = job[1]
                    op = act.activation(xT3[:, 2 * k:2 * k + 2, :], src.rearrange("p (c t) -> p c t", c=2), ACT.Copy)
                elif kind == "cnat":
                    op = act.activation(c_nat[:, job[1], :], src[:, 0:C_COLS], ACT.Copy)
                elif kind == "tile1":
                    n = job[1]
                    q = n < 2 or 4 <= n < 10
                    op = act.activation(tile3[:, n, :], src[:, 0:T], ACT.Copy, scale=(HD ** -0.5 if q else 1.0))
                elif kind == "avn":
                    op = act.activation(va, src[:, 0:256].rearrange("p (t n) -> p t n", t=2), ACT.Copy)
                elif kind == "ct":
                    for c in range(2):
                        op = act.activation(c_qT[:, c, :], src[:, T * c:T * c + T], ACT.Copy,
                                            scale=vecs[:, 32 + c:33 + c])
                elif kind == "ckt":
                    act.activation(c_kvT, src[:, 0:T], ACT.Copy, scale=vecs[:, 34:35])
                    op = act.activation(kc3[C_NOPE:C_QK, :, :],
                                        src[0:C_ROPE, T:2 * T].unsqueeze(1).to_broadcast([C_ROPE, C_HEADS, T]),
                                        ACT.Copy)
                elif kind == "cq":
                    tt, half = job[1:]
                    op = act.activation(qc_nat[:, tt, 384 * half:384 * half + 384], src[:, 0:384], ACT.Copy)
                elif kind == "ck":
                    k = job[1]
                    op = act.activation(kc3[0:C_NOPE, 2 * k:2 * k + 2, :],
                                        src[0:C_NOPE, :].rearrange("p (c t) -> p c t", c=2), ACT.Copy)
                elif kind == "cv":
                    op = act.activation(vc3[:, job[1], :], src, ACT.Copy)
                elif kind == "cqt":
                    k = job[1]
                    op = act.activation(qc3[0:C_QK, 2 * k:2 * k + 2, :],
                                        src[0:C_QK, :].rearrange("p (c t) -> p c t", c=2), ACT.Copy)
                elif kind == "bv":
                    g, tt = job[1:]
                    op = act.activation(vb[:, tt, g, :], src[:, 0:256], ACT.Copy)
                elif kind == "mt":
                    k = job[1]
                    for l in range(LAYERS):
                        for c in range(2):
                            at = 16 + 8 * l + 2 * k + c
                            op = act.activation(memT[l][:, 2 * k + c, :], src[:, T * c:T * c + T], ACT.Copy,
                                                scale=vecs[:, at:at + 1])
                elif kind == "mk":
                    l, n = job[1:]
                    op = act.activation(mem_k[:, l, n, :], src[:, 0:T], ACT.Copy)
                elif kind == "mv":
                    l, tt = job[1:]
                    op = act.activation(mem_v[:, l, tt, :], src[:, 0:256], ACT.Copy)
                elif kind == "tile2":
                    l, n = job[1:]
                    if 12 <= n <= 15:
                        act.activation(sq_tile(n), src[:, 0:T], ACT.Square).then_inc(squared, 1)
                        at = (37 if n < 15 else 39) + l
                        op = act.activation(tile3[:, n, :], src[:, 0:T], ACT.Copy, scale=vecs[:, at:at + 1])
                    elif n in GATE_TILES:
                        act.activation(exp_tile(n), src[:, 0:T], ACT.Exp, scale=-1.0)
                        op = act.activation(tile3[:, n, :], src[:, 0:T], ACT.Copy)
                    else:
                        op = act.activation(tile3[:, n, :], src[:, 0:T], ACT.Copy)
                elif kind == "vn":
                    l, n = job[1:]
                    op = act.activation(v2[:, :, V_TILES.index(n), :], src[:, 0:256].rearrange("p (t n) -> p t n", t=2),
                                        ACT.Copy)
                elif kind in ("hsq", "hso"):
                    dst = sq_tile(job[2])
                    link(act.activation(dst, src[:, 0:T], ACT.Ln, scale=1.0 / HD, bias=eps6))
                    op = act.activation(dst, dst, ACT.Exp, scale=-0.5)
                elif kind == "y2":
                    l, s, tt = job[1:]
                    act.activation(xn2[:, tt, 256 * s:256 * s + 256], src[:, 0:256], ACT.Square,
                                   accum_out=y_sq[:, 4 * tt + s:4 * tt + s + 1])
                    op = act.activation(y_nat[:, tt, 256 * s:256 * s + 256], src[:, 0:256], ACT.Copy)
                op.then_inc(p_act, 1)

            def gate_sigmoid(l, n):
                e = exp_tile(n)
                act.wait_ge(p_act, taken(JOB[("tile2", l, n)]))
                link(act.activation(e, e, ACT.Ln, bias=1.0))
                act.activation(e, e, ACT.Exp, scale=-1.0).then_inc(sigmoid, 1)

            def exps(step):
                kind, l, h = STEPS[step]
                act.wait_ge(maxed, step + 1)
                pr = probs[:, 1152 * (step % 2):1152 * (step % 2) + 1152]
                par = step % 2
                n_, s_ = nm[:, 4 * par:4 * par + 4], sm[:, 4 * par:4 * par + 4]
                if step >= 2:
                    act.wait_ge(turned, t_first(step - 1))
                b0 = s_first(step)
                if kind == "A":
                    act.activation(sink_e[:, 2 * par:2 * par + 2], n_[:, 0:2], ACT.Exp, bias=sink[:, h:h + 1])
                    act.activation(pr[:, 0:P], pr[:, 0:P], ACT.Exp, bias=n_[:, 0:1], accum_out=s_[:, 0:1])
                    op = act.activation(pr[:, P:3 * P], pr[:, P:3 * P], ACT.Exp, bias=n_[:, 1:2],
                                        accum_out=s_[:, 1:2])
                elif kind == "B":
                    act.activation(pr[:, 0:384], pr[:, 0:384], ACT.Exp, bias=n_[:, 0:1], accum_out=s_[:, 0:1])
                    op = act.activation(pr[:, 384:1152], pr[:, 384:1152], ACT.Exp, bias=n_[:, 1:2],
                                        accum_out=s_[:, 1:2])
                elif kind == "C":
                    s = bank(b0 % 3)
                    sc = C_QK ** -0.5
                    act.activation(pr[:, 0:P], s[:, 0:P], ACT.Exp, bias=n_[:, 0:1], scale=sc, accum_out=s_[:, 0:1])
                    op = act.activation(pr[:, P:3 * P], s[:, P:3 * P], ACT.Exp, bias=n_[:, 1:2], scale=sc,
                                        accum_out=s_[:, 1:2])
                elif kind == "D":
                    for m in range(2):
                        for tt in range(2):
                            c = 2 * m + tt
                            op = act.activation(pr[:, T * c:T * c + T], bank((b0 + m) % 3)[:, T * tt:T * tt + T],
                                                ACT.Exp, bias=n_[:, c:c + 1], scale=32 ** -0.5,
                                                accum_out=s_[:, c:c + 1])
                else:
                    s = bank(b0 % 3)
                    for tt in range(2):
                        op = act.activation(pr[:, T * tt:T * tt + T], s[:, T * tt:T * tt + T], ACT.Exp,
                                            bias=n_[:, tt:tt + 1], scale=HD ** -0.5, accum_out=s_[:, tt:tt + 1])
                op.then_inc(exped, 1)

            def outs(step):
                h = STEPS[step][2]
                rows = slice(HD * (h % 2), HD * (h % 2) + HD)
                act.wait_ge(o_out, step)
                act.wait_ge(o_ready, step + 1)
                act.activation(mix3[rows, h // 2, :], bank(5)[rows, T * (step % 2):T * (step % 2) + T], ACT.Copy
                               ).then_inc(o_out, 1)

            def take_turned(step):
                kind = STEPS[step][0]
                w = 3 * P if kind in "ABC" else 4 * P
                for m in range(T_JOBS[kind]):
                    n = t_first(step) + m
                    if n >= 4:
                        owner = max(s for s in range(len(STEPS)) if t_first(s) <= n - 4)
                        act.wait_ge(o_ready, owner + 1)
                    act.wait_ge(turned, n + 1)
                    act.activation(probsT[:, 512 * (n % 4):512 * (n % 4) + w], bank(3 + n % 2)[:, 0:w], ACT.Copy
                                   ).then_inc(turned_out, 1)

            def inverse_root(dst, src, scale=1.0, bias=0.0):
                link(act.activation(dst, src, ACT.Ln, scale=scale, bias=bias))
                return act.activation(dst, dst, ACT.Exp, scale=-0.5)

            def layer_stats(n, tt):
                act.wait_ge(ln_var, 2 * n + tt + 1)
                inverse_root(ln_rs[:, tt:tt + 1], mv3[:, tt, 1:2], bias=eps5).then_inc(ln_rstd, 1)

            def start_layer(l, tt):
                if l == 0:
                    act.wait_ge(ln_done, 2 + tt + 1)
                else:
                    act.wait_ge(x_done, 2 * (l - 1) + tt + 1)
                link(act.activation(xn2[:, tt, :], x2[:, tt, :], ACT.Square, accum_out=x_sq[:, tt:tt + 1]))
                inverse_root(x_rs[:, tt:tt + 1], x_sq[:, tt:tt + 1], 1.0 / D, eps6).then_inc(x_rstd, 1)

            def high(n):
                item = item_split(n)
                act.wait_ge(loaded[slot_of(item)], all_loaded(item))
                if freed_by(n) >= 0:
                    act.wait_ge(p_ready, freed_by(n) + 1)
                act.activation(split_of(n)[0], raw_of(n), ACT.Copy).then_inc(highs, 1)

            def x_high(phase, part):
                if phase == 0:
                    act.wait_ge(p_act, taken(JOB[("xt", 3)]))
                else:
                    act.wait_ge(p_dve, taken(JOB[("xt2", phase - 1, part // 2, part % 2)]))
                own = X_PARTS[phase][part]
                act.activation(a_high3[own], xT3[own], ACT.Copy).then_inc(x_highs, 1)

            def mix_high(phase, part):
                if part == 0:
                    act.wait_ge(p_ready, max(users(SPLIT[("y1", 0) if phase == 0 else ("y2", phase - 1, 0)] - 1)) + 1)
                    if phase:
                        act.wait_ge(gated, D_HEADS // 2 * phase)
                act.wait_ge(o_out, STEP[MIX_LAST[phase][part]] + 1)
                own = slice(*MIX_PARTS[phase][part])
                act.activation(a_high3[:, own, :], mix3[:, own, :], ACT.Copy).then_inc(mix_highs, 1)

            def memory():
                act.wait_ge(mem_sum, 1)
                link(inverse_root(mem_rs, mem_sq))
                for tt in range(2):
                    act.activation(mem_nat[:, tt, :], mem_nat[:, tt, :], ACT.Copy, scale=mem_rs[:, tt:tt + 1]
                                   ).then_inc(mem_scaled, 1)

            def bunch(i):
                for half in range(2):
                    act.wait_ge(gathered_ready, 2 * i + half + 1)
                    act.activation(gathered[:, 4 * half:4 * half + 4, :],
                                   bank(4 + half).rearrange("p (k s) -> p k s", k=4), ACT.Copy
                                   ).then_inc(gathered_out, 1)
                act.wait_ge(gu_ready, i + 1)
                act.activation(gate_e, bank(6)[:, 0:DE], ACT.Exp, scale=-1.0).then_inc(gate_exped, 1)
                act.wait_ge(hT_ready, i + 1)
                act.activation(hiddenT, bank(4)[:, 0:256].rearrange("p (k s) -> p k s", k=2), ACT.Copy
                               ).then_inc(hT_out, 1)
                act.wait_ge(y_ready, 2 * i + 1)
                if not isinstance(i, int):
                    act.wait_ge(summed, i)
                act.activation(y_e[:, 0:512], bank(7), ACT.Copy).then_inc(y0_out, 1)

            def experts():
                bunch(0)
                with act.Fori(1, BUNCHES) as i:
                    bunch(i)
                act.wait_ge(routed, 1)
                some = act.value_load(flags[0:1, 112:113], min_val=0, max_val=1)
                with act.If(some):
                    with act.Fori(0, ROUNDS - 1) as r:
                        with act.Fori(0, BUNCHES) as g:
                            flag = act.value_load(flags[0:1, bass.ds(r * BUNCHES + g, 1)], min_val=0, max_val=1)
                            with act.If(flag):
                                n = act.value_load(flags[0:1, bass.ds(r * BUNCHES + g + 56, 1)], min_val=0, max_val=55)
                                bunch(n + BUNCHES)
                for n in AT_EXPERTS:
                    high(n)
                for tt in range(2):
                    layer_stats(1, tt)

            j = step = drained = 0
            gates_due = []
            for jobs, what in TURNS:
                if what in STEP:
                    step = STEP[what]
                    if not opens(step) and not opens(step - 1) and STEPS[step - 2][0] == "D":
                        outs(step - 2)
                    exps(step)
                    if what == ("C", 0, 0):
                        memory()
                    if what == ("B", 0, 2):
                        mix_high(0, 0)
                    drained = 0
                for job in jobs:
                    for n in SPLIT_AT.get(j, ()):
                        high(n)
                    if job == ("xt2", 0, 0, 0):
                        for tt in range(2):
                            start_layer(0, tt)
                    if job == ("xt2", 1, 1, 0):
                        start_layer(1, 1)
                    if job[0] == "xt2":
                        x_high(job[1] + 1, 2 * job[2] + job[3])
                    if job == ("tile1", 0):
                        act.wait_ge(c_sums, 1)
                        inverse_root(c_rs, c_sq).then_inc(c_rstd, 1)
                    if not BY_DVE[j]:
                        take(job, j)
                        if job == ("xt", 3):
                            for half in range(2):
                                x_high(0, half)
                        if job[0] == "y2" and job[2] == 3:
                            l, tt = job[1], job[3]
                            act.wait_ge(y_sum, 2 * l + tt + 1)
                            inverse_root(y_rs[:, tt:tt + 1], y_ms[:, tt:tt + 1], 1.0 / D, eps6).then_inc(y_rstd, 1)
                        if job == ("y2", 0, 2, 1):
                            start_layer(1, 0)
                        if job == ("tile2", 0, 3):
                            act.wait_ge(lam_sum, 1)
                            act.activation(lam_e, lam_s, ACT.Exp).then_inc(lam_exp, 1)
                    elif job[:2] == ("y1", 3):
                        layer_stats(0, job[2])
                    elif job[0] == "logitT":
                        act.wait_ge(route_dif, 1)
                        act.activation(g_exp, g_dif, ACT.Exp).then_inc(route_exp, 1)
                        act.wait_ge(route_m, 1)
                        act.activation(e_x, e_t, ACT.Exp).then_inc(route_x, 1)
                    if job[0] == "tile2" and job[2] in GATE_TILES:
                        gates_due.append(job[1:])
                    j += 1
                if what == "experts":
                    experts()
                elif what is not None:
                    if not opens(step):
                        take_turned(step - 1)
                    for due in gates_due:
                        gate_sigmoid(*due)
                    gates_due = []
                    if what[0] in "DG" and STEP[what] - STEP[("D", what[1], 0)] in (4, 6, 8):
                        n = (STEP[what] - STEP[("D", what[1], 0)]) // 2 - 2
                        act.wait_ge(o_out, step - 2)
                        act.activation(sq_tile(n), mix3[:, n, :], ACT.Square).then_inc(o_squared, 1)
                elif jobs == []:
                    if drained == 0:
                        if STEPS[step][0] == "M":
                            mix_high(STEPS[step][1] + 1, 0)
                        else:
                            mix_high(0, 1)
                        take_turned(step)
                    elif STEPS[step][0] == "M":
                        mix_high(STEPS[step][1] + 1, 1)
                    else:
                        mix_high(0, 2)
                    drained += 1

        @block.vector
        def _(dve):
            chain = [0]

            def link(ins_):
                chain[0] += 1
                ins_.then_inc(dve_chain, 1)
                dve.wait_ge(dve_chain, chain[0])

            def rope4(dst1, dst2, cos, sin, t, last=None):
                t1, t2, t3, t4 = t
                dve.tensor_tensor(t1, dst1, cos, ALU.mult)
                dve.tensor_tensor(t2, dst2, sin, ALU.mult)
                dve.tensor_tensor(t3, dst1, sin, ALU.mult)
                link(dve.tensor_tensor(t4, dst2, cos, ALU.mult))
                link(dve.tensor_tensor(dst1, t1, t2, ALU.subtract))
                return dve.tensor_tensor(dst2, t3, t4, ALU.add)

            dve.memset(eps6, 1e-6)
            dve.memset(eps5, 1e-5)
            dve.memset(bucket_sb[:, VALS:VALS + 1], 0.0)
            dve.memset(zeros_b[:, :], 0.0).then_inc(setup, 1)
            dve.wait_ge(const_in, 16)
            dve.tensor_copy(ident_b[:, :], ident)
            dve.tensor_copy(causal_b[:, :], c_("causal")).then_inc(setup, 1)
            def rms(dst, src, n, junk, eps):
                link(dve.tensor_tensor_reduce(out=junk, in0=src, in1=src, scale=1.0, scalar=0.0,
                                              op0=ALU.mult, op1=ALU.add, accum_out=dst))
                return dve.tensor_scalar(dst, dst, 1.0 / n, eps, ALU.mult, ALU.add)

            def lambda_sums():
                dve.wait_ge(small_in, 64)
                lp = lam_p.rearrange("p (l a b d) -> p l a b d", l=2, a=2, b=2)
                for l in range(LAYERS):
                    link(dve.tensor_tensor(lp[:, l, :, 0, :], lp[:, l, :, 0, :], lp[:, l, :, 1, :], ALU.mult))
                for l in range(LAYERS):
                    op = dve.tensor_reduce(lam_s[:, 2 * l:2 * l + 2], lp[:, l, :, 0, :], X, ALU.add)
                op.then_inc(lam_sum, 1)

            def latent_sums():
                dve.wait_ge(p_act, taken(JOB[("cnat", 1)]))
                for tt in range(2):
                    link(rms(c_sq[:, tt:tt + 1], c_nat[:, tt, 0:Q_LORA], Q_LORA, rope_t[:, 0:Q_LORA], 1e-6))
                    op = rms(c_sq[:, 2 + tt:3 + tt], c_nat[:, tt, Q_LORA:Q_LORA + KV_LORA], KV_LORA,
                             rope_t[:, 256:256 + KV_LORA], 1e-6)
                    if tt == 0:
                        link(op)
                op.then_inc(c_sums, 1)

            def latent_norm():
                dve.wait_ge(c_rstd, 1)
                for tt in range(2):
                    op = dve.tensor_scalar(c_nat[:, tt, 0:Q_LORA], c_nat[:, tt, 0:Q_LORA], c_rs[:, tt:tt + 1], None,
                                           ALU.mult)
                op.then_inc(c_scaled, 1)
                for tt in range(2):
                    op = dve.tensor_scalar(c_nat[:, tt, Q_LORA:Q_LORA + KV_LORA],
                                           c_nat[:, tt, Q_LORA:Q_LORA + KV_LORA], c_rs[:, 2 + tt:3 + tt], None,
                                           ALU.mult)
                link(op)
                a = Q_LORA + KV_LORA
                t = [rope_t[:, 32 * m:32 * m + 32].rearrange("p (t n) -> p t n", t=2) for m in range(4)]
                rope4(c_nat[:, :, a:a + HALF], c_nat[:, :, a + HALF:a + 2 * HALF],
                      c_("cos_c").rearrange("p (t n) -> p t n", t=2), c_("sin_c").rearrange("p (t n) -> p t n", t=2),
                      t).then_inc(kc_roped, 1)

            def latent_rope():
                dve.wait_ge(p_act, taken(JOB[("cq", 1, 1)]))
                for tt in range(2):
                    q = qc_nat[:, tt, :].rearrange("p (h n) -> p h n", h=C_HEADS)
                    a, b = (c_(n)[:, HALF * tt:HALF * tt + HALF].unsqueeze(1).to_broadcast([P, C_HEADS, HALF])
                            for n in ("cos_c", "sin_c"))
                    t = [rope_s[:, P * m:P * m + P].rearrange("p (h n) -> p h n", h=C_HEADS) for m in range(4)]
                    op = rope4(q[:, :, C_NOPE:C_NOPE + HALF], q[:, :, C_NOPE + HALF:C_QK], a, b, t)
                    if tt == 0:
                        link(op)
                op.then_inc(qc_roped, 1)

            def take(job, j):
                kind = job[0]
                src = bank(6 + j % 2)
                dve.wait_ge(p_ready, j + 1)
                if kind == "bias":
                    dve.wait_ge(table_in, 48)
                    dve.tensor_tensor(bias_sb, src[0:BIAS_HEADS, 0:VALS], unseen_sb, ALU.add).then_inc(p_dve, 1)
                elif kind == "y1":
                    s, tt = job[1:]
                    xs = x2[:, tt, 256 * s:256 * s + 256]
                    dve.scalar_tensor_tensor(xs, xs, ALPHA, src[:, 0:256], ALU.mult, ALU.add).then_inc(p_dve, 1)
                elif kind == "logit":
                    n = GROUPS + EXPERTS
                    dve.tensor_scalar(logitT_sb[0:n, :], src[0:n, 0:T], route_b[0:n, :], None, ALU.add
                                      ).then_inc(p_dve, 1)
                elif kind == "logitT":
                    dve.tensor_copy(lg, src[:, 0:72].rearrange("p (t n) -> p t n", t=2)).then_inc(p_dve, 1)
                elif kind == "xt2":
                    l, tt, half = job[1:]
                    g = vecs[:, 8 * l + 4 * half:8 * l + 4 * half + 4].unsqueeze(2).to_broadcast([P, 4, P])
                    dve.tensor_tensor(xT3[:, 4 * half:4 * half + 4, P * tt:P * tt + P],
                                      src.rearrange("p (c t) -> p c t", c=4), g, ALU.mult).then_inc(p_dve, 1)
                elif kind == "rank":
                    e = EXPERTS
                    link(dve.tensor_tensor(rank, src[:, 0:2 * e], chosen, ALU.mult))
                    link(dve.tensor_scalar(e_sc, chosen, -ABSENT, ABSENT, ALU.mult, ALU.add))
                    link(dve.tensor_tensor(rank, rank, e_sc, ALU.add))
                    dve.tensor_reduce(cnt_b, src[:, 2 * e:3 * e].rearrange("p (b e) -> p b e", b=BUNCHES), X, ALU.max
                                      ).then_inc(p_dve, 1)
                elif kind == "swap":
                    l, n = job[1:]
                    cos, sin = (("cos_lin", "sin_lin") if n < 6 else ("cos_ax", "sin_ax"))
                    tl = tile3[:, n, :]
                    if n >= 12:
                        dve.wait_ge(p_act, taken(JOB[("hsq", l, n)]))
                    else:
                        dve.wait_ge(p_act, taken(JOB[("tile2", l, n)]))
                    if rope_nth(l, n) > 1:
                        dve.wait_ge(roped, rope_nth(l, n) - 1)
                    link(dve.tensor_tensor(rope_a, src[:, 0:T], c_(sin), ALU.mult))
                    op = dve.tensor_tensor(tl, tl, c_(cos), ALU.mult)
                    op.then_inc(p_dve, 1)
                    dve.wait_ge(p_dve, taken(j))
                    op = dve.tensor_tensor(tl, tl, rope_a, ALU.add)
                    if n >= 12:
                        link(op)
                        op = dve.tensor_tensor(tl, tl, sq_tile(n), ALU.mult)
                    op.then_inc(roped, 1)

            def exchange(l):
                dve.wait_ge(roped, rope_nth(l, 15))
                dve.wait_ge(p_act, taken(JOB[("vn", l, 16)]))
                link(dve.tensor_copy(tile3[0:HD, 16, :], tile3[HD:P, 15, :]))
                dve.tensor_copy(tile3[HD:P, 16, :], tile3[0:HD, 15, :]).then_inc(k_copied, 1)

            def maxes(step):
                kind, l, h = STEPS[step]
                par = step % 2
                m_, n_ = mx[:, 8 * par:8 * par + 8], nm[:, 4 * par:4 * par + 4]
                pr = probs[:, 1152 * par:1152 * par + 1152]
                b0 = s_first(step)
                if kind in "AB" and step >= 2:
                    dve.wait_ge(turned, t_first(step - 1))

                def biased(dst, s, b, m):
                    return dve.tensor_tensor_reduce(out=dst, in0=s, in1=b, scale=1.0, scalar=LOW, op0=ALU.add,
                                                    op1=ALU.max, accum_out=m)

                if kind == "A":
                    dve.wait_ge(scores, b0 + 1)
                    s = bank(b0 % 3)
                    biased(pr[:, 0:P], s[:, 0:P], bias3[:, h, P:T], m_[:, 0:1])
                    link(biased(pr[:, P:3 * P], s[:, P:3 * P], bias3[:, h, :], m_[:, 1:2]))
                    dve.tensor_scalar(n_[:, 0:2], m_[:, 0:2], sink[:, h:h + 1], -1.0, ALU.max, ALU.mult
                                      ).then_inc(maxed, 1)
                elif kind == "B":
                    heads = A_HEADS + h
                    dve.wait_ge(scores, b0 + 1)
                    biased(pr[:, 0:384].rearrange("p (g t) -> p g t", g=3),
                           bank(b0 % 3)[:, 0:384].rearrange("p (g t) -> p g t", g=3),
                           bias3[:, heads:BIAS_HEADS:B_HEADS, P:T], m_[:, 0:1])
                    dve.wait_ge(scores, b0 + 2)
                    biased(pr[:, 384:896].rearrange("p (g t) -> p g t", g=2),
                           bank((b0 + 1) % 3).rearrange("p (g t) -> p g t", g=2),
                           bias3[:, heads:heads + B_HEADS + 1:B_HEADS, :], m_[:, 1:2])
                    dve.wait_ge(scores, b0 + 3)
                    link(biased(pr[:, 896:1152], bank((b0 + 2) % 3)[:, 0:T], bias3[:, heads + 2 * B_HEADS, :],
                                m_[:, 2:3]))
                    link(dve.tensor_tensor(m_[:, 1:2], m_[:, 1:2], m_[:, 2:3], ALU.max))
                    dve.tensor_scalar(n_[:, 0:2], m_[:, 0:2], -1.0, None, ALU.mult).then_inc(maxed, 1)
                elif kind == "C":
                    dve.wait_ge(scores, b0 + 1)
                    s = bank(b0 % 3)
                    dve.tensor_reduce(m_[:, 0:1], s[:, 0:P], X, ALU.max)
                    link(dve.tensor_reduce(m_[:, 1:2], s[:, P:3 * P], X, ALU.max))
                    dve.tensor_scalar(n_[:, 0:2], m_[:, 0:2], -(C_QK ** -0.5), None, ALU.mult).then_inc(maxed, 1)
                elif kind == "D":
                    for tt in range(2):
                        dve.wait_ge(scores, b0 + tt + 1)
                        op = dve.tensor_reduce(m_[:, 2 * tt:2 * tt + 2],
                                               bank((b0 + tt) % 3).rearrange("p (m t) -> p m t", m=2), X, ALU.max)
                    link(op)
                    dve.tensor_scalar(n_[:, 0:4], m_[:, 0:4], -(32 ** -0.5), None, ALU.mult).then_inc(maxed, 1)
                else:
                    dve.wait_ge(scores, b0 + 1)
                    link(dve.tensor_reduce(m_[:, 0:2], bank(b0 % 3).rearrange("p (m t) -> p m t", m=2), X, ALU.max))
                    dve.tensor_scalar(n_[:, 0:2], m_[:, 0:2], -(HD ** -0.5), None, ALU.mult).then_inc(maxed, 1)

            def norms(step):
                kind, l, h = STEPS[step]
                par = step % 2
                s_ = sm[:, 4 * par:4 * par + 4]
                pr = probs[:, 1152 * par:1152 * par + 1152]
                dve.wait_ge(exped, step + 1)
                w = 4 if kind == "D" else 2
                if kind == "A":
                    link(dve.tensor_tensor(s_[:, 0:2], s_[:, 0:2], sink_e[:, 2 * par:2 * par + 2], ALU.add))
                link(dve.reciprocal(s_[:, 0:w], s_[:, 0:w]))
                if kind == "D":
                    dve.tensor_scalar(s_[:, 2:4], s_[:, 2:4], neg_lam[:, l:l + 1], None, ALU.mult)
                    for tt in range(2):
                        op = dve.tensor_scalar(pr[:, T * tt:T * tt + T], pr[:, T * tt:T * tt + T],
                                               s_[:, tt:tt + 1], None, ALU.mult)
                    link(op)
                    for tt in range(2):
                        op = dve.scalar_tensor_tensor(pr[:, T * tt:T * tt + T], pr[:, 512 + T * tt:512 + T * tt + T],
                                                      s_[:, 2 + tt:3 + tt], pr[:, T * tt:T * tt + T],
                                                      ALU.mult, ALU.add)
                else:
                    cut = {"A": (P, 3 * P), "C": (P, 3 * P), "B": (384, 1152)}.get(kind, (T, 2 * T))
                    dve.tensor_scalar(pr[:, 0:cut[0]], pr[:, 0:cut[0]], s_[:, 0:1], None, ALU.mult)
                    op = dve.tensor_scalar(pr[:, cut[0]:cut[1]], pr[:, cut[0]:cut[1]], s_[:, 1:2], None, ALU.mult)
                op.then_inc(normed, 1)

            def outs(step):
                kind, l, h = STEPS[step]
                par = h % 2
                chunk = {"A": 0, "B": 2, "C": 4, "D": 0, "G": 3, "M": 6}[kind] + h // 2
                dve.wait_ge(o_ready, step + 1)
                rows = slice(HD * par, HD * par + HD)
                src = bank(5)[rows, T * (step % 2):T * (step % 2) + T]
                if kind in "GM":
                    n = GATE_TILES[chunk]
                    if (kind, h) == ("G", 0):
                        dve.wait_ge(o_out, step)
                    dve.wait_ge(gate_silu, silu_nth(l, n))
                    dve.tensor_tensor(mix3[rows, chunk, :], src, tile3[rows, n, :], ALU.mult).then_inc(o_out, 1)
                else:
                    dve.tensor_copy(mix3[rows, chunk, :], src).then_inc(o_out, 1)

            def moments(tt):
                for c in range(2):
                    op = dve.bn_stats(stats4[:, tt, c, :], x2[:, tt, 512 * c:512 * c + 512])
                link(op)
                dve.bn_aggr(mv3[:, tt, :], stats4[:, tt, :, :].rearrange("p c s -> p (c s)")).then_inc(ln_var, 1)

            def centred(n, tt, ready):
                dve.wait_ge(ready, 32)
                dve.wait_ge(ln_var, 2 * n + tt + 1)
                xs = x2[:, tt, :]
                link(dve.scalar_tensor_tensor(xs, xs, mv3[:, tt, 0:1], ln_row[:, 0, :], ALU.subtract, ALU.mult))

            def scaled(n, tt):
                dve.wait_ge(ln_rstd, 2 * n + tt + 1)
                xs = x2[:, tt, :]
                dve.scalar_tensor_tensor(xs, xs, ln_rs[:, tt:tt + 1], ln_row[:, 1, :], ALU.mult, ALU.add
                                         ).then_inc(ln_done, 1)

            def first_of(one, score, best, values3, n):
                def wide(a):
                    return a.unsqueeze(2).to_broadcast([P, 2, n])

                order = c_("first32")[:, EXPERTS - n:EXPERTS].unsqueeze(1).to_broadcast([P, 2, n])
                one3, score3 = (a.rearrange("p (t n) -> p t n", t=2) for a in (one, score))
                link(dve.tensor_reduce(best, values3, X, ALU.max))
                link(dve.tensor_tensor(score3, values3, wide(best), ALU.is_equal))
                link(dve.tensor_tensor(score3, score3, order, ALU.mult))
                link(dve.tensor_reduce(e_t, score3, X, ALU.max))
                link(dve.tensor_tensor(one3, score3, wide(e_t), ALU.is_equal))

            def route():
                dve.memset(ones, 1.0)
                dve.wait_ge(p_dve, taken(JOB[("logitT",)]))
                g3, e3 = lg[:, :, 0:GROUPS], lg[:, :, GROUPS:GROUPS + EXPERTS]
                first_of(g_one, g_sc, g_mx, g3, GROUPS)
                gw = g_mx.unsqueeze(2).to_broadcast([P, 2, GROUPS])
                dve.tensor_tensor(g_dif.rearrange("p (t n) -> p t n", t=2), g3, gw, ALU.subtract
                                  ).then_inc(route_dif, 1)
                m4 = e_m.rearrange("p (t g e) -> p t g e", t=2, g=GROUPS)
                s4 = e_sc.rearrange("p (t g e) -> p t g e", t=2, g=GROUPS)
                one = g_one.rearrange("p (t g) -> p t g", t=2)
                for tt in range(2):
                    ow = one[:, tt, :].unsqueeze(2).to_broadcast([P, GROUPS, PER_GROUP])
                    ev = e3[:, tt, :].rearrange("p (g e) -> p g e", g=GROUPS)
                    dve.tensor_tensor(m4[:, tt], ev, ow, ALU.mult)
                    link(dve.tensor_scalar(s4[:, tt], ow, -NEG, NEG, ALU.mult, ALU.add))
                link(dve.tensor_tensor(e_m, e_m, e_sc, ALU.add))
                m3 = e_m.rearrange("p (t n) -> p t n", t=2)
                first_of(e_one1, e_sc, e_mx1, m3, EXPERTS)
                link(dve.scalar_tensor_tensor(e_m, e_one1, 3.0 * NEG, e_m, ALU.mult, ALU.add))
                first_of(e_one2, e_sc, e_mx2, m3, EXPERTS)
                dve.tensor_tensor(chosen, e_one1, e_one2, ALU.add).then_inc(chosen_done, 1)
                dve.tensor_tensor(e_t, e_mx2, e_mx1, ALU.subtract).then_inc(route_m, 1)
                dve.wait_ge(route_exp, 1)
                link(dve.tensor_reduce(g_sum, g_exp.rearrange("p (t n) -> p t n", t=2), X, ALU.add))
                dve.wait_ge(route_x, 1)
                link(dve.tensor_scalar(w_1, e_x, 1.0, None, ALU.add))
                link(dve.tensor_tensor(w_1, w_1, g_sum, ALU.mult))
                link(dve.reciprocal(w_1, w_1))
                link(dve.tensor_tensor(w_2, w_1, e_x, ALU.mult))
                ww = [a.unsqueeze(2).to_broadcast([P, 2, EXPERTS]) for a in (w_1, w_2)]
                one1, one2 = (a.rearrange("p (t n) -> p t n", t=2) for a in (e_one1, e_one2))
                link(dve.tensor_tensor(gates3, one1, ww[0], ALU.mult))
                link(dve.tensor_tensor(m3, one2, ww[1], ALU.mult))
                link(dve.tensor_tensor(gates, gates, e_m, ALU.add))

            def more_rounds():
                dve.wait_ge(p_dve, taken(JOB[("rank",)]))
                n = (ROUNDS - 1) * BUNCHES
                cw = cnt_b.unsqueeze(1).to_broadcast([P, ROUNDS - 1, BUNCHES])
                link(dve.tensor_tensor(more_f.rearrange("p (r b) -> p r b", r=ROUNDS - 1), cw,
                                       c_("round_from").rearrange("p (r b) -> p r b", r=ROUNDS - 1), ALU.is_gt))
                link(dve.tensor_reduce(any_more, more_f, X, ALU.max))
                a, b = scan, e_sc[:, 0:n]
                link(dve.memset(a[:, 0:1], 0.0))
                link(dve.tensor_copy(a[:, 1:n], more_f[:, 0:n - 1]))
                d = 1
                while d < n:
                    link(dve.tensor_copy(b[:, 0:d], a[:, 0:d]))
                    link(dve.tensor_tensor(b[:, d:n], a[:, d:n], a[:, 0:n - d], ALU.add))
                    a, b = b, a
                    d *= 2
                link(dve.tensor_copy(flags[:, 0:n], more_f))
                link(dve.tensor_copy(flags[:, n:2 * n], a))
                dve.tensor_copy(flags[:, 2 * n:2 * n + 1], any_more).then_inc(routed, 1)

            LINKS = 4

            def bunch(i, g, r):
                def mlink(ins_, n):
                    ins_.then_inc(moe_chain, 1)
                    dve.wait_ge(moe_chain, i * LINKS + n)

                if isinstance(g, int):
                    rk, gt = (a[:, :, AT_ONCE * g:AT_ONCE * g + AT_ONCE] for a in (rank3, gates3))
                    pl = c_("places")[:, 0:PLACES]
                else:
                    rk, gt = (a[:, :, bass.ds(g * AT_ONCE, AT_ONCE)] for a in (rank3, gates3))
                    if r is None:
                        pl = c_("places")[:, 0:PLACES]
                    else:
                        at = CONST["places"][0] + PLACES
                        pl = const[:, bass.ds(r * PLACES + at, PLACES)]
                pw = pl.unsqueeze(1).to_broadcast([P, AT_ONCE, PLACES])
                for tt in range(2):
                    rw = rk[:, tt, :].unsqueeze(2).to_broadcast([P, AT_ONCE, PLACES])
                    op = dve.tensor_tensor(places4[:, tt], rw, pw, ALU.is_equal)
                mlink(op, 1)
                for tt in range(2):
                    gw = gt[:, tt, :].unsqueeze(2).to_broadcast([P, AT_ONCE, PLACES])
                    op = dve.tensor_tensor(weighed4[:, tt], places4[:, tt], gw, ALU.mult)
                op.then_inc(placed, 1)
                dve.wait_ge(back_ready, i + 1)
                if not isinstance(i, int):
                    dve.wait_ge(summed, i)
                dve.tensor_copy(back, bank(7)[:, 0:256]).then_inc(back_out, 1)
                dve.wait_ge(gate_exped, i + 1)
                mlink(dve.tensor_scalar(gate_e, gate_e, 1.0, None, ALU.add), 2)
                mlink(dve.reciprocal(gate_e, gate_e), 3)
                mlink(dve.tensor_tensor(gate_e, gate_e, bank(6)[:, 0:DE], ALU.mult), 4)
                dve.tensor_tensor(hidden, gate_e, bank(6)[:, DE:2 * DE], ALU.mult).then_inc(hidden_done, 1)
                dve.wait_ge(y_ready, 2 * i + 2)
                dve.tensor_copy(y_e[:, 512:1024], bank(5)).then_inc(y1_out, 1)

            def experts():
                bunch(0, 0, None)
                more_rounds()
                with dve.Fori(1, BUNCHES) as i:
                    bunch(i, i, None)
                some = dve.value_load(flags[0:1, 112:113], min_val=0, max_val=1)
                with dve.If(some):
                    with dve.Fori(0, ROUNDS - 1) as r:
                        with dve.Fori(0, BUNCHES) as g:
                            flag = dve.value_load(flags[0:1, bass.ds(r * BUNCHES + g, 1)], min_val=0, max_val=1)
                            with dve.If(flag):
                                n = dve.value_load(flags[0:1, bass.ds(r * BUNCHES + g + 56, 1)], min_val=0, max_val=55)
                                bunch(n + BUNCHES, g, r)
                for n in AT_EXPERTS:
                    low(n)
                for tt in range(2):
                    dve.wait_ge(moe_done, tt + 1)
                    for half in range(2):
                        xs = x2[:, tt, 512 * half:512 * half + 512]
                        op = dve.scalar_tensor_tensor(xs, xs, ALPHA, bank(2 * tt + half), ALU.mult, ALU.add)
                    link(op)
                    moments(tt)
                    if tt:
                        scaled(1, 0)
                    centred(1, tt, ln2_in)
                scaled(1, 1)

            def start_layer(l, tt):
                dve.wait_ge(x_rstd, 2 * l + tt + 1)
                dve.tensor_scalar(xn2[:, tt, :], x2[:, tt, :], x_rs[:, tt:tt + 1], None, ALU.mult
                                  ).then_inc(x_scaled, 1)

            def low(n):
                dve.wait_ge(highs, n + 1)
                dve.tensor_tensor(split_of(n)[1], raw_of(n), as_f32(split_of(n)[0]), ALU.subtract).then_inc(lows, 1)

            def x_low_part(phase, part):
                dve.wait_ge(x_highs, x_part(phase, part))
                if phase == 0:
                    dve.wait_ge(p_ready, JOB[("cnat", 1)] + 1)
                own = X_PARTS[phase][part]
                dve.tensor_tensor(x_low3[own], xT3[own], as_f32(a_high3[own]), ALU.subtract).then_inc(x_lows, 1)

            def mix_low_part(phase, part):
                dve.wait_ge(mix_highs, mix_part(phase, part))
                own = slice(*MIX_PARTS[phase][part])
                dve.tensor_tensor(mix_low3[:, own, :], mix3[:, own, :], as_f32(a_high3[:, own, :]), ALU.subtract
                                  ).then_inc(mix_lows, 1)

            def silu(l, n):
                dve.wait_ge(sigmoid, silu_nth(l, n))
                tl = tile3[:, n, :]
                dve.tensor_tensor(tl, tl, exp_tile(n), ALU.mult).then_inc(gate_silu, 1)
                if n in GATE_TILES[1:3]:
                    gate(l, GATE_TILES.index(n))

            def sub_norm(l, n):
                dve.wait_ge(p_act, taken(JOB[("hso", l, n)]))
                dve.scalar_tensor_tensor(mix3[:, n, :], mix3[:, n, :], sub_g[:, l:l + 1], sq_tile(n),
                                         ALU.mult, ALU.mult).then_inc(sub_done, 1)
                if n == 0:
                    gate(l, n)

            def gate(l, c):
                dve.wait_ge(gate_silu, silu_nth(l, GATE_TILES[c]))
                dve.wait_ge(sub_done, 3 * l + c + 1)
                dve.tensor_tensor(mix3[:, c, :], mix3[:, c, :], tile3[:, GATE_TILES[c], :], ALU.mult
                                  ).then_inc(gated, 1)

            def gained(l, m, tt):
                if (m, tt) == (0, 0):
                    dve.wait_ge(post_in, 32)
                dve.wait_ge(p_act, taken(JOB[("y2", l, m, tt)]))
                own = slice(COLS * m, COLS * m + COLS)
                return dve.tensor_tensor(y_nat[:, tt, own], y_nat[:, tt, own], post_row[:, l, own], ALU.mult)

            def end_layer(l, tt):
                dve.wait_ge(p_act, taken(JOB[("y2", l, 3, tt)]))
                dve.tensor_reduce(y_ms[:, tt:tt + 1], y_sq[:, 4 * tt:4 * tt + 4], X, ALU.add).then_inc(y_sum, 1)
                link(gained(l, 3, tt))
                dve.wait_ge(y_rstd, 2 * l + tt + 1)
                dve.scalar_tensor_tensor(x2[:, tt, :], y_nat[:, tt, :], y_rs[:, tt:tt + 1], x2[:, tt, :],
                                         ALU.mult, ALU.add).then_inc(x_done, 1)

            j = step = drained = 0
            subs_due, gates_due, lows_due = [], [], []
            for jobs, what in TURNS:
                if what in STEP:
                    step = STEP[what]
                    if step == 0:
                        dve.wait_ge(bias_in, 16)
                    if not opens(step):
                        norms(step - 1)
                    maxes(step)
                    if not opens(step) and not opens(step - 1) and STEPS[step - 2][0] != "D":
                        outs(step - 2)
                    for due in subs_due:
                        sub_norm(*due)
                    for due in gates_due:
                        silu(*due)
                    for n in lows_due:
                        low(n)
                    subs_due, gates_due, lows_due = [], [], []
                    if what == ("B", 0, 3):
                        mix_low_part(0, 0)
                    if what[0] == "D" and what[2] == 4:
                        exchange(what[1])
                    drained = 0
                for job in jobs:
                    if job == ("vec",):
                        for half in range(2):
                            x_low_part(0, half)
                    if job == ("y2", 0, 3, 1):
                        start_layer(1, 0)
                    if job == ("xt2", 0, 0, 0):
                        for tt in range(2):
                            start_layer(0, tt)
                    if job == ("xt2", 1, 1, 0):
                        start_layer(1, 1)
                    if what is None:
                        for n in lows_due:
                            low(n)
                        lows_due = []
                    lows_due = lows_due + SPLIT_AT.get(j, [])
                    if job == ("tile1", 0):
                        latent_sums()
                    if job == ("tile1", 2):
                        latent_norm()
                    if job == ("ct",):
                        lambda_sums()
                    if BY_DVE[j]:
                        take(job, j)
                    if job[0] == "xt2" and job[3] == 1:
                        for part in (2 * job[2], 2 * job[2] + 1):
                            x_low_part(job[1] + 1, part)
                    if job == ("cq", 0, 0):
                        dve.wait_ge(mem_in, 16)
                        link(rms(mem_sq[:, 0:1], mem_nat[:, 0, :], D, mem_junk, 1e-6))
                        rms(mem_sq[:, 1:2], mem_nat[:, 1, :], D, mem_junk, 1e-6).then_inc(mem_sum, 1)
                    if job == ("cq", 1, 1):
                        latent_rope()
                    if job[:2] == ("y1", 3):
                        dve.wait_ge(p_dve, taken(j))
                        moments(job[2])
                        centred(0, job[2], ln1_in)
                        scaled(0, job[2])
                    if job == ("logitT",):
                        route()
                    if job[0] == "tile2" and job[2] in GATE_TILES:
                        gates_due.append(job[1:])
                    if job == ("tile2", 0, 3):
                        dve.wait_ge(lam_exp, 1)
                        le = lam_e.rearrange("p (l a) -> p l a", l=2)
                        link(dve.tensor_tensor(neg_lam, le[:, :, 1], le[:, :, 0], ALU.subtract))
                        for l in range(LAYERS):
                            dve.tensor_scalar(neg_lam[:, l:l + 1], neg_lam[:, l:l + 1], -LAMBDA_INIT[l], None, ALU.add)
                            op = dve.tensor_scalar(sub_g[:, l:l + 1], vecs[:, 35 + l:36 + l], 1.0 - LAMBDA_INIT[l],
                                                   None, ALU.mult)
                        link(op)
                    if job[0] == "hso":
                        subs_due.append(job[1:])
                    if job[0] == "y2" and job[2] < 3:
                        gained(*job[1:])
                    if job[0] == "y2" and job[2] == 3:
                        end_layer(job[1], job[3])
                    j += 1
                if what == "experts":
                    experts()
                elif what is None and jobs == []:
                    if drained == 0:
                        norms(step)
                        outs(step - 1)
                    else:
                        outs(step)
                    if STEPS[step][0] == "M":
                        mix_low_part(STEPS[step][1] + 1, drained)
                    else:
                        mix_low_part(0, drained + 1)
                    drained += 1


_INS = ["x", "w_in", "w_out", "sinks", "rel_bias", "mla_q_norm", "mla_kv_norm", "w_uq", "w_ukv", "ln1_g", "ln1_b",
        "w_route_group", "b_route_group", "w_route_expert", "b_route_expert", "w_expert_gate", "w_expert_up",
        "w_expert_down", "ln2_g", "ln2_b", "mem_2", "pre_norm_2", "w_in_2", "diff_lambda_2", "diff_subln_2",
        "gqa_q_norm_2", "gqa_k_norm_2", "mem_norm_2", "w_mem_kv_2", "w_out_2", "post_norm_2"]


def kernel(**inputs):
    import numpy as _np
    import concourse.bacc as _bacc
    from concourse import mybir as _mybir
    from concourse.bass_utils import run_bass_kernel_spmd as _run

    nc = _bacc.Bacc("TRN2", target_bir_lowering=False, num_devices=1, dynamic_dma_scratch_size=4096)
    arrays, args = {}, {}
    given = {name: _np.ascontiguousarray(inputs[name]) for name in _INS}
    given.update(constants())
    for name, a in given.items():
        arrays[f"in_{name}_dram"] = a
        args[name] = nc.dram_tensor(f"in_{name}_dram", a.shape, _mybir.dt.from_np(a.dtype), kind="ExternalInput").ap()
    out = nc.dram_tensor("out_0_dram", (1, T, D), F32, kind="ExternalOutput").ap()
    build(nc, args, out)
    r = _run(nc, [arrays], core_ids=[0])
    return r.results[0]["out_0_dram"]
```
